# Optimizing a Trainium2 kernel written in Bass

```python
import math
import jax, jax.numpy as jnp
from jax import lax
import numpy as np

D_MODEL = 1024
BATCH = 1
SEQ = 2048
DEPTH = 1

CHUNK = 64
Q_BLOCK = 128

D_MIX = D_MODEL
SB_HEAD_DIM = 64
SB_HEADS = (D_MIX // 2) // SB_HEAD_DIM
SB_W = SB_HEADS * SB_HEAD_DIM
MLA_V_DIM = 64
MLA_HEADS = (D_MIX - SB_W) // MLA_V_DIM
MLA_W = MLA_HEADS * MLA_V_DIM
MLA_NOPE_DIM = 64
MLA_ROPE_DIM = 32
MLA_QK_DIM = MLA_NOPE_DIM + MLA_ROPE_DIM
MLA_Q_RANK = (3 * D_MODEL) // 8
MLA_KV_RANK = D_MODEL // 4
ROPE_BASE = 10000.0

IN_SPLITS = (SB_W, SB_W, SB_W, MLA_Q_RANK, MLA_KV_RANK, MLA_ROPE_DIM)
D_IN = sum(IN_SPLITS)

D_FF = 4 * D_MODEL

LN_EPS = 1e-5
RMS_EPS = 1e-6
DEEPNORM_ALPHA = (2.0 * DEPTH) ** 0.25
DEEPNORM_BETA = (8.0 * DEPTH) ** -0.25
N_MOD = 6

kernel_name = "hybrid_sb_mla_deepnorm_adaln_block"

def layer_norm(x, g, b):
    xf = x.astype(jnp.float32)
    mu = jnp.mean(xf, axis=-1, keepdims=True)
    var = jnp.mean(jnp.square(xf - mu), axis=-1, keepdims=True)
    return ((xf - mu) * lax.rsqrt(var + LN_EPS) * g.astype(jnp.float32) + b.astype(jnp.float32)).astype(x.dtype)

def rms_norm(x, g):
    xf = x.astype(jnp.float32)
    ms = jnp.mean(jnp.square(xf), axis=-1, keepdims=True)
    return (xf * lax.rsqrt(ms + RMS_EPS) * g.astype(jnp.float32)).astype(x.dtype)

def rope_tables(seq):
    inv_freq = 1.0 / (ROPE_BASE ** (jnp.arange(0, MLA_ROPE_DIM, 2, dtype=jnp.float32) / MLA_ROPE_DIM))
    ang = jnp.arange(seq, dtype=jnp.float32)[:, None] * inv_freq[None, :]
    return jnp.cos(ang), jnp.sin(ang)

def apply_rope(x, cos, sin):
    xf = x.astype(jnp.float32)
    x1, x2 = jnp.split(xf, 2, axis=-1)
    return jnp.concatenate([x1 * cos - x2 * sin, x2 * cos + x1 * sin], axis=-1).astype(x.dtype)

def stick_breaking_block(q_blk, k_pre, v_pre, q_start):
    qb = q_blk.shape[1]
    kl = k_pre.shape[1]
    z = jnp.einsum('bqhd,bkhd->bhqk', q_blk, k_pre).astype(jnp.float32) * (SB_HEAD_DIM ** -0.5)
    t_idx = q_start + jnp.arange(qb)
    s_idx = jnp.arange(kl)
    strict = s_idx[None, :] < t_idx[:, None]
    log_keep = jnp.where(strict, jax.nn.log_sigmoid(-z), 0.0)
    log_later = lax.cumsum(log_keep, axis=3, reverse=True) - log_keep
    w = jnp.where(strict, jnp.exp(jax.nn.log_sigmoid(z) + log_later), 0.0)
    return jnp.einsum('bhqk,bkhd->bqhd', w.astype(v_pre.dtype), v_pre)

def mla_block(qn_blk, qr_blk, kn_pre, kr_pre, v_pre, q_start):
    qb = qn_blk.shape[1]
    kl = kn_pre.shape[1]
    scores = (jnp.einsum('bqhd,bkhd->bhqk', qn_blk, kn_pre)
              + jnp.einsum('bqhr,bkr->bhqk', qr_blk, kr_pre)).astype(jnp.float32) * (MLA_QK_DIM ** -0.5)
    q_chunk = (q_start + jnp.arange(qb)) // CHUNK
    k_chunk = jnp.arange(kl) // CHUNK
    allowed = k_chunk[None, :] <= q_chunk[:, None]
    scores = jnp.where(allowed, scores, jnp.finfo(jnp.float32).min)
    p = jax.nn.softmax(scores, axis=-1)
    return jnp.einsum('bhqk,bkhd->bqhd', p.astype(v_pre.dtype), v_pre)

def setup_inputs(seed: int = 0) -> dict:
    key = jax.random.key(seed)
    ks = jax.random.split(key, 24)
    f32 = jnp.float32
    nrm = lambda k, shape, s: jax.random.normal(k, shape, f32) * s
    L, D = DEPTH, D_MODEL
    x = jax.random.normal(ks[0], (BATCH, SEQ, D), f32)
    c = jax.random.normal(ks[1], (BATCH, D), f32)
    ln_in_g = 1.0 + nrm(ks[2], (D,), 0.02)
    ln_in_b = nrm(ks[3], (D,), 0.02)
    w_ada = nrm(ks[4], (L, D, N_MOD * D), 0.1 * D ** -0.5)
    b_ada = nrm(ks[5], (L, N_MOD * D), 0.02)
    w_in_qk = nrm(ks[6], (L, D, 2 * SB_W), D ** -0.5)
    w_in_v = nrm(ks[7], (L, D, SB_W), D ** -0.5) * DEEPNORM_BETA
    w_in_lat = nrm(ks[8], (L, D, MLA_Q_RANK + MLA_KV_RANK + MLA_ROPE_DIM), D ** -0.5)
    w_in = jnp.concatenate([w_in_qk, w_in_v, w_in_lat], axis=-1)
    q_norm_g = 1.0 + nrm(ks[9], (L, MLA_Q_RANK), 0.02)
    kv_norm_g = 1.0 + nrm(ks[10], (L, MLA_KV_RANK), 0.02)
    w_uq = nrm(ks[11], (L, MLA_Q_RANK, MLA_HEADS * MLA_QK_DIM), MLA_Q_RANK ** -0.5)
    w_uk = nrm(ks[12], (L, MLA_KV_RANK, MLA_HEADS * MLA_NOPE_DIM), MLA_KV_RANK ** -0.5)
    w_uv = nrm(ks[13], (L, MLA_KV_RANK, MLA_HEADS * MLA_V_DIM), MLA_KV_RANK ** -0.5) * DEEPNORM_BETA
    w_ukv = jnp.concatenate([w_uk, w_uv], axis=-1)
    w_o = nrm(ks[14], (L, D_MIX, D), D_MIX ** -0.5) * DEEPNORM_BETA
    ln1_g = 1.0 + nrm(ks[15], (L, D), 0.02)
    ln1_b = nrm(ks[16], (L, D), 0.02)
    w_up = nrm(ks[17], (L, D, D_FF), D ** -0.5)
    w_down = nrm(ks[18], (L, D_FF, D), D_FF ** -0.5) * DEEPNORM_BETA
    ln2_g = 1.0 + nrm(ks[19], (L, D), 0.02)
    ln2_b = nrm(ks[20], (L, D), 0.02)
    return {"x": x, "c": c, "ln_in_g": ln_in_g, "ln_in_b": ln_in_b,
            "w_ada": w_ada, "b_ada": b_ada, "w_in": w_in,
            "q_norm_g": q_norm_g, "kv_norm_g": kv_norm_g, "w_uq": w_uq, "w_ukv": w_ukv,
            "w_o": w_o, "ln1_g": ln1_g, "ln1_b": ln1_b,
            "w_up": w_up, "w_down": w_down, "ln2_g": ln2_g, "ln2_b": ln2_b}

def reference(x, c, ln_in_g, ln_in_b, w_ada, b_ada, w_in, q_norm_g, kv_norm_g, w_uq, w_ukv,
              w_o, ln1_g, ln1_b, w_up, w_down, ln2_g, ln2_b):
    bsz, seq, _ = x.shape
    n_blocks = seq // Q_BLOCK
    cos, sin = rope_tables(seq)
    split_at = list(np.cumsum(IN_SPLITS)[:-1])
    c_act = jax.nn.silu(c)

    x = layer_norm(x, ln_in_g, ln_in_b)

    for l in range(DEPTH):
        mod = c_act @ w_ada[l] + b_ada[l]
        shift1, scale1, gate1, shift2, scale2, gate2 = [m[:, None, :] for m in jnp.split(mod, N_MOD, axis=-1)]

        h = x * (1.0 + scale1) + shift1
        proj = h @ w_in[l]
        sb_q, sb_k, sb_v, c_q, c_kv, k_rope = jnp.split(proj, split_at, axis=-1)
        sb_q = sb_q.reshape(bsz, seq, SB_HEADS, SB_HEAD_DIM)
        sb_k = sb_k.reshape(bsz, seq, SB_HEADS, SB_HEAD_DIM)
        sb_v = sb_v.reshape(bsz, seq, SB_HEADS, SB_HEAD_DIM)

        q_all = (rms_norm(c_q, q_norm_g[l]) @ w_uq[l]).reshape(bsz, seq, MLA_HEADS, MLA_QK_DIM)
        q_nope, q_rot = q_all[..., :MLA_NOPE_DIM], q_all[..., MLA_NOPE_DIM:]
        q_rot = apply_rope(q_rot, cos[None, :, None, :], sin[None, :, None, :])
        kv = rms_norm(c_kv, kv_norm_g[l]) @ w_ukv[l]
        k_nope = kv[..., :MLA_HEADS * MLA_NOPE_DIM].reshape(bsz, seq, MLA_HEADS, MLA_NOPE_DIM)
        mla_v = kv[..., MLA_HEADS * MLA_NOPE_DIM:].reshape(bsz, seq, MLA_HEADS, MLA_V_DIM)
        k_rot = apply_rope(k_rope, cos[None], sin[None])

        sb_out, mla_out = [], []
        for i in range(n_blocks):
            q0 = i * Q_BLOCK
            q1 = q0 + Q_BLOCK
            sb_out.append(stick_breaking_block(sb_q[:, q0:q1], sb_k[:, :q1], sb_v[:, :q1], q0))
            mla_out.append(mla_block(q_nope[:, q0:q1], q_rot[:, q0:q1], k_nope[:, :q1],
                                     k_rot[:, :q1], mla_v[:, :q1], q0))
        sb_y = jnp.concatenate(sb_out, axis=1).reshape(bsz, seq, SB_W)
        mla_y = jnp.concatenate(mla_out, axis=1).reshape(bsz, seq, MLA_W)
        mix = jnp.concatenate([sb_y, mla_y], axis=-1) @ w_o[l]
        x = layer_norm(DEEPNORM_ALPHA * x + (1.0 + gate1) * mix, ln1_g[l], ln1_b[l])

        h2 = x * (1.0 + scale2) + shift2
        ff = jnp.square(jax.nn.relu(h2 @ w_up[l])) @ w_down[l]
        x = layer_norm(DEEPNORM_ALPHA * x + (1.0 + gate2) * ff, ln2_g[l], ln2_b[l])

    return x


_drawn_inputs = setup_inputs


def setup_inputs(seed=0):
    import zlib

    import numpy as np

    out = dict(_drawn_inputs(seed))
    spreads = {}
    factors = {'ln_in_b': 2.769,
     'q_norm_g': 8.0,
     'kv_norm_g': 8.0,
     'w_uq': 3.2,
     'ln1_g': 2.744,
     'ln1_b': 2.737,
     'ln2_g': 2.84,
     'ln2_b': 2.95}
    for name, (base, spread) in spreads.items():
        noise = np.random.default_rng([zlib.crc32(name.encode()), seed]).standard_normal(out[name].shape)
        drawn = base * np.exp(spread * noise) if base else spread * noise
        out[name] = __import__('jax').numpy.asarray(drawn.astype(out[name].dtype))
    for name, factor in factors.items():
        out[name] = (out[name] * factor).astype(out[name].dtype)
    return out
```

```python
from contextlib import ExitStack

import concourse.bass as bass
from concourse import mybir

ALU = mybir.AluOpType
ACT = mybir.ActivationFunctionType
F32 = mybir.dt.float32
F32R = mybir.dt.float32r

P = 128
SEQ = 2048
D = 1024
KD = D // P
TG = 512
NG = SEQ // TG
TILES = SEQ // P
N_MOD = 6
HEADS = 8
HD = 64
ROPE = 32
QK = HD + ROPE
SBW = HEADS * HD
Q_RANK = 384
KV_RANK = 256
KQ = Q_RANK // P
KV = KV_RANK // P
D_FF = 4 * D
LN_EPS = 1e-5
RMS_EPS = 1e-6
ALPHA = 2.0 ** 0.25
SB_SCALE = HD ** -0.5
MLA_SCALE = QK ** -0.5
MASKED = -1e30


class Chain:

    def __init__(self, eng, sem, base=0, spare=None):
        self.eng, self.sem, self.base, self.spare, self.n = eng, sem, base, spare, 0

    def stand(self):
        self.eng.sem_inc(self.spare, 1)

    def step(self, instruction):
        self.n += 1
        instruction.then_inc(self.sem, 1)
        self.eng.wait_ge(self.sem, self.base + self.n)


class Scope:

    def __init__(self, nc, phase):
        self.nc, self.phase, self.ctx, self.sems = nc, phase, ExitStack(), []

    def __enter__(self):
        return self

    def __exit__(self, *exc):
        self.ctx.__exit__(*exc)
        if self.sems and exc[0] is None:
            self.nc.clear_and_free_semaphores(self.sems)
            self.nc.all_engine_barrier()

    def sb(self, name, shape, dtype=F32):
        return self.ctx.enter_context(self.nc.sbuf_tensor(f"{self.phase}_{name}", shape, dtype))

    def psum(self, name, shape):
        return self.ctx.enter_context(self.nc.psum_tensor(f"{self.phase}_{name}", shape, F32))

    def sem(self, name):
        self.sems.append(self.nc.alloc_semaphore(f"{self.phase}_{name}"))
        return self.sems[-1]

    def block(self):
        return self.ctx.enter_context(self.nc.Block())


def products(pe, out, wh, wl, xh, xl, first, last):
    pe.matmul(out, wh, xh, start=first, stop=False)
    pe.matmul(out, wl, xh, start=False, stop=False)
    return pe.matmul(out, wh, xl, start=False, stop=last)


def layer_norm_moments(nc, own, x, stats, moments):
    nc.vector.bn_stats(stats[:, 0, :], x[:, 0:512])
    own.step(nc.vector.bn_stats(stats[:, 1, :], x[:, 512:1024]))
    own.stand()
    own.step(nc.vector.bn_aggr(moments, stats[:, :, :].rearrange("p a b -> p (a b)")))


def refine_rsqrt(nc, own, rstd, var, root, tmp):
    own.step(nc.vector.reciprocal(rstd, root))
    own.step(nc.vector.tensor_tensor(tmp, rstd, rstd, ALU.mult))
    own.step(nc.vector.scalar_tensor_tensor(out=tmp, in0=tmp, scalar=-0.5, in1=var, op0=ALU.mult, op1=ALU.mult))
    own.step(nc.vector.scalar_tensor_tensor(out=rstd, in0=tmp, scalar=1.5, in1=rstd, op0=ALU.add, op1=ALU.mult))


def phase_modulation(nc, T, W, R):
    with Scope(nc, "m") as s:
        c_col = s.sb("c_col", [P, KD])
        c_sig = s.sb("c_sig", [P, KD])
        c_act = s.sb("c_act", [P, KD])
        c_rep = s.sb("c_rep", [P, KD, P])
        gate = s.sb("gate", [1, 2, D])
        ones = s.sb("ones", [P, P])
        w = s.sb("w", [P, 3, KD, 512])
        mod = s.sb("mod", [P, N_MOD * D])
        b_row = s.sb("b_row", [P, 3, 512])
        gb = s.sb("gb", [P, 2, D])
        x = s.sb("x", [P, 4, D])
        xhat = s.sb("xhat", [P, D])
        xg = s.sb("xg", [P, 2, D])
        xn = s.sb("xn", [P, 2, D])
        xt = s.sb("xt", [P, 2, KD, P])
        stats = s.sb("stats", [P, 2, 6])
        moments = s.sb("moments", [P, 4, 2])
        var, root, rstd, tmp = (s.sb(n, [P, 4]) for n in ("var", "root", "rstd", "tmp"))
        ps_mod = s.psum("ps_mod", [P, 3, 512])
        ps_t = s.psum("ps_t", [P, 4, 4, P])
        ps_col = s.psum("ps_col", [P, 512])

        c_loaded, gb_loaded = s.sem("c_loaded"), s.sem("gb_loaded")
        w_loaded = [s.sem(f"w_loaded{i}") for i in range(3)]
        x_loaded = [s.sem(f"x_loaded{i}") for i in range(4)]
        xn_stored = [s.sem(f"xn_stored{i}") for i in range(2)]
        xt_stored = [s.sem(f"xt_stored{i}") for i in range(2)]
        ones_set, ident_set, c_sigmoid, c_ready = s.sem("ones_set"), s.sem("ident_set"), s.sem("c_sigmoid"), s.sem("c_ready")
        mod_summed, cols_made = s.sem("mod_summed"), s.sem("cols_made")
        mod_added = s.sem("mod_added")
        x_free = s.sem("x_free")
        xg_made, xg_free = s.sem("xg_made"), s.sem("xg_free")
        xn_made = s.sem("xn_made")
        x_turned = s.sem("x_turned")
        x_evacuated = s.sem("x_evacuated")
        gate_made, gate_stored = s.sem("gate_made"), s.sem("gate_stored")
        var_made, root_made = s.sem("var_made"), s.sem("root_made")
        dve_own, pool_own, spare = s.sem("dve_own"), s.sem("pool_own"), s.sem("spare")
        block = s.block()
        OWN = 4 * 2 + 4 + 4 * 2

        @block.sync
        def _(sp):
            sp.dma_start(c_col[:, :], T["c"].rearrange("a (p k) -> (a p) k", k=KD)).then_inc(c_loaded, 16)
            for n, name in enumerate(("ln_in_g", "ln_in_b")):
                sp.dma_start(gb[:, n, :], T[name].rearrange("(a d) -> a d", a=1).to_broadcast([P, D])).then_inc(gb_loaded, 16)
            with sp.Fori(0, 4) as i:
                for b in range(4):
                    sp.wait_ge(x_free, i * 4 + b + 1)
                    sp.dma_start(x[:, b, :], T["x"][0, bass.ds((i * 4 + b) * P, P), :]).then_inc(x_loaded[b], 16)
                for a in range(3):
                    sp.wait_ge(mod_added, i * 3 + a + 1)
                    sp.dma_start(w[:, a, :, :], T["w_ada"][0].rearrange("(p k) n -> p k n", k=KD)[:, :, bass.ds((i * 3 + a) * 512, 512)]).then_inc(w_loaded[a], 16)
                    sp.dma_start(b_row[:, a, :], T["b_ada"][:, bass.ds((i * 3 + a) * 512, 512)].to_broadcast([P, 512])).then_inc(w_loaded[a], 16)

        @block.scalar
        def _(act):
            act.sem_inc(x_evacuated, 2)
            for a in range(2):
                act.sem_inc(xt_stored[a], 16)
                act.sem_inc(xn_stored[a], 16)
            act.wait_ge(c_loaded, 16)
            nc.scalar.activation(c_sig[:, :], c_col[:, :], ACT.Sigmoid).then_inc(c_sigmoid, 1)
            with act.Fori(0, 4) as i:
                act.wait_ge(var_made, i + 1)
                nc.scalar.activation(root[:, :], var[:, :], ACT.Sqrt).then_inc(root_made, 1)
                for b in range(4):
                    a = b % 2
                    act.wait_ge(x_turned, i * 4 + b + 3)
                    act.dma_start(W["xn"][bass.ds((i * 4 + b) * P, P), :], xn[:, a, :]).then_inc(xn_stored[a], 16)
                    act.wait_ge(xt_stored[a], i * 32 + (b // 2) * 16 + 16)
                    nc.scalar.activation(xt[:, a, 0:4, :], ps_t[:, 2 * a, :, :], ACT.Copy)
                    nc.scalar.activation(xt[:, a, 4:8, :], ps_t[:, 2 * a + 1, :, :], ACT.Copy).then_inc(x_evacuated, 1)
                    act.wait_ge(x_evacuated, i * 4 + b + 3)
                    act.dma_start(W["xt"].rearrange("(k p) t -> p k t", p=P)[:, :, bass.ds((i * 4 + b) * P, P)], xt[:, a, :, :]).then_inc(xt_stored[a], 16)
            act.wait_ge(gate_made, 1)
            act.dma_start(W["gate"].rearrange("(a g) d -> a g d", a=1), gate[:, :, :]).then_inc(gate_stored, 16)
            act.wait_ge(gate_stored, 16)
            for a in range(2):
                act.wait_ge(xt_stored[a], 16 + 16 * (TILES // 2))
                act.wait_ge(xn_stored[a], 16 + 16 * (TILES // 2))

        @block.gpsimd
        def _(pool):
            pool.sem_inc(xg_free, 2)
            nc.gpsimd.memset(ones[:, :], 1.0).then_inc(ones_set, 1)
            pool.wait_ge(ones_set, 1)
            nc.gpsimd.affine_select(out=R["ident"][:, :], in_=ones[:, :], compare_op=ALU.is_equal, fill=0.0,
                                    base=0, pattern=[[-1, P]], channel_multiplier=1).then_inc(ident_set, 1)
            nc.gpsimd.affine_select(out=R["ident_r"][:, :], in_=ones[:, :], compare_op=ALU.is_equal, fill=0.0,
                                    base=0, pattern=[[-1, P]], channel_multiplier=1)
            nc.gpsimd.memset(R["zeros"][:, :], 0.0).then_inc(pool_own, 1)
            pool.wait_ge(pool_own, 1)
            nc.gpsimd.affine_select(out=R["strict"][:, :], in_=R["zeros"][:, :], compare_op=ALU.is_gt, fill=MASKED,
                                    base=0, pattern=[[-1, P]], channel_multiplier=1)
            nc.gpsimd.affine_select(out=R["halves"][:, :], in_=R["zeros"][:, 0:64], compare_op=ALU.is_ge, fill=MASKED,
                                    base=-64, pattern=[[0, 64]], channel_multiplier=1)
            pool.wait_ge(gb_loaded, 32)
            with pool.Fori(0, TILES // 2) as i:
                for a in range(2):
                    pool.wait_ge(xg_made, i * 2 + a + 1)
                    pool.wait_ge(xn_stored[a], i * 16 + 16)
                    pool.wait_ge(x_turned, i * 2 + a + 1)
                    nc.gpsimd.tensor_tensor(xn[:, a, :], xg[:, a, :], gb[:, 1, :], ALU.add).then_inc(xn_made, 1)
                    pool.wait_ge(xn_made, i * 2 + a + 1)
                    pool.sem_inc(xg_free, 1)

        @block.vector
        def _(dve):
            dve.sem_inc(mod_added, 3)
            dve.sem_inc(x_free, 4)
            dve.wait_ge(c_sigmoid, 1)
            own = Chain(dve, dve_own)
            own.step(nc.vector.tensor_tensor(c_act[:, :], c_col[:, :], c_sig[:, :], ALU.mult))
            dve.wait_ge(ones_set, 1)
            for k in range(KD):
                last = nc.vector.tensor_scalar(c_rep[:, k, :], ones[:, :], c_act[:, k:k + 1], None, ALU.mult)
            last.then_inc(c_ready, 1)
            dve.wait_ge(gb_loaded, 32)
            with dve.Fori(0, 4) as i:
                for a in range(3):
                    dve.wait_ge(mod_summed, i * 3 + a + 1)
                    dve.wait_ge(w_loaded[a], i * 32 + 32)
                    nc.vector.tensor_tensor(mod[:, bass.ds((i * 3 + a) * 512, 512)], ps_mod[:, a, :], b_row[:, a, :], ALU.add).then_inc(mod_added, 1)
                own = Chain(dve, dve_own, i * OWN + 1, spare)
                for b in range(4):
                    dve.wait_ge(x_loaded[b], i * 16 + 16)
                    layer_norm_moments(nc, own, x[:, b, :], stats, moments[:, b, :])
                nc.vector.tensor_scalar(var[:, :], moments[:, :, 1], LN_EPS, None, ALU.add).then_inc(var_made, 1)
                dve.wait_ge(root_made, i + 1)
                refine_rsqrt(nc, own, rstd[:, :], var[:, :], root[:, :], tmp[:, :])
                for b in range(4):
                    own.step(nc.vector.tensor_scalar(xhat[:, :], x[:, b, :], moments[:, b, 0:1], rstd[:, b:b + 1], ALU.subtract, ALU.mult))
                    dve.sem_inc(x_free, 1)
                    dve.wait_ge(xg_free, i * 4 + b + 1)
                    own.step(nc.vector.tensor_tensor(xg[:, b % 2, :], xhat[:, :], gb[:, 0, :], ALU.mult))
                    dve.sem_inc(xg_made, 1)
                assert own.n == OWN
            dve.wait_ge(mod_added, 15)
            nc.vector.tensor_scalar(gate[:, 0, :], mod[0:1, 2 * D:3 * D], 1.0, None, ALU.add)
            nc.vector.tensor_scalar(gate[:, 1, :], mod[0:1, 5 * D:6 * D], 1.0, None, ALU.add).then_inc(gate_made, 1)
            dve.wait_ge(cols_made, 1)
            cols = ps_col[:, 0:4 * KD].rearrange("p (v k) -> p v k", v=4)
            nc.vector.tensor_copy(R["shift"][:, :, :], cols[:, 0::2, :])
            nc.vector.tensor_scalar(R["scale"][:, :, :], cols[:, 1::2, :], 1.0, None, ALU.add)

        @block.tensor
        def _(pe):
            pe.sem_inc(x_turned, 2)
            pe.wait_ge(c_ready, 1)
            pe.wait_ge(ident_set, 1)
            with pe.Fori(0, 4) as i:
                for a in range(3):
                    pe.wait_ge(w_loaded[a], i * 32 + 32)
                    pe.wait_ge(mod_added, i * 3 + a + 1)
                    for k in range(KD):
                        mm = pe.matmul(ps_mod[:, a, :], c_rep[:, k, :], w[:, a, k, :], start=(k == 0), stop=(k == KD - 1))
                    mm.then_inc(mod_summed, 1)
                for b in range(4):
                    a = b % 2
                    pe.wait_ge(xn_made, i * 4 + b + 1)
                    pe.wait_ge(x_evacuated, i * 4 + b + 1)
                    for k in range(KD):
                        mm = pe.transpose(ps_t[:, 2 * a + k // 4, k % 4, :], xn[:, a, k * P:(k + 1) * P], R["ident"][:, :])
                    mm.then_inc(x_turned, 1)
            pe.wait_ge(mod_added, 15)
            for v, m in enumerate((0, 1, 3, 4)):
                for k in range(KD):
                    mm = pe.matmul(ps_col[:, v * KD + k:v * KD + k + 1], mod[0:1, m * D + k * P:m * D + (k + 1) * P], ones[0:1, 0:1], start=True, stop=True)
            mm.then_inc(cols_made, 1)


def phase_projection(nc, T, W, R):
    JOBS, BANKS = 36, 6
    UNIT_JOB = [0, 1, 2, 3, 4, 5, 6, 7, 8, 10, 11, 13, 14, 15]
    STREAM = len(UNIT_JOB)
    SUM_Q, SUM_KV, V_JOB, Q_JOB, K_JOB, LV_JOB = 9, 12, 16, 20, 28, 32
    STAGED_JOBS = [6, 7, 8, 10, 11, 13, 14, 15] + list(range(16, 36))
    STAGED = len(STAGED_JOBS)
    STAGES = 4
    FIXED = 9
    LAT = KQ + KV
    LATENT_AT, ROTARY_AT = 3 * SBW, 3 * SBW + Q_RANK + KV_RANK
    with Scope(nc, "p") as s:
        xraw = s.sb("xraw", [P, 2, TG])
        hmod = s.sb("hmod", [P, 2, TG])
        hh = s.sb("hh", [P, KD, TG], F32R)
        hl = s.sb("hl", [P, KD, TG], F32R)
        wraw = s.sb("wraw", [P, 2, 1024])
        wh = s.sb("wh", [P, 2, 1024], F32R)
        wl = s.sb("wl", [P, 2, 1024], F32R)
        wvh = s.sb("wvh", [P, KD, SBW], F32R)
        wvl = s.sb("wvl", [P, KD, SBW], F32R)
        wqh = s.sb("wqh", [P, KQ, HEADS, P], F32R)
        wql = s.sb("wql", [P, KQ, HEADS, P], F32R)
        wkh = s.sb("wkh", [P, KV, 1024], F32R)
        wkl = s.sb("wkl", [P, KV, 1024], F32R)
        gains = s.sb("gains", [P, LAT])
        ones = s.sb("ones", [P, P])
        lat = s.sb("lat", [P, LAT, TG])
        lsq = s.sb("lsq", [P, KQ, TG])
        var, root, rstd, tmp = (s.sb(n, [P, TG]) for n in ("var", "root", "rstd", "tmp"))
        lath = s.sb("lath", [P, LAT, TG], F32R)
        latl = s.sb("latl", [P, LAT, TG], F32R)
        table = s.sb("table", [P, SEQ])
        turn = s.sb("turn", [P, 2, TG])
        kr = s.sb("kr", [ROPE, TG])
        stage = s.sb("stage", [P, STAGES, TG])
        seed = s.sb("seed", [1, 16])
        ps = s.psum("ps", [P, BANKS, TG])

        xraw_loaded = [s.sem(f"xraw_loaded{i}") for i in range(2)]
        h_made = s.sem("h_made")
        w_loaded = [s.sem(f"w_loaded{i}") for i in range(2)]
        gains_loaded, table_loaded = s.sem("gains_loaded"), s.sem("table_loaded")
        hh_made, hl_made, wh_made, wl_made, ones_set = (s.sem(n) for n in ("hh_made", "hl_made", "wh_made", "wl_made", "ones_set"))
        job_done = s.sem("job_done")
        bank_free = [s.sem(f"bank_free{i}") for i in range(BANKS)]
        lsq_made, var_made, root_made, latn_made = (s.sem(n) for n in ("lsq_made", "var_made", "root_made", "latn_made"))
        lath_made, latl_made = s.sem("lath_made"), s.sem("latl_made")
        act_staged, dve_staged, kr_made = s.sem("act_staged"), s.sem("dve_staged"), s.sem("kr_made")
        stage_free = s.sem("stage_free")
        kr_free = s.sem("kr_free")
        stored = [s.sem(f"stored{i}") for i in range(2)]
        kr_stored, seed_set = s.sem("kr_stored"), s.sem("seed_set")
        dve_own, spare = s.sem("dve_own"), s.sem("spare")
        block = s.block()
        OWN = 2 * (HEADS + 1) + 4 * 2

        fixed_dmas = [1] * 4 + [3] * 3 + [1] * 2
        unit_dmas = [3 if u == 5 else 1 for u in range(STREAM)]

        def arrived(eng, g, m):
            slot = m % 2
            before = sum(n for j, n in enumerate(fixed_dmas) if j % 2 == slot and j <= m)
            if m >= FIXED:
                per_group = sum(n for u, n in enumerate(unit_dmas) if (FIXED + u) % 2 == slot)
                before += sum(n for u, n in enumerate(unit_dmas) if (FIXED + u) % 2 == slot and u <= m - FIXED)
                eng.wait_ge(w_loaded[slot], g * (16 * per_group) + 16 * before)
            else:
                eng.wait_ge(w_loaded[slot], 16 * before)

        def target(m, high):
            w, v, q, k = (wh, wvh, wqh, wkh) if high else (wl, wvl, wql, wkl)
            if m < 4:
                return v[:, 2 * m:2 * m + 2, :].rearrange("p k n -> p (k n)")
            if m < 7:
                return q[:, m - 4, :, :].rearrange("p h n -> p (h n)")
            if m < FIXED:
                return k[:, m - 7, :]
            return w[:, m % 2, 0:KD * 2 * ROPE] if m - FIXED == 5 else w[:, m % 2, :]

        def raw(m):
            return wraw[:, m % 2, 0:KD * 2 * ROPE] if m - FIXED == 5 else wraw[:, m % 2, :]

        def load_fixed(sp, m):
            done = w_loaded[m % 2]
            if m < 4:
                sp.dma_start(raw(m).rearrange("p (k n) -> p k n", k=2),
                             T["w_in"][0, m * 256:(m + 1) * 256, 2 * SBW:3 * SBW].rearrange("(k p) n -> p k n", p=P)).then_inc(done, 16)
            elif m < 7:
                rows = T["w_uq"][0, (m - 4) * P:(m - 3) * P, :].rearrange("p (h n) -> p h n", n=QK)
                to = raw(m).rearrange("p (h n) -> p h n", n=P)
                sp.dma_start(to[:, :, 0:QK], rows).then_inc(done, 16)
                sp.dma_start(to[:, :, QK:QK + 16], rows[:, :, HD + 16:QK]).then_inc(done, 16)
                sp.dma_start(to[:, :, QK + 16:P], rows[:, :, HD:HD + 16]).then_inc(done, 16)
            else:
                sp.dma_start(raw(m), T["w_ukv"][0, (m - 7) * P:(m - 6) * P, :]).then_inc(done, 16)

        def load_unit(sp, u):
            source = T["w_in"][0].rearrange("(k p) n -> p k n", p=P)
            to = raw(FIXED + u).rearrange("p (k n) -> p k n", k=KD)
            done = w_loaded[(FIXED + u) % 2]
            if u == 5:
                c = ROTARY_AT
                sp.dma_start(to[:, :, 0:ROPE], source[:, :, c:c + ROPE]).then_inc(done, 16)
                sp.dma_start(to[:, :, ROPE:ROPE + 16], source[:, :, c + 16:c + ROPE]).then_inc(done, 16)
                sp.dma_start(to[:, :, ROPE + 16:2 * ROPE], source[:, :, c:c + 16]).then_inc(done, 16)
            else:
                c = LATENT_AT + u * P if u < 5 else (u - 6) * P
                sp.dma_start(to, source[:, :, c:c + P]).then_inc(done, 16)

        @block.sync
        def _(sp):
            sp.dma_start(table[:, :], T["rope"]).then_inc(table_loaded, 16)
            with nc.allow_non_contiguous_dma(reason="five columns of gains"):
                sp.dma_start(gains[:, 0:KQ], T["q_norm_g"][0].rearrange("(k p) -> p k", p=P)).then_inc(gains_loaded, 16)
                sp.dma_start(gains[:, KQ:LAT], T["kv_norm_g"][0].rearrange("(k p) -> p k", p=P)).then_inc(gains_loaded, 16)
            for m in range(FIXED):
                if m >= 2:
                    sp.wait_ge(wl_made, m - 1)
                load_fixed(sp, m)
            with sp.Fori(0, NG) as g:
                for u in range(2):
                    sp.wait_ge(wl_made, g * STREAM + FIXED + u - 1)
                    load_unit(sp, u)
                for k in range(KD):
                    sp.wait_ge(h_made, g * KD + k + 1)
                    sp.dma_start(xraw[:, k % 2, :], W["xt"][k * P:(k + 1) * P, bass.ds(g * TG, TG)]).then_inc(xraw_loaded[k % 2], 16)
                for u in range(2, STREAM):
                    sp.wait_ge(wl_made, g * STREAM + FIXED + u - 1)
                    load_unit(sp, u)

        @block.scalar
        def _(act):
            for b in range(BANKS):
                act.sem_inc(bank_free[b], 1)
            act.sem_inc(h_made, 2)
            act.sem_inc(stage_free, 3)

            def high_half(g, m):
                arrived(act, g, m)
                nc.scalar.activation(target(m, True), raw(m), ACT.Copy).then_inc(wh_made, 1)

            def high_slice(g, k, first):
                act.wait_ge(xraw_loaded[k % 2], g * (16 * KD // 2) + 16 * (k // 2 + 1))
                if k >= 2 or not first:
                    act.wait_ge(hl_made, g * KD + k - 1)
                nc.scalar.activation(hmod[:, k % 2, :], xraw[:, k % 2, :], ACT.Identity,
                                     bias=R["shift"][:, 0, k:k + 1], scale=R["scale"][:, 0, k:k + 1]).then_inc(h_made, 1)
                act.wait_ge(h_made, g * KD + k + 3)
                nc.scalar.activation(hh[:, k, :], hmod[:, k % 2, :], ACT.Copy).then_inc(hh_made, 1)

            def to_stage(g, job, rows=P):
                n = STAGED_JOBS.index(job)
                act.wait_ge(job_done, g * JOBS + job + 1)
                act.wait_ge(stage_free, g * STAGED + n + 1)
                out = nc.scalar.activation(stage[0:rows, n % STAGES, :], ps[0:rows, job % BANKS, :], ACT.Copy)
                if rows == P:
                    out.then_inc(bank_free[job % BANKS], 1)
                    act.wait_ge(bank_free[job % BANKS], g * (JOBS // BANKS) + job // BANKS + 2)
                    act.sem_inc(act_staged, 1)
                else:
                    out.then_inc(act_staged, 1)

            def group(g, more):
                for u in range(STREAM):
                    job = UNIT_JOB[u]
                    if u < LAT:
                        act.wait_ge(job_done, g * JOBS + job + 1)
                        if u < KQ:
                            nc.scalar.activation(lsq[:, u, :], ps[:, job % BANKS, :], ACT.Square).then_inc(lsq_made, 1)
                        nc.scalar.activation(lat[:, u, :], ps[:, job % BANKS, :], ACT.Copy).then_inc(bank_free[job % BANKS], 1)
                    elif u == 5:
                        act.wait_ge(job_done, g * JOBS + job + 1)
                    else:
                        to_stage(g, job)
                    if u + 2 < STREAM:
                        high_half(g, FIXED + u + 2)
                    if job == SUM_Q + 1:
                        for j in range(KV):
                            nc.scalar.activation(lsq[:, j, :], lat[:, KQ + j, :], ACT.Square).then_inc(lsq_made, 1)
                        act.wait_ge(var_made, g * 2 + 1)
                        nc.scalar.activation(root[:, :], var[:, :], ACT.Sqrt).then_inc(root_made, 1)
                    if job == SUM_Q + 2:
                        for j in range(KQ):
                            act.wait_ge(latn_made, g * LAT + j + 1)
                            nc.scalar.activation(lath[:, j, :], lat[:, j, :], ACT.Copy).then_inc(lath_made, 1)
                    if job == SUM_KV + 1:
                        act.wait_ge(var_made, g * 2 + 2)
                        nc.scalar.activation(root[:, :], var[:, :], ACT.Sqrt).then_inc(root_made, 1)
                for j in range(KQ, LAT):
                    act.wait_ge(latn_made, g * LAT + j + 1)
                    nc.scalar.activation(lath[:, j, :], lat[:, j, :], ACT.Copy).then_inc(lath_made, 1)
                for t in range(4):
                    to_stage(g, V_JOB + t)
                if more:
                    high_half(g + 1, FIXED)
                    high_half(g + 1, FIXED + 1)
                for h in range(HEADS):
                    to_stage(g, Q_JOB + h, HD)
                    if more:
                        high_slice(g + 1, h, False)
                for job in range(K_JOB, JOBS):
                    to_stage(g, job)

            for m in range(FIXED + 2):
                if m >= FIXED:
                    high_half(0, m)
                else:
                    high_half(0, m)
            for k in range(KD):
                high_slice(0, k, True)
            with act.Fori(0, NG - 1) as g:
                group(g, True)
            group(NG - 1, False)

        @block.vector
        def _(dve):
            def low_half(g, m):
                done = m + 1 if m < FIXED else g * STREAM + m + 1
                dve.wait_ge(wh_made, done)
                nc.vector.tensor_tensor(target(m, False), raw(m), target(m, True).bitcast(F32), ALU.subtract).then_inc(wl_made, 1)

            def low_slice(g, k):
                dve.wait_ge(hh_made, g * KD + k + 1)
                nc.vector.tensor_tensor(hl[:, k, :], hmod[:, k % 2, :], hh[:, k, :].bitcast(F32), ALU.subtract).then_inc(hl_made, 1)

            def rotate(own, g, job, lo, out):
                position = bass.ds(g * TG, TG)
                own.step(nc.vector.tensor_tensor(turn[lo:lo + ROPE, 0, :], ps[lo:lo + ROPE, job % BANKS, :], table[lo:lo + ROPE, position], ALU.mult))
                own.step(nc.vector.tensor_tensor(turn[lo:lo + ROPE, 1, :], ps[lo + ROPE:lo + 2 * ROPE, job % BANKS, :], table[lo + ROPE:lo + 2 * ROPE, position], ALU.mult))
                return nc.vector.tensor_tensor(out, turn[lo:lo + ROPE, 0, :], turn[lo:lo + ROPE, 1, :], ALU.add)

            def normalise(own, g, which, first, last, width):
                job = (SUM_Q, SUM_KV)[which]
                dve.wait_ge(job_done, g * JOBS + job + 1)
                nc.vector.tensor_scalar(var[:, :], ps[:, job % BANKS, :], 1.0 / width, RMS_EPS, ALU.mult, ALU.add).then_inc(var_made, 1)
                dve.wait_ge(var_made, g * 2 + which + 1)
                dve.sem_inc(bank_free[job % BANKS], 1)
                dve.wait_ge(root_made, g * 2 + which + 1)
                refine_rsqrt(nc, own, rstd[:, :], var[:, :], root[:, :], tmp[:, :])
                for j in range(first, last):
                    nc.vector.scalar_tensor_tensor(out=lat[:, j, :], in0=lat[:, j, :], scalar=gains[:, j:j + 1], in1=rstd[:, :],
                                                   op0=ALU.mult, op1=ALU.mult).then_inc(latn_made, 1)

            def low_latents(g, first, last):
                for j in range(first, last):
                    dve.wait_ge(lath_made, g * LAT + j + 1)
                    nc.vector.tensor_tensor(latl[:, j, :], lat[:, j, :], lath[:, j, :].bitcast(F32), ALU.subtract).then_inc(latl_made, 1)

            def group(g, more):
                own = Chain(dve, dve_own, g * OWN)
                for u in range(STREAM):
                    job = UNIT_JOB[u]
                    if u == 5:
                        dve.wait_ge(job_done, g * JOBS + job + 1)
                        dve.wait_ge(kr_free, g + 1)
                        rotate(own, g, job, 0, kr[:, :]).then_inc(kr_made, 1)
                        dve.sem_inc(bank_free[job % BANKS], 1)
                    if u + 2 < STREAM:
                        low_half(g, FIXED + u + 2)
                    if job == SUM_Q + 1:
                        normalise(own, g, 0, 0, KQ, Q_RANK)
                    if job == SUM_Q + 2:
                        low_latents(g, 0, KQ)
                    if job == SUM_KV + 1:
                        dve.wait_ge(latn_made, g * LAT + KQ)
                        normalise(own, g, 1, KQ, LAT, KV_RANK)
                low_latents(g, KQ, LAT)
                if more:
                    low_half(g + 1, FIXED)
                    low_half(g + 1, FIXED + 1)
                for h in range(HEADS):
                    n = STAGED_JOBS.index(Q_JOB + h)
                    dve.wait_ge(job_done, g * JOBS + Q_JOB + h + 1)
                    if h:
                        dve.wait_ge(dve_staged, g * HEADS + h)
                    dve.wait_ge(act_staged, g * STAGED + n + 1)
                    rotate(own, g, Q_JOB + h, HD, stage[HD:QK, n % STAGES, :]).then_inc(dve_staged, 1)
                    dve.sem_inc(bank_free[(Q_JOB + h) % BANKS], 1)
                    if more:
                        low_slice(g + 1, h)
                dve.wait_ge(dve_staged, g * HEADS + HEADS)
                assert own.n == OWN

            dve.wait_ge(table_loaded, 16)
            dve.wait_ge(gains_loaded, 32)
            for m in range(FIXED + 2):
                low_half(0, m)
            for k in range(KD):
                low_slice(0, k)
            with dve.Fori(0, NG - 1) as g:
                group(g, True)
            group(NG - 1, False)

        @block.gpsimd
        def _(pool):
            nc.gpsimd.memset(ones[:, :], 1.0).then_inc(ones_set, 1)
            nc.gpsimd.memset(seed[:, :], 0.0).then_inc(seed_set, 1)
            pool.sem_inc(kr_free, 1)
            pool.wait_ge(seed_set, 1)
            pool.dma_start(W["seed"], seed[:, :]).then_inc(stored[1], 16)

            def target_of(g, job):
                tokens = bass.ds(g * TG, TG)
                if job < V_JOB:
                    r = UNIT_JOB.index(job) - 6
                    return W["qk"][r * P:(r + 1) * P, tokens], P
                if job < Q_JOB:
                    return W["v"][bass.ds(g * TG + (job - V_JOB) * P, P), :], P
                if job < K_JOB:
                    return W["lq"][job - Q_JOB][:, tokens], QK
                if job < LV_JOB:
                    return W["lk"][(job - K_JOB) * P:(job - K_JOB + 1) * P, tokens], P
                return W["lv"][bass.ds(g * TG + (job - LV_JOB) * P, P), :], P

            with pool.Fori(0, NG) as g:
                for n, job in enumerate(STAGED_JOBS):
                    if Q_JOB <= job < K_JOB:
                        pool.wait_ge(dve_staged, g * HEADS + job - Q_JOB + 1)
                    pool.wait_ge(act_staged, g * STAGED + n + 1)
                    pool.sem_inc(spare, 1)
                    to, rows = target_of(g, job)
                    pool.dma_start(to, stage[0:rows, n % STAGES, :]).then_inc(stored[n % 2], 16)
                    before = (n - 1) % 2
                    uses = g * (STAGED // 2) + ((n - 1) // 2 + 1) + before
                    pool.wait_ge(stored[before], uses * 16)
                    pool.sem_inc(stage_free, 1)
                    if n == 0:
                        pool.wait_ge(kr_made, g + 1)
                        pool.sem_inc(spare, 1)
                        pool.dma_start(W["lkr"][:, bass.ds(g * TG, TG)], kr[:, :]).then_inc(kr_stored, 16)
                        pool.wait_ge(kr_stored, g * 16 + 16)
                        pool.sem_inc(kr_free, 1)
            pool.wait_ge(stored[0], 16 * NG * STAGED // 2)
            pool.wait_ge(stored[1], 16 * (NG * STAGED // 2 + 1))

        @block.tensor
        def _(pe):
            def open_job(g, job):
                pe.wait_ge(bank_free[job % BANKS], g * (JOBS // BANKS) + job // BANKS + 1)
                return ps[:, job % BANKS, :]

            def squares_summed(g, job, first, n):
                pe.wait_ge(lsq_made, g * LAT + first + n)
                bank = open_job(g, job)
                for j in range(n):
                    mm = pe.matmul(bank, ones[:, :], lsq[:, j, :], start=(j == 0), stop=(j == n - 1))
                mm.then_inc(job_done, 1)

            pe.wait_ge(ones_set, 1)
            with pe.Fori(0, NG) as g:
                for u in range(STREAM):
                    job = UNIT_JOB[u]
                    if job == SUM_Q + 1:
                        squares_summed(g, SUM_Q, 0, KQ)
                    if job == SUM_KV + 1:
                        squares_summed(g, SUM_KV, KQ, KV)
                    m = FIXED + u
                    width = 2 * ROPE if u == 5 else P
                    high = target(m, True).rearrange("p (k n) -> p k n", k=KD)
                    low = target(m, False).rearrange("p (k n) -> p k n", k=KD)
                    pe.wait_ge(wl_made, g * STREAM + m + 1)
                    out = open_job(g, job)[0:width, :]
                    for k in range(KD):
                        if u == 0:
                            pe.wait_ge(hl_made, g * KD + k + 1)
                        mm = products(pe, out, high[:, k, :], low[:, k, :], hh[:, k, :], hl[:, k, :], k == 0, k == KD - 1)
                    mm.then_inc(job_done, 1)
                for t in range(4):
                    out = open_job(g, V_JOB + t)
                    rows = slice(t * P, (t + 1) * P)
                    for k in range(KD):
                        mm = products(pe, out, hh[:, k, rows], hl[:, k, rows], wvh[:, k, :], wvl[:, k, :], k == 0, k == KD - 1)
                    mm.then_inc(job_done, 1)
                pe.wait_ge(latl_made, g * LAT + LAT)
                for h in range(HEADS):
                    out = open_job(g, Q_JOB + h)
                    for k in range(KQ):
                        mm = products(pe, out, wqh[:, k, h, :], wql[:, k, h, :], lath[:, k, :], latl[:, k, :], k == 0, k == KQ - 1)
                    mm.then_inc(job_done, 1)
                for t in range(4):
                    out = open_job(g, K_JOB + t)
                    cols = slice(t * P, (t + 1) * P)
                    for k in range(KV):
                        mm = products(pe, out, wkh[:, k, cols], wkl[:, k, cols], lath[:, KQ + k, :], latl[:, KQ + k, :], k == 0, k == KV - 1)
                    mm.then_inc(job_done, 1)
                for t in range(4):
                    out = open_job(g, LV_JOB + t)
                    rows = slice(t * P, (t + 1) * P)
                    for k in range(KV):
                        mm = products(pe, out, lath[:, KQ + k, rows], latl[:, KQ + k, rows], wkh[:, k, 512:1024], wkl[:, k, 512:1024], k == 0, k == KV - 1)
                    mm.then_inc(job_done, 1)


S_BANKS, T_BANKS = 5, 2


def chunks_of(qb):
    length = (qb + 1) * P
    return [slice(c, min(c + 512, length)) for c in range(0, length, 512)]


def chunk_base(qb):
    return sum(len(chunks_of(q)) for q in range(qb))


CHUNKS = chunk_base(TILES)


class AttentionSide:

    def __init__(self, nc, s, W, row0):
        self.nc, self.W, self.row0 = nc, W, row0
        self.v_raw = s.sb("v_raw", [P, TILES, HD])
        self.v_halves = [s.sb(f"v_halves{a}", [P, TILES, 2 * HD], F32R) for a in range(2)]
        self.turned_high = s.sb("turned_high", [P, TILES, TG], F32R)
        self.turned_low = s.sb("turned_low", [P, TILES, TG], F32R)
        self.y_low = s.sb("y_low", [HD, TG])
        self.y = s.sb("y", [HD, 2, TG])
        self.ps_s = s.psum("ps_s", [P, S_BANKS, 512])
        self.ps_t = s.psum("ps_t", [P, T_BANKS, 4, P])
        self.ps_y = s.psum("ps_y", [P, TG])
        sem = s.sem
        self.raw_loaded, self.split_high, self.split_low = sem("raw_loaded"), sem("split_high"), sem("split_low")
        self.scores_done = sem("scores_done")
        self.scores_used = sem("scores_used")
        self.weights_made = sem("weights_made")
        self.turn_done = sem("turn_done")
        self.high_done = sem("high_done")
        self.low_done = sem("low_done")
        self.values_done = sem("values_done")
        self.y_low_made = sem("y_low_made")
        self.y_made = sem("y_made")
        self.y_stored = [sem(f"y_stored{i}") for i in range(2)]

    def turn(self, pe, H, qb, order, weights, ident):
        for j, cols in enumerate(order):
            n = chunk_base(qb) + j
            pe.wait_ge(self.weights_made, H * CHUNKS + n + 1)
            pe.wait_ge(self.low_done, H * CHUNKS + n + 1)
            for b in range((cols.stop - cols.start) // P):
                at = cols.start + b * P
                mm = pe.transpose(self.ps_t[:, n % T_BANKS, b, :], weights[:, at:at + P], ident[:, :])
            mm.then_inc(self.turn_done, 1)

    def values(self, pe, H, qb, order, a):
        group = qb // 4
        pe.wait_ge(self.y_made, H * NG + group + 1)
        first = True
        for j, cols in enumerate(order):
            pe.wait_ge(self.low_done, H * CHUNKS + chunk_base(qb) + j + 1 + T_BANKS)
            for kb in range(cols.start // P, cols.stop // P):
                lo = max(0, kb - 4 * group) * P
                last = j == len(order) - 1 and kb == cols.stop // P - 1
                pe.matmul(self.ps_y[:, lo:TG], self.v_halves[a][:, kb, :], self.turned_high[:, kb, lo:TG], start=first, stop=False)
                mm = pe.matmul(self.ps_y[:, lo:TG], self.v_halves[a][:, kb, :], self.turned_low[:, kb, lo:TG], start=False, stop=last)
                first = False
        mm.then_inc(self.values_done, 1)

    def blocks(self, cols, qb, halves):
        at = (qb % 4) * P
        return halves[:, cols.start // P:cols.stop // P, at:at + P]

    def late_scalar(self, act, H, qb, order):
        nc = self.nc
        for j, cols in enumerate(order):
            n = chunk_base(qb) + j
            act.wait_ge(self.turn_done, H * CHUNKS + n + 1)
            if j == 0:
                act.wait_ge(self.values_done, H * NG + qb // 4 + 1)
            nb = (cols.stop - cols.start) // P
            nc.scalar.activation(self.blocks(cols, qb, self.turned_high), self.ps_t[:, n % T_BANKS, 0:nb, :], ACT.Copy).then_inc(self.high_done, 1)
        if qb % 4 == 3:
            act.wait_ge(self.values_done, H * NG + qb // 4 + 2)
            act.wait_ge(self.y_made, H * NG + qb // 4 + 1)
            nc.scalar.activation(self.y_low[:, :], self.ps_y[HD:P, :], ACT.Copy).then_inc(self.y_low_made, 1)

    def late_vector(self, dve, H, qb, order):
        nc = self.nc
        for j, cols in enumerate(order):
            n = chunk_base(qb) + j
            dve.wait_ge(self.high_done, H * CHUNKS + n + 1)
            nb = (cols.stop - cols.start) // P
            nc.vector.tensor_tensor(self.blocks(cols, qb, self.turned_low), self.ps_t[:, n % T_BANKS, 0:nb, :],
                                    self.blocks(cols, qb, self.turned_high).bitcast(F32), ALU.subtract).then_inc(self.low_done, 1)
        if qb % 4 == 3:
            group = qb // 4
            dve.wait_ge(self.y_low_made, H * NG + group + 1)
            dve.wait_ge(self.y_stored[group % 2], H * 32 + (group // 2) * 16 + 16)
            nc.vector.tensor_tensor(self.y[:, group % 2, :], self.ps_y[0:HD, :], self.y_low[:, :], ALU.add).then_inc(self.y_made, 1)

    def load_values(self, sp, H, name):
        source = self.W[name].rearrange("(b p) n -> p b n", p=P)
        sp.dma_start(self.v_raw[:, :, :], source[:, :, bass.ds(H * HD, HD)]).then_inc(self.raw_loaded, 16)

    def store(self, sp, H):
        for group in range(NG):
            sp.wait_ge(self.y_made, H * NG + group + 2)
            sp.dma_start(self.W["yt"][bass.ds(self.row0 + H * HD, HD), group * TG:(group + 1) * TG], self.y[:, group % 2, :]).then_inc(self.y_stored[group % 2], 16)

    def all_stored(self, sp):
        for i in range(2):
            sp.wait_ge(self.y_stored[i], 16 + 16 * HEADS * NG // 2)


def over_heads(eng, step, late_tail):
    def pair(i, begun, more):
        for a in range(2):
            for qb in range(TILES):
                step(i * 2 + a, a, qb, begun or a > 0 or qb > 0, more or a == 0)
    pair(0, False, True)
    with eng.Fori(1, HEADS // 2 - 1) as i:
        pair(i, True, True)
    pair(HEADS // 2 - 1, True, False)
    late_tail(HEADS - 1)


def before(H, a, qb):
    return (H, a, qb - 1) if qb else (H - 1, 1 - a, TILES - 1)


SPLIT_STEP = 8


def phase_stick_breaking(nc, T, W, R):
    with Scope(nc, "s") as s:
        side = AttentionSide(nc, s, W, 0)
        q_raw = s.sb("q_raw", [P, SEQ])
        k_raw = s.sb("k_raw", [P, SEQ])
        q_stack = [s.sb(f"q_stack{a}", [P, SEQ], F32R) for a in range(2)]
        k_high = [s.sb(f"k_high{a}", [P, SEQ], F32R) for a in range(2)]
        k_low = [s.sb(f"k_low{a}", [P, SEQ], F32R) for a in range(2)]
        sig = s.sb("sig", [P, 2, SEQ])
        weights = s.sb("weights", [P, 2, SEQ])
        later = s.sb("later", [P, 2, SEQ + 8])
        sig_made = side.scores_used
        keep_made, scanned, later_set = s.sem("keep_made"), s.sem("scanned"), s.sem("later_set")
        block = s.block()

        def order(qb):
            return chunks_of(qb)[::-1]

        @block.sync
        def _(sp):
            for i in range(2):
                sp.sem_inc(side.y_stored[i], 16)

            def load(H):
                for half in range(2):
                    sp.dma_start(q_raw[half * HD:(half + 1) * HD, :], W["qk"][bass.ds(H * HD, HD), :]).then_inc(side.raw_loaded, 16)
                    sp.dma_start(k_raw[half * HD:(half + 1) * HD, :], W["qk"][bass.ds(SBW + H * HD, HD), :]).then_inc(side.raw_loaded, 16)
                side.load_values(sp, H, "v")
            load(0)
            with sp.Fori(0, HEADS - 1) as H:
                sp.wait_ge(side.split_low, H * 3 + 3)
                load(H + 1)
                side.store(sp, H)
            side.store(sp, HEADS - 1)
            side.all_stored(sp)

        @block.scalar
        def _(act):
            def split(H, a):
                act.wait_ge(side.raw_loaded, H * 80 + 80)
                nc.scalar.activation(q_stack[a][:, :], q_raw[:, :], ACT.Copy).then_inc(side.split_high, 1)
                nc.scalar.activation(k_high[a][:, :], k_raw[:, :], ACT.Copy).then_inc(side.split_high, 1)
                nc.scalar.activation(side.v_halves[a][:, :, 0:HD], side.v_raw[:, :, :], ACT.Copy).then_inc(side.split_high, 1)

            def step(H, a, qb, begun, more):
                todo = order(qb)

                def keep(j):
                    n = chunk_base(qb) + j
                    act.wait_ge(sig_made, H * CHUNKS + n + 1 + S_BANKS)
                    nc.scalar.activation(weights[:, qb % 2, todo[j]], sig[:, qb % 2, todo[j]], ACT.Copy, scale=-1.0, bias=1.0).then_inc(keep_made, 1)

                for j, cols in enumerate(todo):
                    n = chunk_base(qb) + j
                    act.wait_ge(side.scores_done, H * CHUNKS + n + 1)
                    nc.scalar.activation(sig[:, qb % 2, cols], side.ps_s[:, n % S_BANKS, 0:cols.stop - cols.start], ACT.Sigmoid, scale=SB_SCALE).then_inc(sig_made, 1)
                    if j:
                        keep(j - 1)
                keep(len(todo) - 1)
                if begun:
                    h, _, q = before(H, a, qb)
                    side.late_scalar(act, h, q, order(q))
                if qb == SPLIT_STEP and more:
                    split(H + 1, 1 - a)

            act.sem_inc(side.scores_used, S_BANKS)
            split(0, 0)
            over_heads(act, step, lambda H: side.late_scalar(act, H, TILES - 1, order(TILES - 1)))

        @block.vector
        def _(dve):
            def split(H, a):
                dve.wait_ge(side.split_high, H * 3 + 1)
                nc.vector.tensor_tensor(q_stack[a][HD:P, :], q_raw[HD:P, :], q_stack[a][HD:P, :].bitcast(F32), ALU.subtract).then_inc(side.split_low, 1)
                dve.wait_ge(side.split_high, H * 3 + 2)
                nc.vector.tensor_tensor(k_low[a][:, :], k_raw[:, :], k_high[a][:, :].bitcast(F32), ALU.subtract).then_inc(side.split_low, 1)
                dve.wait_ge(side.split_high, H * 3 + 3)
                nc.vector.tensor_tensor(side.v_halves[a][:, :, HD:P], side.v_raw[:, :, :], side.v_halves[a][:, :, 0:HD].bitcast(F32), ALU.subtract).then_inc(side.split_low, 1)

            def step(H, a, qb, begun, more):
                for j, cols in enumerate(order(qb)):
                    n = chunk_base(qb) + j
                    dve.wait_ge(keep_made, H * CHUNKS + n + 1)
                    if j:
                        dve.wait_ge(scanned, H * CHUNKS + n)
                    back = slice(cols.stop - 1, cols.start - 1 if cols.start else None, -1)
                    start = later[:, qb % 2, cols.stop:cols.stop + 1] if j else 1.0
                    keeps = weights[:, qb % 2, back]
                    nc.vector.tensor_tensor_scan(later[:, qb % 2, back], keeps, keeps, start, ALU.mult, ALU.bypass).then_inc(scanned, 1)
                if begun:
                    h, _, q = before(H, a, qb)
                    side.late_vector(dve, h, q, order(q))
                if qb == SPLIT_STEP and more:
                    split(H + 1, 1 - a)

            nc.vector.memset(later[:, :, :], 1.0).then_inc(later_set, 1)
            dve.wait_ge(later_set, 1)
            dve.sem_inc(side.low_done, T_BANKS)
            dve.sem_inc(side.y_made, 1)
            split(0, 0)
            over_heads(dve, step, lambda H: side.late_vector(dve, H, TILES - 1, order(TILES - 1)))

        @block.gpsimd
        def _(pool):
            def step(H, a, qb, begun, more):
                for j, cols in enumerate(order(qb)):
                    pool.wait_ge(scanned, H * CHUNKS + chunk_base(qb) + j + 1)
                    nc.gpsimd.tensor_tensor(weights[:, qb % 2, cols], sig[:, qb % 2, cols], later[:, qb % 2, cols.start + 1:cols.stop + 1], ALU.mult).then_inc(side.weights_made, 1)
            over_heads(pool, step, lambda H: None)

        @block.tensor
        def _(pe):
            def step(H, a, qb, begun, more):
                if qb == 0:
                    pe.wait_ge(side.split_low, H * 3 + 3)
                queries = q_stack[a][:, qb * P:(qb + 1) * P]
                for j, cols in enumerate(order(qb)):
                    n = chunk_base(qb) + j
                    pe.wait_ge(side.scores_used, H * CHUNKS + n + 1)
                    width = cols.stop - cols.start
                    out = side.ps_s[:, n % S_BANKS, 0:width]
                    pe.matmul(out, queries, k_high[a][:, cols], start=True, stop=False)
                    mm = pe.matmul(out, queries, k_low[a][:, cols], start=False, stop=(j > 0))
                    if j == 0:
                        mm = pe.matmul(out[:, width - P:width], R["ident_r"][:, :], R["strict"][:, :], start=False, stop=True)
                    mm.then_inc(side.scores_done, 1)
                if begun:
                    late(*before(H, a, qb))

            def late(H, a, qb):
                side.turn(pe, H, qb, order(qb), weights[:, qb % 2, :], R["ident"])
                if qb % 4 == 3:
                    side.values(pe, H, qb, order(qb), a)

            pe.sem_inc(side.values_done, 1)
            over_heads(pe, step, lambda H: late(H, 1, TILES - 1))


def phase_latent_attention(nc, T, W, R):
    with Scope(nc, "l") as s:
        side = AttentionSide(nc, s, W, SBW)
        q_raw = s.sb("q_raw", [QK, SEQ])
        k_raw = s.sb("k_raw", [QK, SEQ])
        q_high, q_low, k_high, k_low = ([s.sb(f"{n}{a}", [QK, SEQ], F32R) for a in range(2)] for n in ("q_high", "q_low", "k_high", "k_low"))
        weights = s.sb("weights", [P, 2, SEQ])
        chunk_max = s.sb("chunk_max", [P, 4])
        minus_max = s.sb("minus_max", [P, 1])
        bias = s.sb("bias", [P, 2])
        sums = s.sb("sums", [P, 2, 4])
        total = s.sb("total", [P, 1])
        inverse = s.sb("inverse", [P, 2])
        exp_made = side.scores_used
        bias_made, inverse_made, dve_own, spare = s.sem("bias_made"), s.sem("inverse_made"), s.sem("dve_own"), s.sem("spare")
        block = s.block()
        OWN = CHUNKS + 2 * TILES

        @block.sync
        def _(sp):
            for i in range(2):
                sp.sem_inc(side.y_stored[i], 16)

            def load(H):
                lq = W["lq"].rearrange("h r t -> (h r) t")
                sp.dma_start(q_raw[:, :], lq[bass.ds(H * QK, QK), :]).then_inc(side.raw_loaded, 16)
                sp.dma_start(k_raw[0:HD, :], W["lk"][bass.ds(H * HD, HD), :]).then_inc(side.raw_loaded, 16)
                sp.dma_start(k_raw[HD:QK, :], W["lkr"]).then_inc(side.raw_loaded, 16)
                side.load_values(sp, H, "lv")
            load(0)
            with sp.Fori(0, HEADS - 1) as H:
                sp.wait_ge(side.split_low, H * 3 + 3)
                load(H + 1)
                side.store(sp, H)
            side.store(sp, HEADS - 1)
            side.all_stored(sp)

        @block.scalar
        def _(act):
            def split(H, a):
                act.wait_ge(side.raw_loaded, H * 64 + 64)
                nc.scalar.activation(q_high[a][:, :], q_raw[:, :], ACT.Copy).then_inc(side.split_high, 1)
                nc.scalar.activation(k_high[a][:, :], k_raw[:, :], ACT.Copy).then_inc(side.split_high, 1)
                nc.scalar.activation(side.v_halves[a][:, :, 0:HD], side.v_raw[:, :, :], ACT.Copy).then_inc(side.split_high, 1)

            def step(H, a, qb, begun, more):
                act.wait_ge(bias_made, H * TILES + qb + 1)
                for j, cols in enumerate(chunks_of(qb)):
                    n = chunk_base(qb) + j
                    nc.scalar.activation(weights[:, qb % 2, cols], side.ps_s[:, n % S_BANKS, 0:cols.stop - cols.start], ACT.Exp,
                                         bias=bias[:, qb % 2:qb % 2 + 1], scale=MLA_SCALE, accum_out=sums[:, qb % 2, j:j + 1]).then_inc(exp_made, 1)
                if begun:
                    h, _, q = before(H, a, qb)
                    side.late_scalar(act, h, q, chunks_of(q))
                if qb == SPLIT_STEP and more:
                    split(H + 1, 1 - a)

            act.sem_inc(side.scores_used, S_BANKS)
            split(0, 0)
            over_heads(act, step, lambda H: side.late_scalar(act, H, TILES - 1, chunks_of(TILES - 1)))

        @block.vector
        def _(dve):
            def split(H, a):
                for n, (low, raw, high) in enumerate(((q_low[a], q_raw, q_high[a]), (k_low[a], k_raw, k_high[a]))):
                    dve.wait_ge(side.split_high, H * 3 + n + 1)
                    nc.vector.tensor_tensor(low[:, :], raw[:, :], high[:, :].bitcast(F32), ALU.subtract).then_inc(side.split_low, 1)
                dve.wait_ge(side.split_high, H * 3 + 3)
                nc.vector.tensor_tensor(side.v_halves[a][:, :, HD:P], side.v_raw[:, :, :], side.v_halves[a][:, :, 0:HD].bitcast(F32), ALU.subtract).then_inc(side.split_low, 1)

            def own_count(H, qb):
                return H * OWN + chunk_base(qb) + 2 * qb

            def invert(H, qb):
                nch = len(chunks_of(qb))
                dve.wait_ge(exp_made, H * CHUNKS + chunk_base(qb) + nch + S_BANKS)
                own = Chain(dve, dve_own, own_count(H, qb) + nch + 1)
                own.step(nc.vector.reduce_sum(total[:, :], sums[:, qb % 2, 0:nch], mybir.AxisListType.X))
                nc.vector.reciprocal(inverse[:, qb % 2:qb % 2 + 1], total[:, :]).then_inc(inverse_made, 1)

            def step(H, a, qb, begun, more):
                if begun:
                    h, _, q = before(H, a, qb)
                    invert(h, q)
                todo = chunks_of(qb)
                own = Chain(dve, dve_own, own_count(H, qb))
                for j, cols in enumerate(todo):
                    n = chunk_base(qb) + j
                    dve.wait_ge(side.scores_done, H * CHUNKS + n + 1)
                    own.n += 1
                    nc.vector.reduce_max(chunk_max[:, j:j + 1], side.ps_s[:, n % S_BANKS, 0:cols.stop - cols.start], mybir.AxisListType.X).then_inc(dve_own, 1)
                dve.wait_ge(dve_own, own_count(H, qb) + len(todo))
                own.step(nc.vector.reduce_max(minus_max[:, :], chunk_max[:, 0:len(todo)], mybir.AxisListType.X))
                nc.vector.tensor_scalar(bias[:, qb % 2:qb % 2 + 1], minus_max[:, :], -MLA_SCALE, None, ALU.mult).then_inc(bias_made, 1)
                if begun:
                    side.late_vector(dve, h, q, chunks_of(q))
                if qb == SPLIT_STEP and more:
                    split(H + 1, 1 - a)

            def tail(H):
                invert(H, TILES - 1)
                side.late_vector(dve, H, TILES - 1, chunks_of(TILES - 1))

            dve.sem_inc(side.low_done, T_BANKS)
            dve.sem_inc(side.y_made, 1)
            split(0, 0)
            over_heads(dve, step, tail)

        @block.gpsimd
        def _(pool):
            def step(H, a, qb, begun, more):
                pool.wait_ge(inverse_made, H * TILES + qb + 1)
                pool.sem_inc(spare, 1)
                for cols in chunks_of(qb):
                    nc.gpsimd.tensor_scalar(weights[:, qb % 2, cols], weights[:, qb % 2, cols], inverse[:, qb % 2:qb % 2 + 1], None, ALU.mult).then_inc(side.weights_made, 1)
            over_heads(pool, step, lambda H: None)

        @block.tensor
        def _(pe):
            def step(H, a, qb, begun, more):
                if qb == 0:
                    pe.wait_ge(side.split_low, H * 3 + 3)
                rows = slice(qb * P, (qb + 1) * P)
                todo = chunks_of(qb)
                for j, cols in enumerate(todo):
                    n = chunk_base(qb) + j
                    pe.wait_ge(side.scores_used, H * CHUNKS + n + 1)
                    width = cols.stop - cols.start
                    out = side.ps_s[:, n % S_BANKS, 0:width]
                    diagonal = j == len(todo) - 1
                    mm = products(pe, out, q_high[a][:, rows], q_low[a][:, rows], k_high[a][:, cols], k_low[a][:, cols], True, not diagonal)
                    if diagonal:
                        mm = pe.matmul(out[:, width - 64:width], R["ident_r"][:, :], R["halves"][:, :], start=False, stop=True)
                    mm.then_inc(side.scores_done, 1)
                if begun:
                    late(*before(H, a, qb))

            def late(H, a, qb):
                side.turn(pe, H, qb, chunks_of(qb), weights[:, qb % 2, :], R["ident"])
                if qb % 4 == 3:
                    side.values(pe, H, qb, chunks_of(qb), a)

            pe.sem_inc(side.values_done, 1)
            over_heads(pe, step, lambda H: late(H, 1, TILES - 1))


def load_rows(sp, s_loaded, W, T, gates, gate, gain, bias):
    sp.dma_start(gates[:, 0, :], W["gate"][gate:gate + 1, :].to_broadcast([P, D])).then_inc(s_loaded, 16)
    sp.dma_start(gates[:, 1, :], T[gain].to_broadcast([P, D])).then_inc(s_loaded, 16)
    sp.dma_start(gates[:, 2, :], T[bias].to_broadcast([P, D])).then_inc(s_loaded, 16)


def phase_output_projection(nc, T, W, R):
    PAIRS = TILES // 2
    PIECES = 4
    with Scope(nc, "o") as s:
        wraw = s.sb("wraw", [P, 2, 2, D])
        wh = s.sb("wh", [P, KD, D], F32R)
        wl = s.sb("wl", [P, KD, D], F32R)
        yraw = s.sb("yraw", [P, 2, KD, P])
        yh = s.sb("yh", [P, 2, KD, P], F32R)
        yl = s.sb("yl", [P, 2, KD, P], F32R)
        rows = s.sb("rows", [P, 3, D])
        xn = s.sb("xn", [P, 2, D])
        z = s.sb("z", [P, 2, D])
        xhat = s.sb("xhat", [P, D])
        xg = s.sb("xg", [P, 2, D])
        x1 = s.sb("x1", [P, 2, D])
        h2 = s.sb("h2", [P, 2, KD, P])
        stats = s.sb("stats", [P, 2, 6])
        moments = s.sb("moments", [P, 2, 2])
        var, root, rstd, tmp = (s.sb(n, [P, 2]) for n in ("var", "root", "rstd", "tmp"))
        ps = s.psum("ps", [P, 2, D])
        ps_t = s.psum("ps_t", [P, 2, KD, P])
        rows_loaded = s.sem("rows_loaded")
        w_loaded = [s.sem(f"w_loaded{i}") for i in range(2)]
        y_loaded = [s.sem(f"y_loaded{i}") for i in range(2)]
        xn_loaded = [s.sem(f"xn_loaded{i}") for i in range(2)]
        wh_made, wl_made, yh_made = s.sem("wh_made"), s.sem("wl_made"), s.sem("yh_made")
        yl_made = s.sem("yl_made")
        mixed = s.sem("mixed")
        gated = s.sem("gated")
        summed = s.sem("summed")
        var_made, root_made, xg_made = s.sem("var_made"), s.sem("root_made"), s.sem("xg_made")
        xg_free = s.sem("xg_free")
        x1_made, x1_turned, h2_made = s.sem("x1_made"), s.sem("x1_turned"), s.sem("h2_made")
        x1_free = s.sem("x1_free")
        x1_stored = [s.sem(f"x1_stored{i}") for i in range(2)]
        h2_stored = [s.sem(f"h2_stored{i}") for i in range(2)]
        dve_own, spare = s.sem("dve_own"), s.sem("spare")
        block = s.block()
        OWN = 2 * 1 + 2 * 2 + 4 + 2 * 2

        @block.sync
        def _(sp):
            load_rows(sp, rows_loaded, W, T, rows, 0, "ln1_g", "ln1_b")
            for m in range(PIECES):
                if m >= 2:
                    sp.wait_ge(wl_made, m - 1)
                sp.dma_start(wraw[:, m % 2, :, :], T["w_o"][0, m * 256:(m + 1) * 256, :].rearrange("(k p) n -> p k n", p=P)).then_inc(w_loaded[m % 2], 16)
            with sp.Fori(0, PAIRS) as i:
                for a in range(2):
                    tokens = bass.ds((i * 2 + a) * P, P)
                    sp.wait_ge(yl_made, i * 2 + a + 1)
                    sp.dma_start(yraw[:, a, :, :], W["yt"].rearrange("(k p) t -> p k t", p=P)[:, :, tokens]).then_inc(y_loaded[a], 16)
                    sp.wait_ge(summed, i * 2 + a + 1)
                    sp.dma_start(xn[:, a, :], W["xn"][tokens, :]).then_inc(xn_loaded[a], 16)

        @block.scalar
        def _(act):
            act.sem_inc(x1_free, 2)
            for a in range(2):
                act.sem_inc(h2_stored[a], 16)
            for m in range(PIECES):
                act.wait_ge(w_loaded[m % 2], 16 * (m // 2 + 1))
                nc.scalar.activation(wh[:, 2 * m:2 * m + 2, :], wraw[:, m % 2, :, :], ACT.Copy).then_inc(wh_made, 1)

            def high(i, a):
                act.wait_ge(y_loaded[a], i * 16 + 16)
                nc.scalar.activation(yh[:, a, :, :], yraw[:, a, :, :], ACT.Copy).then_inc(yh_made, 1)

            def late(i):
                for a in range(2):
                    act.wait_ge(x1_turned, i * 2 + a + 1)
                    act.dma_start(W["x1"][bass.ds((i * 2 + a) * P, P), :], x1[:, a, :]).then_inc(x1_stored[a], 16)
                    act.wait_ge(h2_stored[a], i * 16 + 16)
                    for k in range(KD):
                        last = nc.scalar.activation(h2[:, a, k, :], ps_t[:, a, k, :], ACT.Identity, bias=R["shift"][:, 1, k:k + 1], scale=R["scale"][:, 1, k:k + 1])
                    last.then_inc(h2_made, 1)
                    act.wait_ge(h2_made, i * 2 + a + 1)
                    act.dma_start(W["h2t"].rearrange("(k p) t -> p k t", p=P)[:, :, bass.ds((i * 2 + a) * P, P)], h2[:, a, :, :]).then_inc(h2_stored[a], 16)
                    act.wait_ge(x1_stored[a], i * 16 + 16)
                    act.sem_inc(x1_free, 1)

            def pair(i, begun, more):
                for a in range(2):
                    if more:
                        act.wait_ge(mixed, i * 2 + a + 1)
                        high(i + 1, a)
                act.wait_ge(var_made, i + 1)
                nc.scalar.activation(root[:, :], var[:, :], ACT.Sqrt).then_inc(root_made, 1)
                if begun:
                    late(i - 1)

            high(0, 0)
            high(0, 1)
            pair(0, False, True)
            with act.Fori(1, PAIRS - 1) as i:
                pair(i, True, True)
            pair(PAIRS - 1, True, False)
            late(PAIRS - 1)
            for a in range(2):
                act.wait_ge(h2_stored[a], 16 + 16 * PAIRS)

        @block.vector
        def _(dve):
            dve.sem_inc(gated, 2)
            dve.sem_inc(summed, 2)
            dve.sem_inc(yl_made, 2)
            dve.wait_ge(rows_loaded, 48)
            for m in range(PIECES):
                dve.wait_ge(wh_made, m + 1)
                nc.vector.tensor_tensor(wl[:, 2 * m:2 * m + 2, :], wraw[:, m % 2, :, :], wh[:, 2 * m:2 * m + 2, :].bitcast(F32), ALU.subtract).then_inc(wl_made, 1)

            def low(i, a):
                dve.wait_ge(yh_made, i * 2 + a + 1)
                nc.vector.tensor_tensor(yl[:, a, :, :], yraw[:, a, :, :], yh[:, a, :, :].bitcast(F32), ALU.subtract).then_inc(yl_made, 1)

            def pair(i, more):
                own = Chain(dve, dve_own, i * OWN, spare)
                for a in range(2):
                    dve.wait_ge(mixed, i * 2 + a + 1)
                    nc.vector.tensor_tensor(z[:, a, :], ps[:, a, :], rows[:, 0, :], ALU.mult).then_inc(gated, 1)
                    if more:
                        low(i + 1, a)
                    dve.wait_ge(gated, i * 2 + a + 3)
                    dve.wait_ge(xn_loaded[a], i * 16 + 16)
                    own.step(nc.vector.scalar_tensor_tensor(out=z[:, a, :], in0=xn[:, a, :], scalar=ALPHA, in1=z[:, a, :], op0=ALU.mult, op1=ALU.add))
                    dve.sem_inc(summed, 1)
                    layer_norm_moments(nc, own, z[:, a, :], stats, moments[:, a, :])
                nc.vector.tensor_scalar(var[:, :], moments[:, :, 1], LN_EPS, None, ALU.add).then_inc(var_made, 1)
                dve.wait_ge(root_made, i + 1)
                refine_rsqrt(nc, own, rstd[:, :], var[:, :], root[:, :], tmp[:, :])
                for a in range(2):
                    own.step(nc.vector.tensor_scalar(xhat[:, :], z[:, a, :], moments[:, a, 0:1], rstd[:, a:a + 1], ALU.subtract, ALU.mult))
                    dve.wait_ge(xg_free, i * 2 + a + 1)
                    own.step(nc.vector.tensor_tensor(xg[:, a, :], xhat[:, :], rows[:, 1, :], ALU.mult))
                    dve.sem_inc(xg_made, 1)
                assert own.n == OWN

            low(0, 0)
            low(0, 1)
            with dve.Fori(0, PAIRS - 1) as i:
                pair(i, True)
            pair(PAIRS - 1, False)

        @block.gpsimd
        def _(pool):
            pool.sem_inc(xg_free, 2)
            pool.wait_ge(rows_loaded, 48)
            with pool.Fori(0, PAIRS) as i:
                for a in range(2):
                    pool.wait_ge(xg_made, i * 2 + a + 1)
                    pool.wait_ge(x1_free, i * 2 + a + 1)
                    nc.gpsimd.tensor_tensor(x1[:, a, :], xg[:, a, :], rows[:, 2, :], ALU.add).then_inc(x1_made, 1)
                    pool.wait_ge(x1_made, i * 2 + a + 1)
                    pool.sem_inc(xg_free, 1)

        @block.tensor
        def _(pe):
            def late(i):
                for a in range(2):
                    pe.wait_ge(x1_made, i * 2 + a + 1)
                    for k in range(KD):
                        mm = pe.transpose(ps_t[:, a, k, :], x1[:, a, k * P:(k + 1) * P], R["ident"][:, :])
                    mm.then_inc(x1_turned, 1)

            def pair(i, begun, first):
                for a in range(2):
                    pe.wait_ge(yl_made, i * 2 + a + 3)
                    pe.wait_ge(gated, i * 2 + a + 1)
                    for half in range(2):
                        cols = slice(half * 512, half * 512 + 512)
                        for k in range(KD):
                            if first and a == 0 and half == 0 and k % 2 == 0:
                                pe.wait_ge(wl_made, k // 2 + 1)
                            mm = products(pe, ps[:, a, cols], yh[:, a, k, :], yl[:, a, k, :], wh[:, k, cols], wl[:, k, cols], k == 0, k == KD - 1)
                    mm.then_inc(mixed, 1)
                if begun:
                    late(i - 1)
            pair(0, False, True)
            with pe.Fori(1, PAIRS) as i:
                pair(i, True, False)
            late(PAIRS - 1)


def phase_mlp(nc, T, W, R):
    ROUNDS = D_FF // 512
    with Scope(nc, "f") as s:
        hraw = s.sb("hraw", [P, 2, TG])
        hh = s.sb("hh", [P, KD, TG], F32R)
        hl = s.sb("hl", [P, KD, TG], F32R)
        up_raw = s.sb("up_raw", [P, 2, KD, 256])
        down_raw = s.sb("down_raw", [P, 2, 2, D])
        uph = s.sb("uph", [P, 2, KD, 256], F32R)
        upl = s.sb("upl", [P, 2, KD, 256], F32R)
        downh = s.sb("downh", [P, 2, 2, D], F32R)
        downl = s.sb("downl", [P, 2, 2, D], F32R)
        relu = s.sb("relu", [P, 2, TG])
        act2 = s.sb("act2", [P, 2, TG])
        ah = s.sb("ah", [P, 4, TG], F32R)
        al = s.sb("al", [P, 4, TG], F32R)
        total = s.sb("total", [P, 4, D])
        ps_u = s.psum("ps_u", [P, 4, TG])
        ps_d = s.psum("ps_d", [P, 2, D])
        h_loaded = [s.sem(f"h_loaded{i}") for i in range(2)]
        up_loaded = [s.sem(f"up_loaded{i}") for i in range(2)]
        down_loaded = [s.sem(f"down_loaded{i}") for i in range(2)]
        hh_made = s.sem("hh_made")
        hl_made = s.sem("hl_made")
        uph_made, downh_made = s.sem("uph_made"), s.sem("downh_made")
        upl_made, downl_made = s.sem("upl_made"), s.sem("downl_made")
        up_done = s.sem("up_done")
        relu_made, act2_made, ah_made = s.sem("relu_made"), s.sem("act2_made"), s.sem("ah_made")
        al_made = s.sem("al_made")
        down_done = s.sem("down_done")
        added = s.sem("added")
        cleared = s.sem("cleared")
        total_stored = s.sem("total_stored")
        spare = s.sem("spare")
        block = s.block()

        def n_of(g, j):
            return g * ROUNDS + j

        @block.sync
        def _(sp):
            sp.sem_inc(total_stored, 16)
            with sp.Fori(0, NG) as g:
                for k in range(KD):
                    sp.wait_ge(hl_made, g * KD + k + 1)
                    sp.dma_start(hraw[:, k % 2, :], W["h2t"][k * P:(k + 1) * P, bass.ds(g * TG, TG)]).then_inc(h_loaded[k % 2], 16)
                with sp.Fori(0, ROUNDS) as j:
                    for a in range(2):
                        at = j * 512 + a * 256
                        sp.wait_ge(upl_made, g * (2 * ROUNDS) + j * 2 + a + 1)
                        sp.dma_start(up_raw[:, a, :, :], T["w_up"][0].rearrange("(k p) n -> p k n", p=P)[:, :, bass.ds(at, 256)]).then_inc(up_loaded[a], 16)
                        sp.wait_ge(downl_made, g * (2 * ROUNDS) + j * 2 + a + 1)
                        sp.dma_start(down_raw[:, a, :, :], T["w_down"][0, bass.ds(at, 256), :].rearrange("(k p) n -> p k n", p=P)).then_inc(down_loaded[a], 16)

        @block.scalar
        def _(act):
            act.sem_inc(hl_made, 2)
            with act.Fori(0, NG) as g:
                for k in range(KD):
                    act.wait_ge(h_loaded[k % 2], g * (16 * KD // 2) + 16 * (k // 2 + 1))
                    if k == 0:
                        act.wait_ge(up_done, g * (4 * ROUNDS) + 4)
                    nc.scalar.activation(hh[:, k, :], hraw[:, k % 2, :], ACT.Copy).then_inc(hh_made, 1)
                with act.Fori(0, ROUNDS) as j:
                    n = g * ROUNDS + j
                    for a in range(2):
                        act.wait_ge(up_loaded[a], n * 16 + 16)
                        act.wait_ge(down_done, n * 4 + 4)
                        nc.scalar.activation(uph[:, a, :, :], up_raw[:, a, :, :], ACT.Copy).then_inc(uph_made, 1)
                        act.wait_ge(down_loaded[a], n * 16 + 16)
                        nc.scalar.activation(downh[:, a, :, :], down_raw[:, a, :, :], ACT.Copy).then_inc(downh_made, 1)
                    for f in range(4):
                        b = f % 2
                        act.wait_ge(up_done, n * 4 + f + 5)
                        act.wait_ge(al_made, n * 4 + f + 1)
                        nc.scalar.activation(relu[:, b, :], ps_u[:, f, :], ACT.Relu).then_inc(relu_made, 1)
                        act.wait_ge(relu_made, n * 4 + f + 1)
                        nc.scalar.activation(act2[:, b, :], relu[:, b, :], ACT.Square).then_inc(act2_made, 1)
                        act.wait_ge(act2_made, n * 4 + f + 1)
                        nc.scalar.activation(ah[:, f, :], act2[:, b, :], ACT.Copy).then_inc(ah_made, 1)
                act.wait_ge(added, g * (4 * ROUNDS) + 4 * ROUNDS + 2)
                act.dma_start(W["ff"][bass.ds(g * TG, TG), :].rearrange("(t p) n -> p t n", p=P), total[:, :, :]).then_inc(total_stored, 16)
            act.wait_ge(total_stored, 16 + 16 * NG)

        @block.gpsimd
        def _(pool):
            with pool.Fori(0, NG) as g:
                pool.wait_ge(total_stored, g * 16 + 16)
                pool.sem_inc(cleared, 1)
                nc.gpsimd.memset(total[:, :, :], 0.0).then_inc(cleared, 1)

        @block.vector
        def _(dve):
            dve.sem_inc(upl_made, 2)
            dve.sem_inc(downl_made, 2)
            dve.sem_inc(al_made, 2)
            dve.sem_inc(added, 2)
            with dve.Fori(0, NG) as g:
                for k in range(KD):
                    dve.wait_ge(hh_made, g * KD + k + 1)
                    nc.vector.tensor_tensor(hl[:, k, :], hraw[:, k % 2, :], hh[:, k, :].bitcast(F32), ALU.subtract).then_inc(hl_made, 1)
                with dve.Fori(0, ROUNDS) as j:
                    n = g * ROUNDS + j
                    for a in range(2):
                        dve.wait_ge(uph_made, n * 2 + a + 1)
                        nc.vector.tensor_tensor(upl[:, a, :, :], up_raw[:, a, :, :], uph[:, a, :, :].bitcast(F32), ALU.subtract).then_inc(upl_made, 1)
                        dve.wait_ge(downh_made, n * 2 + a + 1)
                        nc.vector.tensor_tensor(downl[:, a, :, :], down_raw[:, a, :, :], downh[:, a, :, :].bitcast(F32), ALU.subtract).then_inc(downl_made, 1)
                    for f in range(4):
                        dve.wait_ge(ah_made, n * 4 + f + 1)
                        nc.vector.tensor_tensor(al[:, f, :], act2[:, f % 2, :], ah[:, f, :].bitcast(F32), ALU.subtract).then_inc(al_made, 1)
                    dve.wait_ge(cleared, g * 2 + 2)
                    for t in range(4):
                        dve.wait_ge(down_done, n * 4 + t + 5)
                        dve.wait_ge(added, n * 4 + 2)
                        nc.vector.tensor_tensor(total[:, t, :], ps_d[:, t % 2, :], total[:, t, :], ALU.add).then_inc(added, 1)

        @block.tensor
        def _(pe):
            pe.sem_inc(up_done, 4)
            pe.sem_inc(down_done, 4)
            with pe.Fori(0, NG) as g:
                pe.wait_ge(hl_made, g * KD + KD + 2)
                pe.sem_inc(spare, 1)
                with pe.Fori(0, ROUNDS) as j:
                    n = g * ROUNDS + j
                    for f in range(4):
                        a, cols = f // 2, slice((f % 2) * P, (f % 2) * P + P)
                        if f % 2 == 0:
                            pe.wait_ge(upl_made, n * 2 + a + 3)
                        for k in range(KD):
                            mm = products(pe, ps_u[:, f, :], uph[:, a, k, cols], upl[:, a, k, cols], hh[:, k, :], hl[:, k, :], k == 0, k == KD - 1)
                        mm.then_inc(up_done, 1)
                    for t in range(4):
                        tokens = slice(t * P, (t + 1) * P)
                        pe.wait_ge(added, n * 4 + t + 1)
                        for half in range(2):
                            cols = slice(half * 512, half * 512 + 512)
                            for f in range(4):
                                if t == 0 and half == 0:
                                    pe.wait_ge(al_made, n * 4 + f + 3)
                                    if f % 2 == 0:
                                        pe.wait_ge(downl_made, n * 2 + f // 2 + 3)
                                mm = products(pe, ps_d[:, t % 2, cols], ah[:, f, tokens], al[:, f, tokens], downh[:, f // 2, f % 2, cols], downl[:, f // 2, f % 2, cols], f == 0, f == 3)
                        mm.then_inc(down_done, 1)


def phase_last_norm(nc, T, W, R):
    GROUPS = TILES // 4
    with Scope(nc, "n") as s:
        rows = s.sb("rows", [P, 3, D])
        ff = s.sb("ff", [P, 4, D])
        x1 = s.sb("x1", [P, 4, D])
        z = s.sb("z", [P, 4, D])
        xhat = s.sb("xhat", [P, D])
        xg = s.sb("xg", [P, 2, D])
        y = s.sb("y", [P, 2, D])
        stats = s.sb("stats", [P, 2, 6])
        moments = s.sb("moments", [P, 4, 2])
        var, root, rstd, tmp = (s.sb(n, [P, 4]) for n in ("var", "root", "rstd", "tmp"))
        rows_loaded = s.sem("rows_loaded")
        loaded = [s.sem(f"loaded{i}") for i in range(4)]
        summed = s.sem("summed")
        var_made, root_made, xg_made, y_made = s.sem("var_made"), s.sem("root_made"), s.sem("xg_made"), s.sem("y_made")
        xg_free = s.sem("xg_free")
        y_stored = [s.sem(f"y_stored{i}") for i in range(2)]
        dve_own, spare = s.sem("dve_own"), s.sem("spare")
        block = s.block()
        OWN = 4 * 4 + 4 + 4 * 2

        @block.sync
        def _(sp):
            load_rows(sp, rows_loaded, W, T, rows, 1, "ln2_g", "ln2_b")
            with sp.Fori(0, GROUPS) as i:
                for b in range(4):
                    tokens = bass.ds((i * 4 + b) * P, P)
                    sp.wait_ge(summed, i * 4 + b + 1)
                    sp.dma_start(ff[:, b, :], W["ff"][tokens, :]).then_inc(loaded[b], 16)
                    sp.dma_start(x1[:, b, :], W["x1"][tokens, :]).then_inc(loaded[b], 16)

        @block.scalar
        def _(act):
            for a in range(2):
                act.sem_inc(y_stored[a], 16)
            with act.Fori(0, GROUPS) as i:
                act.wait_ge(var_made, i + 1)
                nc.scalar.activation(root[:, :], var[:, :], ACT.Sqrt).then_inc(root_made, 1)
                for b in range(4):
                    act.wait_ge(y_made, i * 4 + b + 1)
                    act.dma_start(W["out"][bass.ds((i * 4 + b) * P, P), :], y[:, b % 2, :]).then_inc(y_stored[b % 2], 16)
            for a in range(2):
                act.wait_ge(y_stored[a], 16 + 16 * (TILES // 2))

        @block.vector
        def _(dve):
            dve.sem_inc(summed, 4)
            dve.wait_ge(rows_loaded, 48)
            with dve.Fori(0, GROUPS) as i:
                own = Chain(dve, dve_own, i * OWN, spare)
                for b in range(4):
                    dve.wait_ge(loaded[b], i * 32 + 32)
                    own.step(nc.vector.tensor_tensor(z[:, b, :], ff[:, b, :], rows[:, 0, :], ALU.mult))
                    own.step(nc.vector.scalar_tensor_tensor(out=z[:, b, :], in0=x1[:, b, :], scalar=ALPHA, in1=z[:, b, :], op0=ALU.mult, op1=ALU.add))
                    dve.sem_inc(summed, 1)
                    layer_norm_moments(nc, own, z[:, b, :], stats, moments[:, b, :])
                nc.vector.tensor_scalar(var[:, :], moments[:, :, 1], LN_EPS, None, ALU.add).then_inc(var_made, 1)
                dve.wait_ge(root_made, i + 1)
                refine_rsqrt(nc, own, rstd[:, :], var[:, :], root[:, :], tmp[:, :])
                for b in range(4):
                    own.step(nc.vector.tensor_scalar(xhat[:, :], z[:, b, :], moments[:, b, 0:1], rstd[:, b:b + 1], ALU.subtract, ALU.mult))
                    dve.wait_ge(xg_free, i * 4 + b + 1)
                    own.step(nc.vector.tensor_tensor(xg[:, b % 2, :], xhat[:, :], rows[:, 1, :], ALU.mult))
                    dve.sem_inc(xg_made, 1)
                assert own.n == OWN

        @block.gpsimd
        def _(pool):
            pool.sem_inc(xg_free, 2)
            pool.wait_ge(rows_loaded, 48)
            with pool.Fori(0, GROUPS) as i:
                for b in range(4):
                    pool.wait_ge(xg_made, i * 4 + b + 1)
                    pool.wait_ge(y_stored[b % 2], i * 32 + (b // 2) * 16 + 16)
                    nc.gpsimd.tensor_tensor(y[:, b % 2, :], xg[:, b % 2, :], rows[:, 2, :], ALU.add).then_inc(y_made, 1)
                    pool.wait_ge(y_made, i * 4 + b + 1)
                    pool.sem_inc(xg_free, 1)



PHASES = [phase_modulation, phase_projection, phase_stick_breaking, phase_latent_attention, phase_output_projection, phase_mlp, phase_last_norm]
DEBUG = None

def build(nc, T, out):
    W = {
        "xn": nc.dram_tensor("xn_scratch", (SEQ, D), F32).ap(),
        "xt": nc.dram_tensor("xt_scratch", (D, SEQ), F32).ap(),
        "qk": nc.dram_tensor("qk_scratch", (2 * SBW, SEQ), F32).ap(),
        "v": nc.dram_tensor("v_scratch", (SEQ, SBW), F32).ap(),
        "lq": nc.dram_tensor("lq_scratch", (HEADS, QK, SEQ), F32).ap(),
        "lk": nc.dram_tensor("lk_scratch", (HEADS * HD, SEQ), F32).ap(),
        "lkr": nc.dram_tensor("lkr_scratch", (ROPE, SEQ), F32).ap(),
        "lv": nc.dram_tensor("lv_scratch", (SEQ, HEADS * HD), F32).ap(),
        "yt": nc.dram_tensor("yt_scratch", (D, SEQ), F32).ap(),
        "x1": nc.dram_tensor("x1_scratch", (SEQ, D), F32).ap(),
        "h2t": nc.dram_tensor("h2t_scratch", (D, SEQ), F32).ap(),
        "gate": nc.dram_tensor("gate_scratch", (2, D), F32).ap(),
        "seed": nc.dram_tensor("seed_scratch", (1, 16), F32).ap(),
        "ff": nc.dram_tensor("ff_scratch", (SEQ, D), F32).ap(),
    }
    W["out"] = out[0]
    with Scope(nc, "r") as s:
        R = {
            "ident": s.sb("ident", [P, P]), "ident_r": s.sb("ident_r", [P, P], F32R), "zeros": s.sb("zeros", [P, P]),
            "strict": s.sb("strict", [P, P], F32R), "halves": s.sb("halves", [P, 64], F32R),
            "shift": s.sb("shift", [P, 2, KD]), "scale": s.sb("scale", [P, 2, KD]),
        }
        for phase in PHASES:
            phase(nc, T, W, R)
        if DEBUG:
            with Scope(nc, "dbg") as d:
                done = d.sem("done")
                block = d.block()

                @block.sync
                def _(sp):
                    w = W[DEBUG] if len(W[DEBUG].shape) == 2 else W[DEBUG].rearrange("a b c -> (a b) c")
                    w = w.rearrange("a b -> (a b)").rearrange("(a b) -> a b", b=D)
                    n = min(SEQ, w.shape[0])
                    sp.dma_start(out[0, 0:n, :], w[0:n, :]).then_inc(done, 16)
                    sp.wait_ge(done, 16)


_INS = ['x', 'c', 'ln_in_g', 'ln_in_b', 'w_ada', 'b_ada', 'w_in', 'q_norm_g', 'kv_norm_g', 'w_uq', 'w_ukv', 'w_o',
        'ln1_g', 'ln1_b', 'w_up', 'w_down', 'ln2_g', 'ln2_b']
_OUTS = [((1, 2048, 1024), 'float32')]


def _rope_table():
    import numpy as _np
    inv_freq = (1.0 / (_np.float32(10000.0) ** (_np.arange(0, 32, 2, dtype=_np.float32) / _np.float32(32)))).astype(_np.float32)
    ang = (_np.arange(2048, dtype=_np.float32)[:, None] * inv_freq[None, :]).astype(_np.float32)
    cos, sin = _np.cos(ang).T.astype(_np.float32), _np.sin(ang).T.astype(_np.float32)
    half = _np.concatenate([cos, cos, -sin, sin], axis=0)
    return _np.ascontiguousarray(_np.concatenate([half, half], axis=0))


def kernel(**inputs):
    import numpy as _np
    import concourse.bacc as _bacc
    from concourse import mybir as _mybir
    from concourse.bass_utils import run_bass_kernel_spmd as _run

    nc = _bacc.Bacc("TRN2", target_bir_lowering=False, num_devices=1)
    arrays, T = {}, {}
    for name in _INS:
        a = _np.ascontiguousarray(inputs[name])
        arrays[f"in_{name}_dram"] = a
        T[name] = nc.dram_tensor(f"in_{name}_dram", a.shape, _mybir.dt.from_np(a.dtype), kind="ExternalInput").ap()
    arrays["rope_dram"] = _rope_table()
    T["rope"] = nc.dram_tensor("rope_dram", (128, 2048), F32, kind="ExternalInput").ap()
    (shape, dtype), = _OUTS
    out = nc.dram_tensor("out_0_dram", shape, _mybir.dt.from_np(_np.dtype(dtype)), kind="ExternalOutput").ap()
    build(nc, T, out)
    r = _run(nc, [arrays], core_ids=[0])
    return r.results[0]["out_0_dram"]
```

```python
from contextlib import ExitStack

import concourse.bass as bass
from concourse import mybir

ALU = mybir.AluOpType
ACT = mybir.ActivationFunctionType
F32 = mybir.dt.float32
F32R = mybir.dt.float32r

P = 128
SEQ = 2048
D = 1024
KD = D // P
TG = 512
NG = SEQ // TG
TILES = SEQ // P
N_MOD = 6
HEADS = 8
HD = 64
ROPE = 32
QK = HD + ROPE
SBW = HEADS * HD
Q_RANK = 384
KV_RANK = 256
KQ = Q_RANK // P
KV = KV_RANK // P
D_FF = 4 * D
LN_EPS = 1e-5
RMS_EPS = 1e-6
ALPHA = 2.0 ** 0.25
SB_SCALE = HD ** -0.5
MLA_SCALE = QK ** -0.5
MASKED = -1e30


class Chain:

    def __init__(self, eng, sem, base=0, spare=None):
        self.eng, self.sem, self.base, self.spare, self.n = eng, sem, base, spare, 0

    def stand(self):
        self.eng.sem_inc(self.spare, 1)

    def step(self, instruction):
        self.n += 1
        instruction.then_inc(self.sem, 1)
        self.eng.wait_ge(self.sem, self.base + self.n)


class Scope:

    def __init__(self, nc, phase):
        self.nc, self.phase, self.ctx, self.sems = nc, phase, ExitStack(), []

    def __enter__(self):
        return self

    def __exit__(self, *exc):
        self.ctx.__exit__(*exc)
        if self.sems and exc[0] is None:
            self.nc.clear_and_free_semaphores(self.sems)
            self.nc.all_engine_barrier()

    def sb(self, name, shape, dtype=F32):
        return self.ctx.enter_context(self.nc.sbuf_tensor(f"{self.phase}_{name}", shape, dtype))

    def psum(self, name, shape):
        return self.ctx.enter_context(self.nc.psum_tensor(f"{self.phase}_{name}", shape, F32))

    def sem(self, name):
        self.sems.append(self.nc.alloc_semaphore(f"{self.phase}_{name}"))
        return self.sems[-1]

    def block(self):
        return self.ctx.enter_context(self.nc.Block())


def products(pe, out, wh, wl, xh, xl, first, last):
    pe.matmul(out, wh, xh, start=first, stop=False)
    pe.matmul(out, wl, xh, start=False, stop=False)
    return pe.matmul(out, wh, xl, start=False, stop=last)


def layer_norm_moments(nc, own, x, stats, moments):
    nc.vector.bn_stats(stats[:, 0, :], x[:, 0:512])
    own.step(nc.vector.bn_stats(stats[:, 1, :], x[:, 512:1024]))
    own.stand()
    own.step(nc.vector.bn_aggr(moments, stats[:, :, :].rearrange("p a b -> p (a b)")))


def refine_rsqrt(nc, own, rstd, var, root, tmp):
    own.step(nc.vector.reciprocal(rstd, root))
    own.step(nc.vector.tensor_tensor(tmp, rstd, rstd, ALU.mult))
    own.step(nc.vector.scalar_tensor_tensor(out=tmp, in0=tmp, scalar=-0.5, in1=var, op0=ALU.mult, op1=ALU.mult))
    own.step(nc.vector.scalar_tensor_tensor(out=rstd, in0=tmp, scalar=1.5, in1=rstd, op0=ALU.add, op1=ALU.mult))


def phase_modulation(nc, T, W, R):
    with Scope(nc, "m") as s:
        c_col = s.sb("c_col", [P, KD])
        c_sig = s.sb("c_sig", [P, KD])
        c_act = s.sb("c_act", [P, KD])
        c_rep = s.sb("c_rep", [P, KD, P])
        gate = s.sb("gate", [1, 2, D])
        ones = s.sb("ones", [P, P])
        w = s.sb("w", [P, 3, KD, 512])
        mod = s.sb("mod", [P, N_MOD * D])
        b_row = s.sb("b_row", [P, 3, 512])
        gb = s.sb("gb", [P, 2, D])
        x = s.sb("x", [P, 4, D])
        xhat = s.sb("xhat", [P, D])
        xg = s.sb("xg", [P, 2, D])
        xn = s.sb("xn", [P, 2, D])
        xt = s.sb("xt", [P, 2, KD, P])
        stats = s.sb("stats", [P, 2, 6])
        moments = s.sb("moments", [P, 4, 2])
        var, root, rstd, tmp = (s.sb(n, [P, 4]) for n in ("var", "root", "rstd", "tmp"))
        ps_mod = s.psum("ps_mod", [P, 3, 512])
        ps_t = s.psum("ps_t", [P, 4, 4, P])
        ps_col = s.psum("ps_col", [P, 512])

        c_loaded, gb_loaded = s.sem("c_loaded"), s.sem("gb_loaded")
        w_loaded = [s.sem(f"w_loaded{i}") for i in range(3)]
        x_loaded = [s.sem(f"x_loaded{i}") for i in range(4)]
        xn_stored = [s.sem(f"xn_stored{i}") for i in range(2)]
        xt_stored = [s.sem(f"xt_stored{i}") for i in range(2)]
        ones_set, ident_set, c_sigmoid, c_ready = s.sem("ones_set"), s.sem("ident_set"), s.sem("c_sigmoid"), s.sem("c_ready")
        mod_summed, cols_made = s.sem("mod_summed"), s.sem("cols_made")
        mod_added = s.sem("mod_added")
        x_free = s.sem("x_free")
        xg_made, xg_free = s.sem("xg_made"), s.sem("xg_free")
        xn_made = s.sem("xn_made")
        x_turned = s.sem("x_turned")
        x_evacuated = s.sem("x_evacuated")
        gate_made, gate_stored = s.sem("gate_made"), s.sem("gate_stored")
        var_made, root_made = s.sem("var_made"), s.sem("root_made")
        dve_own, pool_own, spare = s.sem("dve_own"), s.sem("pool_own"), s.sem("spare")
        block = s.block()
        OWN = 4 * 2 + 4 + 4 * 2

        @block.sync
        def _(sp):
            sp.dma_start(c_col[:, :], T["c"].rearrange("a (p k) -> (a p) k", k=KD)).then_inc(c_loaded, 16)
            for n, name in enumerate(("ln_in_g", "ln_in_b")):
                sp.dma_start(gb[:, n, :], T[name].rearrange("(a d) -> a d", a=1).to_broadcast([P, D])).then_inc(gb_loaded, 16)
            with sp.Fori(0, 4) as i:
                for b in range(4):
                    sp.wait_ge(x_free, i * 4 + b + 1)
                    sp.dma_start(x[:, b, :], T["x"][0, bass.ds((i * 4 + b) * P, P), :]).then_inc(x_loaded[b], 16)
                for a in range(3):
                    sp.wait_ge(mod_added, i * 3 + a + 1)
                    sp.dma_start(w[:, a, :, :], T["w_ada"][0].rearrange("(p k) n -> p k n", k=KD)[:, :, bass.ds((i * 3 + a) * 512, 512)]).then_inc(w_loaded[a], 16)
                    sp.dma_start(b_row[:, a, :], T["b_ada"][:, bass.ds((i * 3 + a) * 512, 512)].to_broadcast([P, 512])).then_inc(w_loaded[a], 16)

        @block.scalar
        def _(act):
            act.sem_inc(x_evacuated, 2)
            for a in range(2):
                act.sem_inc(xt_stored[a], 16)
                act.sem_inc(xn_stored[a], 16)
            act.wait_ge(c_loaded, 16)
            nc.scalar.activation(c_sig[:, :], c_col[:, :], ACT.Sigmoid).then_inc(c_sigmoid, 1)
            with act.Fori(0, 4) as i:
                act.wait_ge(var_made, i + 1)
                nc.scalar.activation(root[:, :], var[:, :], ACT.Sqrt).then_inc(root_made, 1)
                for b in range(4):
                    a = b % 2
                    act.wait_ge(x_turned, i * 4 + b + 3)
                    act.dma_start(W["xn"][bass.ds((i * 4 + b) * P, P), :], xn[:, a, :]).then_inc(xn_stored[a], 16)
                    act.wait_ge(xt_stored[a], i * 32 + (b // 2) * 16 + 16)
                    nc.scalar.activation(xt[:, a, 0:4, :], ps_t[:, 2 * a, :, :], ACT.Copy)
                    nc.scalar.activation(xt[:, a, 4:8, :], ps_t[:, 2 * a + 1, :, :], ACT.Copy).then_inc(x_evacuated, 1)
                    act.wait_ge(x_evacuated, i * 4 + b + 3)
                    act.dma_start(W["xt"].rearrange("(k p) t -> p k t", p=P)[:, :, bass.ds((i * 4 + b) * P, P)], xt[:, a, :, :]).then_inc(xt_stored[a], 16)
            act.wait_ge(gate_made, 1)
            act.dma_start(W["gate"].rearrange("(a g) d -> a g d", a=1), gate[:, :, :]).then_inc(gate_stored, 16)
            act.wait_ge(gate_stored, 16)
            for a in range(2):
                act.wait_ge(xt_stored[a], 16 + 16 * (TILES // 2))
                act.wait_ge(xn_stored[a], 16 + 16 * (TILES // 2))

        @block.gpsimd
        def _(pool):
            pool.sem_inc(xg_free, 2)
            nc.gpsimd.memset(ones[:, :], 1.0).then_inc(ones_set, 1)
            pool.wait_ge(ones_set, 1)
            nc.gpsimd.affine_select(out=R["ident"][:, :], in_=ones[:, :], compare_op=ALU.is_equal, fill=0.0,
                                    base=0, pattern=[[-1, P]], channel_multiplier=1).then_inc(ident_set, 1)
            nc.gpsimd.affine_select(out=R["ident_r"][:, :], in_=ones[:, :], compare_op=ALU.is_equal, fill=0.0,
                                    base=0, pattern=[[-1, P]], channel_multiplier=1)
            nc.gpsimd.memset(R["zeros"][:, :], 0.0).then_inc(pool_own, 1)
            pool.wait_ge(pool_own, 1)
            nc.gpsimd.affine_select(out=R["strict"][:, :], in_=R["zeros"][:, :], compare_op=ALU.is_gt, fill=MASKED,
                                    base=0, pattern=[[-1, P]], channel_multiplier=1)
            nc.gpsimd.affine_select(out=R["halves"][:, :], in_=R["zeros"][:, 0:64], compare_op=ALU.is_ge, fill=MASKED,
                                    base=-64, pattern=[[0, 64]], channel_multiplier=1)
            pool.wait_ge(gb_loaded, 32)
            with pool.Fori(0, TILES // 2) as i:
                for a in range(2):
                    pool.wait_ge(xg_made, i * 2 + a + 1)
                    pool.wait_ge(xn_stored[a], i * 16 + 16)
                    pool.wait_ge(x_turned, i * 2 + a + 1)
                    nc.gpsimd.tensor_tensor(xn[:, a, :], xg[:, a, :], gb[:, 1, :], ALU.add).then_inc(xn_made, 1)
                    pool.wait_ge(xn_made, i * 2 + a + 1)
                    pool.sem_inc(xg_free, 1)

        @block.vector
        def _(dve):
            dve.sem_inc(mod_added, 3)
            dve.sem_inc(x_free, 4)
            dve.wait_ge(c_sigmoid, 1)
            own = Chain(dve, dve_own)
            own.step(nc.vector.tensor_tensor(c_act[:, :], c_col[:, :], c_sig[:, :], ALU.mult))
            dve.wait_ge(ones_set, 1)
            for k in range(KD):
                last = nc.vector.tensor_scalar(c_rep[:, k, :], ones[:, :], c_act[:, k:k + 1], None, ALU.mult)
            last.then_inc(c_ready, 1)
            dve.wait_ge(gb_loaded, 32)
            with dve.Fori(0, 4) as i:
                for a in range(3):
                    dve.wait_ge(mod_summed, i * 3 + a + 1)
                    dve.wait_ge(w_loaded[a], i * 32 + 32)
                    nc.vector.tensor_tensor(mod[:, bass.ds((i * 3 + a) * 512, 512)], ps_mod[:, a, :], b_row[:, a, :], ALU.add).then_inc(mod_added, 1)
                own = Chain(dve, dve_own, i * OWN + 1, spare)
                for b in range(4):
                    dve.wait_ge(x_loaded[b], i * 16 + 16)
                    layer_norm_moments(nc, own, x[:, b, :], stats, moments[:, b, :])
                nc.vector.tensor_scalar(var[:, :], moments[:, :, 1], LN_EPS, None, ALU.add).then_inc(var_made, 1)
                dve.wait_ge(root_made, i + 1)
                refine_rsqrt(nc, own, rstd[:, :], var[:, :], root[:, :], tmp[:, :])
                for b in range(4):
                    own.step(nc.vector.tensor_scalar(xhat[:, :], x[:, b, :], moments[:, b, 0:1], rstd[:, b:b + 1], ALU.subtract, ALU.mult))
                    dve.sem_inc(x_free, 1)
                    dve.wait_ge(xg_free, i * 4 + b + 1)
                    own.step(nc.vector.tensor_tensor(xg[:, b % 2, :], xhat[:, :], gb[:, 0, :], ALU.mult))
                    dve.sem_inc(xg_made, 1)
                assert own.n == OWN
            dve.wait_ge(mod_added, 15)
            nc.vector.tensor_scalar(gate[:, 0, :], mod[0:1, 2 * D:3 * D], 1.0, None, ALU.add)
            nc.vector.tensor_scalar(gate[:, 1, :], mod[0:1, 5 * D:6 * D], 1.0, None, ALU.add).then_inc(gate_made, 1)
            dve.wait_ge(cols_made, 1)
            cols = ps_col[:, 0:4 * KD].rearrange("p (v k) -> p v k", v=4)
            nc.vector.tensor_copy(R["shift"][:, :, :], cols[:, 0::2, :])
            nc.vector.tensor_scalar(R["scale"][:, :, :], cols[:, 1::2, :], 1.0, None, ALU.add)

        @block.tensor
        def _(pe):
            pe.sem_inc(x_turned, 2)
            pe.wait_ge(c_ready, 1)
            pe.wait_ge(ident_set, 1)
            with pe.Fori(0, 4) as i:
                for a in range(3):
                    pe.wait_ge(w_loaded[a], i * 32 + 32)
                    pe.wait_ge(mod_added, i * 3 + a + 1)
                    for k in range(KD):
                        mm = pe.matmul(ps_mod[:, a, :], c_rep[:, k, :], w[:, a, k, :], start=(k == 0), stop=(k == KD - 1))
                    mm.then_inc(mod_summed, 1)
                for b in range(4):
                    a = b % 2
                    pe.wait_ge(xn_made, i * 4 + b + 1)
                    pe.wait_ge(x_evacuated, i * 4 + b + 1)
                    for k in range(KD):
                        mm = pe.transpose(ps_t[:, 2 * a + k // 4, k % 4, :], xn[:, a, k * P:(k + 1) * P], R["ident"][:, :])
                    mm.then_inc(x_turned, 1)
            pe.wait_ge(mod_added, 15)
            for v, m in enumerate((0, 1, 3, 4)):
                for k in range(KD):
                    mm = pe.matmul(ps_col[:, v * KD + k:v * KD + k + 1], mod[0:1, m * D + k * P:m * D + (k + 1) * P], ones[0:1, 0:1], start=True, stop=True)
            mm.then_inc(cols_made, 1)


def phase_projection(nc, T, W, R):
    JOBS, BANKS = 36, 6
    UNIT_JOB = [0, 1, 2, 3, 4, 5, 6, 7, 8, 10, 11, 13, 14, 15]
    STREAM = len(UNIT_JOB)
    SUM_Q, SUM_KV, V_JOB, Q_JOB, K_JOB, LV_JOB = 9, 12, 16, 20, 28, 32
    STAGED_JOBS = [6, 7, 8, 10, 11, 13, 14, 15] + list(range(16, 36))
    STAGED = len(STAGED_JOBS)
    STAGES = 4
    FIXED = 9
    LAT = KQ + KV
    LATENT_AT, ROTARY_AT = 3 * SBW, 3 * SBW + Q_RANK + KV_RANK
    with Scope(nc, "p") as s:
        xraw = s.sb("xraw", [P, 2, TG])
        hmod = s.sb("hmod", [P, 2, TG])
        hh = s.sb("hh", [P, KD, TG], F32R)
        hl = s.sb("hl", [P, KD, TG], F32R)
        wraw = s.sb("wraw", [P, 2, 1024])
        wh = s.sb("wh", [P, 2, 1024], F32R)
        wl = s.sb("wl", [P, 2, 1024], F32R)
        wvh = s.sb("wvh", [P, KD, SBW], F32R)
        wvl = s.sb("wvl", [P, KD, SBW], F32R)
        wqh = s.sb("wqh", [P, KQ, HEADS, P], F32R)
        wql = s.sb("wql", [P, KQ, HEADS, P], F32R)
        wkh = s.sb("wkh", [P, KV, 1024], F32R)
        wkl = s.sb("wkl", [P, KV, 1024], F32R)
        gains = s.sb("gains", [P, LAT])
        ones = s.sb("ones", [P, P])
        lat = s.sb("lat", [P, LAT, TG])
        lsq = s.sb("lsq", [P, KQ, TG])
        var, root, rstd, tmp = (s.sb(n, [P, TG]) for n in ("var", "root", "rstd", "tmp"))
        lath = s.sb("lath", [P, LAT, TG], F32R)
        latl = s.sb("latl", [P, LAT, TG], F32R)
        table = s.sb("table", [P, SEQ])
        turn = s.sb("turn", [P, 2, TG])
        kr = s.sb("kr", [ROPE, TG])
        stage = s.sb("stage", [P, STAGES, TG])
        seed = s.sb("seed", [1, 16])
        ps = s.psum("ps", [P, BANKS, TG])

        xraw_loaded = [s.sem(f"xraw_loaded{i}") for i in range(2)]
        h_made = s.sem("h_made")
        w_loaded = [s.sem(f"w_loaded{i}") for i in range(2)]
        gains_loaded, table_loaded = s.sem("gains_loaded"), s.sem("table_loaded")
        hh_made, hl_made, wh_made, wl_made, ones_set = (s.sem(n) for n in ("hh_made", "hl_made", "wh_made", "wl_made", "ones_set"))
        job_done = s.sem("job_done")
        bank_free = [s.sem(f"bank_free{i}") for i in range(BANKS)]
        lsq_made, var_made, root_made, latn_made = (s.sem(n) for n in ("lsq_made", "var_made", "root_made", "latn_made"))
        lath_made, latl_made = s.sem("lath_made"), s.sem("latl_made")
        act_staged, dve_staged, kr_made = s.sem("act_staged"), s.sem("dve_staged"), s.sem("kr_made")
        stage_free = s.sem("stage_free")
        kr_free = s.sem("kr_free")
        stored = [s.sem(f"stored{i}") for i in range(2)]
        kr_stored, seed_set = s.sem("kr_stored"), s.sem("seed_set")
        dve_own, spare = s.sem("dve_own"), s.sem("spare")
        block = s.block()
        OWN = 2 * (HEADS + 1) + 4 * 2

        fixed_dmas = [1] * 4 + [3] * 3 + [1] * 2
        unit_dmas = [3 if u == 5 else 1 for u in range(STREAM)]

        def arrived(eng, g, m):
            slot = m % 2
            before = sum(n for j, n in enumerate(fixed_dmas) if j % 2 == slot and j <= m)
            if m >= FIXED:
                per_group = sum(n for u, n in enumerate(unit_dmas) if (FIXED + u) % 2 == slot)
                before += sum(n for u, n in enumerate(unit_dmas) if (FIXED + u) % 2 == slot and u <= m - FIXED)
                eng.wait_ge(w_loaded[slot], g * (16 * per_group) + 16 * before)
            else:
                eng.wait_ge(w_loaded[slot], 16 * before)

        def target(m, high):
            w, v, q, k = (wh, wvh, wqh, wkh) if high else (wl, wvl, wql, wkl)
            if m < 4:
                return v[:, 2 * m:2 * m + 2, :].rearrange("p k n -> p (k n)")
            if m < 7:
                return q[:, m - 4, :, :].rearrange("p h n -> p (h n)")
            if m < FIXED:
                return k[:, m - 7, :]
            return w[:, m % 2, 0:KD * 2 * ROPE] if m - FIXED == 5 else w[:, m % 2, :]

        def raw(m):
            return wraw[:, m % 2, 0:KD * 2 * ROPE] if m - FIXED == 5 else wraw[:, m % 2, :]

        def load_fixed(sp, m):
            done = w_loaded[m % 2]
            if m < 4:
                sp.dma_start(raw(m).rearrange("p (k n) -> p k n", k=2),
                             T["w_in"][0, m * 256:(m + 1) * 256, 2 * SBW:3 * SBW].rearrange("(k p) n -> p k n", p=P)).then_inc(done, 16)
            elif m < 7:
                rows = T["w_uq"][0, (m - 4) * P:(m - 3) * P, :].rearrange("p (h n) -> p h n", n=QK)
                to = raw(m).rearrange("p (h n) -> p h n", n=P)
                sp.dma_start(to[:, :, 0:QK], rows).then_inc(done, 16)
                sp.dma_start(to[:, :, QK:QK + 16], rows[:, :, HD + 16:QK]).then_inc(done, 16)
                sp.dma_start(to[:, :, QK + 16:P], rows[:, :, HD:HD + 16]).then_inc(done, 16)
            else:
                sp.dma_start(raw(m), T["w_ukv"][0, (m - 7) * P:(m - 6) * P, :]).then_inc(done, 16)

        def load_unit(sp, u):
            source = T["w_in"][0].rearrange("(k p) n -> p k n", p=P)
            to = raw(FIXED + u).rearrange("p (k n) -> p k n", k=KD)
            done = w_loaded[(FIXED + u) % 2]
            if u == 5:
                c = ROTARY_AT
                sp.dma_start(to[:, :, 0:ROPE], source[:, :, c:c + ROPE]).then_inc(done, 16)
                sp.dma_start(to[:, :, ROPE:ROPE + 16], source[:, :, c + 16:c + ROPE]).then_inc(done, 16)
                sp.dma_start(to[:, :, ROPE + 16:2 * ROPE], source[:, :, c:c + 16]).then_inc(done, 16)
            else:
                c = LATENT_AT + u * P if u < 5 else (u - 6) * P
                sp.dma_start(to, source[:, :, c:c + P]).then_inc(done, 16)

        @block.sync
        def _(sp):
            sp.dma_start(table[:, :], T["rope"]).then_inc(table_loaded, 16)
            with nc.allow_non_contiguous_dma(reason="five columns of gains"):
                sp.dma_start(gains[:, 0:KQ], T["q_norm_g"][0].rearrange("(k p) -> p k", p=P)).then_inc(gains_loaded, 16)
                sp.dma_start(gains[:, KQ:LAT], T["kv_norm_g"][0].rearrange("(k p) -> p k", p=P)).then_inc(gains_loaded, 16)
            for m in range(FIXED):
                if m >= 2:
                    sp.wait_ge(wl_made, m - 1)
                load_fixed(sp, m)
            with sp.Fori(0, NG) as g:
                for u in range(2):
                    sp.wait_ge(wl_made, g * STREAM + FIXED + u - 1)
                    load_unit(sp, u)
                for k in range(KD):
                    sp.wait_ge(h_made, g * KD + k + 1)
                    sp.dma_start(xraw[:, k % 2, :], W["xt"][k * P:(k + 1) * P, bass.ds(g * TG, TG)]).then_inc(xraw_loaded[k % 2], 16)
                for u in range(2, STREAM):
                    sp.wait_ge(wl_made, g * STREAM + FIXED + u - 1)
                    load_unit(sp, u)

        @block.scalar
        def _(act):
            for b in range(BANKS):
                act.sem_inc(bank_free[b], 1)
            act.sem_inc(h_made, 2)
            act.sem_inc(stage_free, 3)

            def high_half(g, m):
                arrived(act, g, m)
                nc.scalar.activation(target(m, True), raw(m), ACT.Copy).then_inc(wh_made, 1)

            def high_slice(g, k, first):
                act.wait_ge(xraw_loaded[k % 2], g * (16 * KD // 2) + 16 * (k // 2 + 1))
                if k >= 2 or not first:
                    act.wait_ge(hl_made, g * KD + k - 1)
                nc.scalar.activation(hmod[:, k % 2, :], xraw[:, k % 2, :], ACT.Identity,
                                     bias=R["shift"][:, 0, k:k + 1], scale=R["scale"][:, 0, k:k + 1]).then_inc(h_made, 1)
                act.wait_ge(h_made, g * KD + k + 3)
                nc.scalar.activation(hh[:, k, :], hmod[:, k % 2, :], ACT.Copy).then_inc(hh_made, 1)

            def to_stage(g, job, rows=P):
                n = STAGED_JOBS.index(job)
                act.wait_ge(job_done, g * JOBS + job + 1)
                act.wait_ge(stage_free, g * STAGED + n + 1)
                out = nc.scalar.activation(stage[0:rows, n % STAGES, :], ps[0:rows, job % BANKS, :], ACT.Copy)
                if rows == P:
                    out.then_inc(bank_free[job % BANKS], 1)
                    act.wait_ge(bank_free[job % BANKS], g * (JOBS // BANKS) + job // BANKS + 2)
                    act.sem_inc(act_staged, 1)
                else:
                    out.then_inc(act_staged, 1)

            def group(g, more):
                for u in range(STREAM):
                    job = UNIT_JOB[u]
                    if u < LAT:
                        act.wait_ge(job_done, g * JOBS + job + 1)
                        if u < KQ:
                            nc.scalar.activation(lsq[:, u, :], ps[:, job % BANKS, :], ACT.Square).then_inc(lsq_made, 1)
                        nc.scalar.activation(lat[:, u, :], ps[:, job % BANKS, :], ACT.Copy).then_inc(bank_free[job % BANKS], 1)
                    elif u == 5:
                        act.wait_ge(job_done, g * JOBS + job + 1)
                    else:
                        to_stage(g, job)
                    if u + 2 < STREAM:
                        high_half(g, FIXED + u + 2)
                    if job == SUM_Q + 1:
                        for j in range(KV):
                            nc.scalar.activation(lsq[:, j, :], lat[:, KQ + j, :], ACT.Square).then_inc(lsq_made, 1)
                        act.wait_ge(var_made, g * 2 + 1)
                        nc.scalar.activation(root[:, :], var[:, :], ACT.Sqrt).then_inc(root_made, 1)
                    if job == SUM_Q + 2:
                        for j in range(KQ):
                            act.wait_ge(latn_made, g * LAT + j + 1)
                            nc.scalar.activation(lath[:, j, :], lat[:, j, :], ACT.Copy).then_inc(lath_made, 1)
                    if job == SUM_KV + 1:
                        act.wait_ge(var_made, g * 2 + 2)
                        nc.scalar.activation(root[:, :], var[:, :], ACT.Sqrt).then_inc(root_made, 1)
                for j in range(KQ, LAT):
                    act.wait_ge(latn_made, g * LAT + j + 1)
                    nc.scalar.activation(lath[:, j, :], lat[:, j, :], ACT.Copy).then_inc(lath_made, 1)
                for t in range(4):
                    to_stage(g, V_JOB + t)
                if more:
                    high_half(g + 1, FIXED)
                    high_half(g + 1, FIXED + 1)
                for h in range(HEADS):
                    to_stage(g, Q_JOB + h, HD)
                    if more:
                        high_slice(g + 1, h, False)
                for job in range(K_JOB, JOBS):
                    to_stage(g, job)

            for m in range(FIXED + 2):
                if m >= FIXED:
                    high_half(0, m)
                else:
                    high_half(0, m)
            for k in range(KD):
                high_slice(0, k, True)
            with act.Fori(0, NG - 1) as g:
                group(g, True)
            group(NG - 1, False)

        @block.vector
        def _(dve):
            def low_half(g, m):
                done = m + 1 if m < FIXED else g * STREAM + m + 1
                dve.wait_ge(wh_made, done)
                nc.vector.tensor_tensor(target(m, False), raw(m), target(m, True).bitcast(F32), ALU.subtract).then_inc(wl_made, 1)

            def low_slice(g, k):
                dve.wait_ge(hh_made, g * KD + k + 1)
                nc.vector.tensor_tensor(hl[:, k, :], hmod[:, k % 2, :], hh[:, k, :].bitcast(F32), ALU.subtract).then_inc(hl_made, 1)

            def rotate(own, g, job, lo, out):
                position = bass.ds(g * TG, TG)
                own.step(nc.vector.tensor_tensor(turn[lo:lo + ROPE, 0, :], ps[lo:lo + ROPE, job % BANKS, :], table[lo:lo + ROPE, position], ALU.mult))
                own.step(nc.vector.tensor_tensor(turn[lo:lo + ROPE, 1, :], ps[lo + ROPE:lo + 2 * ROPE, job % BANKS, :], table[lo + ROPE:lo + 2 * ROPE, position], ALU.mult))
                return nc.vector.tensor_tensor(out, turn[lo:lo + ROPE, 0, :], turn[lo:lo + ROPE, 1, :], ALU.add)

            def normalise(own, g, which, first, last, width):
                job = (SUM_Q, SUM_KV)[which]
                dve.wait_ge(job_done, g * JOBS + job + 1)
                nc.vector.tensor_scalar(var[:, :], ps[:, job % BANKS, :], 1.0 / width, RMS_EPS, ALU.mult, ALU.add).then_inc(var_made, 1)
                dve.wait_ge(var_made, g * 2 + which + 1)
                dve.sem_inc(bank_free[job % BANKS], 1)
                dve.wait_ge(root_made, g * 2 + which + 1)
                refine_rsqrt(nc, own, rstd[:, :], var[:, :], root[:, :], tmp[:, :])
                for j in range(first, last):
                    nc.vector.scalar_tensor_tensor(out=lat[:, j, :], in0=lat[:, j, :], scalar=gains[:, j:j + 1], in1=rstd[:, :],
                                                   op0=ALU.mult, op1=ALU.mult).then_inc(latn_made, 1)

            def low_latents(g, first, last):
                for j in range(first, last):
                    dve.wait_ge(lath_made, g * LAT + j + 1)
                    nc.vector.tensor_tensor(latl[:, j, :], lat[:, j, :], lath[:, j, :].bitcast(F32), ALU.subtract).then_inc(latl_made, 1)

            def group(g, more):
                own = Chain(dve, dve_own, g * OWN)
                for u in range(STREAM):
                    job = UNIT_JOB[u]
                    if u == 5:
                        dve.wait_ge(job_done, g * JOBS + job + 1)
                        dve.wait_ge(kr_free, g + 1)
                        rotate(own, g, job, 0, kr[:, :]).then_inc(kr_made, 1)
                        dve.sem_inc(bank_free[job % BANKS], 1)
                    if u + 2 < STREAM:
                        low_half(g, FIXED + u + 2)
                    if job == SUM_Q + 1:
                        normalise(own, g, 0, 0, KQ, Q_RANK)
                    if job == SUM_Q + 2:
                        low_latents(g, 0, KQ)
                    if job == SUM_KV + 1:
                        dve.wait_ge(latn_made, g * LAT + KQ)
                        normalise(own, g, 1, KQ, LAT, KV_RANK)
                low_latents(g, KQ, LAT)
                if more:
                    low_half(g + 1, FIXED)
                    low_half(g + 1, FIXED + 1)
                for h in range(HEADS):
                    n = STAGED_JOBS.index(Q_JOB + h)
                    dve.wait_ge(job_done, g * JOBS + Q_JOB + h + 1)
                    if h:
                        dve.wait_ge(dve_staged, g * HEADS + h)
                    dve.wait_ge(act_staged, g * STAGED + n + 1)
                    rotate(own, g, Q_JOB + h, HD, stage[HD:QK, n % STAGES, :]).then_inc(dve_staged, 1)
                    dve.sem_inc(bank_free[(Q_JOB + h) % BANKS], 1)
                    if more:
                        low_slice(g + 1, h)
                dve.wait_ge(dve_staged, g * HEADS + HEADS)
                assert own.n == OWN

            dve.wait_ge(table_loaded, 16)
            dve.wait_ge(gains_loaded, 32)
            for m in range(FIXED + 2):
                low_half(0, m)
            for k in range(KD):
                low_slice(0, k)
            with dve.Fori(0, NG - 1) as g:
                group(g, True)
            group(NG - 1, False)

        @block.gpsimd
        def _(pool):
            nc.gpsimd.memset(ones[:, :], 1.0).then_inc(ones_set, 1)
            nc.gpsimd.memset(seed[:, :], 0.0).then_inc(seed_set, 1)
            pool.sem_inc(kr_free, 1)
            pool.wait_ge(seed_set, 1)
            pool.dma_start(W["seed"], seed[:, :]).then_inc(stored[1], 16)

            def target_of(g, job):
                tokens = bass.ds(g * TG, TG)
                if job < V_JOB:
                    r = UNIT_JOB.index(job) - 6
                    return W["qk"][r * P:(r + 1) * P, tokens], P
                if job < Q_JOB:
                    return W["v"][bass.ds(g * TG + (job - V_JOB) * P, P), :], P
                if job < K_JOB:
                    return W["lq"][job - Q_JOB][:, tokens], QK
                if job < LV_JOB:
                    return W["lk"][(job - K_JOB) * P:(job - K_JOB + 1) * P, tokens], P
                return W["lv"][bass.ds(g * TG + (job - LV_JOB) * P, P), :], P

            with pool.Fori(0, NG) as g:
                for n, job in enumerate(STAGED_JOBS):
                    if Q_JOB <= job < K_JOB:
                        pool.wait_ge(dve_staged, g * HEADS + job - Q_JOB + 1)
                    pool.wait_ge(act_staged, g * STAGED + n + 1)
                    pool.sem_inc(spare, 1)
                    to, rows = target_of(g, job)
                    pool.dma_start(to, stage[0:rows, n % STAGES, :]).then_inc(stored[n % 2], 16)
                    before = (n - 1) % 2
                    uses = g * (STAGED // 2) + ((n - 1) // 2 + 1) + before
                    pool.wait_ge(stored[before], uses * 16)
                    pool.sem_inc(stage_free, 1)
                    if n == 0:
                        pool.wait_ge(kr_made, g + 1)
                        pool.sem_inc(spare, 1)
                        pool.dma_start(W["lkr"][:, bass.ds(g * TG, TG)], kr[:, :]).then_inc(kr_stored, 16)
                        pool.wait_ge(kr_stored, g * 16 + 16)
                        pool.sem_inc(kr_free, 1)
            pool.wait_ge(stored[0], 16 * NG * STAGED // 2)
            pool.wait_ge(stored[1], 16 * (NG * STAGED // 2 + 1))

        @block.tensor
        def _(pe):
            def open_job(g, job):
                pe.wait_ge(bank_free[job % BANKS], g * (JOBS // BANKS) + job // BANKS + 1)
                return ps[:, job % BANKS, :]

            def squares_summed(g, job, first, n):
                pe.wait_ge(lsq_made, g * LAT + first + n)
                bank = open_job(g, job)
                for j in range(n):
                    mm = pe.matmul(bank, ones[:, :], lsq[:, j, :], start=(j == 0), stop=(j == n - 1))
                mm.then_inc(job_done, 1)

            pe.wait_ge(ones_set, 1)
            with pe.Fori(0, NG) as g:
                for u in range(STREAM):
                    job = UNIT_JOB[u]
                    if job == SUM_Q + 1:
                        squares_summed(g, SUM_Q, 0, KQ)
                    if job == SUM_KV + 1:
                        squares_summed(g, SUM_KV, KQ, KV)
                    m = FIXED + u
                    width = 2 * ROPE if u == 5 else P
                    high = target(m, True).rearrange("p (k n) -> p k n", k=KD)
                    low = target(m, False).rearrange("p (k n) -> p k n", k=KD)
                    pe.wait_ge(wl_made, g * STREAM + m + 1)
                    out = open_job(g, job)[0:width, :]
                    for k in range(KD):
                        if u == 0:
                            pe.wait_ge(hl_made, g * KD + k + 1)
                        mm = products(pe, out, high[:, k, :], low[:, k, :], hh[:, k, :], hl[:, k, :], k == 0, k == KD - 1)
                    mm.then_inc(job_done, 1)
                for t in range(4):
                    out = open_job(g, V_JOB + t)
                    rows = slice(t * P, (t + 1) * P)
                    for k in range(KD):
                        mm = products(pe, out, hh[:, k, rows], hl[:, k, rows], wvh[:, k, :], wvl[:, k, :], k == 0, k == KD - 1)
                    mm.then_inc(job_done, 1)
                pe.wait_ge(latl_made, g * LAT + LAT)
                for h in range(HEADS):
                    out = open_job(g, Q_JOB + h)
                    for k in range(KQ):
                        mm = products(pe, out, wqh[:, k, h, :], wql[:, k, h, :], lath[:, k, :], latl[:, k, :], k == 0, k == KQ - 1)
                    mm.then_inc(job_done, 1)
                for t in range(4):
                    out = open_job(g, K_JOB + t)
                    cols = slice(t * P, (t + 1) * P)
                    for k in range(KV):
                        mm = products(pe, out, wkh[:, k, cols], wkl[:, k, cols], lath[:, KQ + k, :], latl[:, KQ + k, :], k == 0, k == KV - 1)
                    mm.then_inc(job_done, 1)
                for t in range(4):
                    out = open_job(g, LV_JOB + t)
                    rows = slice(t * P, (t + 1) * P)
                    for k in range(KV):
                        mm = products(pe, out, lath[:, KQ + k, rows], latl[:, KQ + k, rows], wkh[:, k, 512:1024], wkl[:, k, 512:1024], k == 0, k == KV - 1)
                    mm.then_inc(job_done, 1)


S_BANKS, T_BANKS = 5, 2


def chunks_of(qb):
    length = (qb + 1) * P
    return [slice(c, min(c + 512, length)) for c in range(0, length, 512)]


def chunk_base(qb):
    return sum(len(chunks_of(q)) for q in range(qb))


CHUNKS = chunk_base(TILES)
UNITS = sum(g + 1 for g in range(NG))
UNIT_RING = 5
LATE = 6
VALUES_AT = (15, 18, 30, 46)
PIECE_AT = {VALUES_AT[g] + i: (g, i) for g in range(NG) for i in range(2 * g + 2)}
Y_AT = {VALUES_AT[g] + 2 * g + 2: g for g in range(NG)}
SLOTS = max(Y_AT) + 1
SPLIT_AT = {26: 0, 29: 1, 32: 2}


def late_chunk(lag):
    return lambda k: k - lag if 0 <= k - lag < CHUNKS else None


def due(what, H, a, k, begun):
    if what(k) is not None:
        return H, a, what(k)
    if begun and k < CHUNKS and what(k + CHUNKS) is not None:
        return H - 1, 1 - a, what(k + CHUNKS)
    return None


def over_heads(eng, slot):
    def pair(i, begun, more):
        for a in range(2):
            for k in range(CHUNKS):
                slot(i * 2 + a, a, k, begun or a > 0, more or a == 0)
    pair(0, False, True)
    with eng.Fori(1, HEADS // 2 - 1) as i:
        pair(i, True, True)
    pair(HEADS // 2 - 1, True, False)
    for k in range(CHUNKS, SLOTS):
        slot(HEADS - 1, 1, k, True, False)


class AttentionSide:

    def __init__(self, nc, s, W, row0, order, ring):
        self.nc, self.W, self.row0, self.order, self.ring = nc, W, row0, order, ring
        self.table = [(qb, j, cols) for qb in range(TILES) for j, cols in enumerate(order(qb))]
        self.v_raw = s.sb("v_raw", [P, TILES, HD])
        self.v_halves = [s.sb(f"v_halves{a}", [P, TILES, 2 * HD], F32R) for a in range(2)]
        self.turned_high = s.sb("turned_high", [P, UNIT_RING * 4, TG], F32R)
        self.turned_low = s.sb("turned_low", [P, UNIT_RING * 4, TG], F32R)
        self.y_low = s.sb("y_low", [HD, TG])
        self.y = s.sb("y", [HD, TG])
        self.ps_s = s.psum("ps_s", [P, S_BANKS, 512])
        self.ps_t = s.psum("ps_t", [P, T_BANKS, 4, P])
        self.ps_y = s.psum("ps_y", [P, TG])
        sem = s.sem
        self.raw_loaded, self.split_high, self.split_low = sem("raw_loaded"), sem("split_high"), sem("split_low")
        self.scores_done = sem("scores_done")
        self.scores_used = sem("scores_used")
        self.turn_done = sem("turn_done")
        self.high_done = sem("high_done")
        self.low_done = sem("low_done")
        self.unit_used = sem("unit_used")
        self.y_low_made = sem("y_low_made")
        self.y_summed = sem("y_summed")
        self.y_stored = sem("y_stored")

    def scores(self, n):
        cols = self.table[n][2]
        return self.ps_s[:, n % S_BANKS, 0:cols.stop - cols.start]

    def place(self, n):
        cols = self.table[n][2]
        return slice(512 - (cols.stop - cols.start), 512)

    def unit(self, group, j):
        return sum(g + 1 for g in range(group)) + j

    def turned(self, n, halves):
        qb, j, cols = self.table[n]
        tile = self.unit(qb // 4, j) % UNIT_RING * 4
        return halves[:, tile:tile + (cols.stop - cols.start) // P, qb % 4 * P:qb % 4 * P + P]

    def late_tensor(self, pe, weights, weights_made, credit, H, a, k, begun):
        late = due(late_chunk(LATE), H, a, k, begun)
        if late:
            h, _, n = late
            pe.wait_ge(weights_made, h * CHUNKS + n + 1 + credit)
            pe.wait_ge(self.low_done, h * CHUNKS + n + 1)
            at = self.place(n)
            for b in range((at.stop - at.start) // P):
                mm = pe.transpose(self.ps_t[:, n % T_BANKS, b, :], weights[:, n % self.ring, at.start + b * P:at.start + b * P + P], self.ident[:, :])
            mm.then_inc(self.turn_done, 1)
        piece = due(PIECE_AT.get, H, a, k, begun)
        if piece:
            h, ha, (group, i) = piece
            if i == 0:
                pe.wait_ge(self.low_done, h * CHUNKS + chunk_base(4 * group + 4) + T_BANKS)
                pe.wait_ge(self.y_summed, h * NG + group + 1)
            j, cols = i // 2, self.order(4 * group + 3)[i // 2]
            for b in (i % 2 * 2, i % 2 * 2 + 1):
                kb = cols.start // P + b
                lo = max(0, kb - 4 * group) * P
                tile = self.unit(group, j) % UNIT_RING * 4 + b
                first, last = i == 0 and b == 0, j == group and b == 3
                pe.matmul(self.ps_y[:, lo:TG], self.v_halves[ha][:, kb, :], self.turned_high[:, tile, lo:TG], start=first, stop=False)
                mm = pe.matmul(self.ps_y[:, lo:TG], self.v_halves[ha][:, kb, :], self.turned_low[:, tile, lo:TG], start=False, stop=last)
            if i % 2 == 1:
                mm.then_inc(self.unit_used, 1)

    def late_scalar(self, act, H, a, k, begun):
        nc = self.nc
        late = due(late_chunk(LATE), H, a, k, begun)
        if late:
            h, _, n = late
            qb, j, _ = self.table[n]
            act.wait_ge(self.turn_done, h * CHUNKS + n + 1)
            if qb % 4 == 0:
                act.wait_ge(self.unit_used, h * UNITS + self.unit(qb // 4, j) + 1)
            blocks = self.turned(n, self.turned_high)
            nc.scalar.activation(blocks, self.ps_t[:, n % T_BANKS, 0:blocks.shape[1], :], ACT.Copy).then_inc(self.high_done, 1)
        sum_ = due(Y_AT.get, H, a, k, begun)
        if sum_:
            h, _, group = sum_
            act.wait_ge(self.unit_used, h * UNITS + self.unit(group + 1, 0) + UNIT_RING)
            act.wait_ge(self.y_summed, h * NG + group + 1)
            nc.scalar.activation(self.y_low[:, :], self.ps_y[HD:P, :], ACT.Copy).then_inc(self.y_low_made, 1)

    def late_vector(self, dve, y, y_free, H, a, k, begun):
        nc = self.nc
        late = due(late_chunk(LATE), H, a, k, begun)
        if late:
            h, _, n = late
            dve.wait_ge(self.high_done, h * CHUNKS + n + 1)
            high = self.turned(n, self.turned_high)
            nc.vector.tensor_tensor(self.turned(n, self.turned_low), self.ps_t[:, n % T_BANKS, 0:high.shape[1], :], high.bitcast(F32), ALU.subtract).then_inc(self.low_done, 1)
        sum_ = due(Y_AT.get, H, a, k, begun)
        if sum_:
            h, _, group = sum_
            dve.wait_ge(self.y_low_made, h * NG + group + 1)
            y_free(h, group)
            nc.vector.tensor_tensor(y[:, :], self.ps_y[0:HD, :], self.y_low[:, :], ALU.add).then_inc(self.y_summed, 1)

    def load_values(self, sp, H, name):
        source = self.W[name].rearrange("(b p) n -> p b n", p=P)
        sp.dma_start(self.v_raw[:, :, :], source[:, :, bass.ds(H * HD, HD)]).then_inc(self.raw_loaded, 16)

    def store(self, sp, y_made, credit, H, group):
        sp.wait_ge(y_made, H * NG + group + 1 + credit)
        sp.dma_start(self.W["yt"][bass.ds(self.row0 + H * HD, HD), group * TG:(group + 1) * TG], self.y[:, :]).then_inc(self.y_stored, 16)


def phase_stick_breaking(nc, T, W, R):
    RING = 8
    SHORT = 5
    with Scope(nc, "s") as s:
        side = AttentionSide(nc, s, W, 0, lambda qb: chunks_of(qb)[::-1], RING)
        side.ident = R["ident"]
        q_raw = s.sb("q_raw", [P, SEQ])
        k_raw = s.sb("k_raw", [P, SEQ])
        q_stack = [s.sb(f"q_stack{a}", [P, SEQ], F32R) for a in range(2)]
        k_high = [s.sb(f"k_high{a}", [P, SEQ], F32R) for a in range(2)]
        k_low = [s.sb(f"k_low{a}", [P, SEQ], F32R) for a in range(2)]
        sig = s.sb("sig", [P, SHORT, 512])
        weights = s.sb("weights", [P, RING, 513])
        later = s.sb("later", [P, SHORT, 513])
        sig_made = side.scores_used
        weights_made = s.sem("weights_made")
        keep_made, scanned, ones_set = s.sem("keep_made"), s.sem("scanned"), s.sem("ones_set")
        block = s.block()

        @block.sync
        def _(sp):
            sp.sem_inc(side.y_stored, 16)

            def load(H):
                for half in range(2):
                    sp.dma_start(q_raw[half * HD:(half + 1) * HD, :], W["qk"][bass.ds(H * HD, HD), :]).then_inc(side.raw_loaded, 16)
                    sp.dma_start(k_raw[half * HD:(half + 1) * HD, :], W["qk"][bass.ds(SBW + H * HD, HD), :]).then_inc(side.raw_loaded, 16)
                side.load_values(sp, H, "v")

            def head(H, begun, more):
                if more:
                    sp.wait_ge(side.split_low, H * 3 + 3)
                    load(H + 1)
                if begun:
                    side.store(sp, side.y_summed, 1, H - 1, NG - 1)
                for group in range(NG - 1):
                    side.store(sp, side.y_summed, 1, H, group)

            load(0)
            head(0, False, True)
            with sp.Fori(1, HEADS - 1) as H:
                head(H, True, True)
            head(HEADS - 1, True, False)
            side.store(sp, side.y_summed, 1, HEADS - 1, NG - 1)
            sp.wait_ge(side.y_stored, 16 + 16 * HEADS * NG)

        @block.scalar
        def _(act):
            def split(H, a, part):
                if part == 0:
                    act.wait_ge(side.raw_loaded, H * 80 + 80)
                to, raw = ((q_stack[a][:, :], q_raw[:, :]), (k_high[a][:, :], k_raw[:, :]), (side.v_halves[a][:, :, 0:HD], side.v_raw[:, :, :]))[part]
                nc.scalar.activation(to, raw, ACT.Copy).then_inc(side.split_high, 1)

            def slot(H, a, k, begun, more):
                if k < CHUNKS:
                    act.wait_ge(side.scores_done, H * CHUNKS + k + 1)
                    act.wait_ge(weights_made, H * CHUNKS + k + 1)
                    nc.scalar.activation(sig[:, k % SHORT, side.place(k)], side.scores(k), ACT.Sigmoid, scale=SB_SCALE).then_inc(sig_made, 1)
                side.late_scalar(act, H, a, k, begun)
                if k < CHUNKS:
                    act.wait_ge(sig_made, H * CHUNKS + k + 1 + S_BANKS)
                    nc.scalar.activation(weights[:, k % RING, side.place(k)], sig[:, k % SHORT, side.place(k)], ACT.Copy, scale=-1.0, bias=1.0).then_inc(keep_made, 1)
                if more and k in SPLIT_AT:
                    split(H + 1, 1 - a, SPLIT_AT[k])

            act.sem_inc(side.scores_used, S_BANKS)
            for part in range(3):
                split(0, 0, part)
            over_heads(act, slot)

        @block.vector
        def _(dve):
            def split(H, a, part):
                dve.wait_ge(side.split_high, H * 3 + part + 1)
                low, raw, high = ((q_stack[a][HD:P, :], q_raw[HD:P, :], q_stack[a][HD:P, :]), (k_low[a][:, :], k_raw[:, :], k_high[a][:, :]),
                                  (side.v_halves[a][:, :, HD:P], side.v_raw[:, :, :], side.v_halves[a][:, :, 0:HD]))[part]
                nc.vector.tensor_tensor(low, raw, high.bitcast(F32), ALU.subtract).then_inc(side.split_low, 1)

            def y_free(h, group):
                dve.wait_ge(side.y_stored, h * (16 * NG) + group * 16 + 16)

            def slot(H, a, k, begun, more):
                if k < CHUNKS:
                    dve.wait_ge(keep_made, H * CHUNKS + k + 1)
                    if side.table[k][1]:
                        dve.wait_ge(scanned, H * CHUNKS + k)
                        start_at = side.place(k - 1).start
                        start = later[:, (k - 1) % SHORT, start_at:start_at + 1]
                    else:
                        start = 1.0
                    first = side.place(k).start
                    back = slice(512, first - 1 if first else None, -1)
                    keeps = weights[:, k % RING, back]
                    nc.vector.tensor_tensor_scan(later[:, k % SHORT, back], keeps, keeps, start, ALU.mult, ALU.bypass).then_inc(scanned, 1)
                side.late_vector(dve, side.y, y_free, H, a, k, begun)
                if more and k in SPLIT_AT:
                    split(H + 1, 1 - a, SPLIT_AT[k])

            nc.vector.memset(weights[:, :, 512:513], 1.0).then_inc(ones_set, 1)
            dve.wait_ge(ones_set, 1)
            dve.sem_inc(side.low_done, T_BANKS)
            dve.sem_inc(side.y_summed, 1)
            for part in range(3):
                split(0, 0, part)
            over_heads(dve, slot)

        @block.gpsimd
        def _(pool):
            def slot(H, a, k, begun, more):
                if k < CHUNKS:
                    pool.wait_ge(scanned, H * CHUNKS + k + 1)
                    at = side.place(k)
                    nc.gpsimd.tensor_tensor(weights[:, k % RING, at], sig[:, k % SHORT, at], later[:, k % SHORT, at.start + 1:513], ALU.mult).then_inc(weights_made, 1)
            pool.sem_inc(weights_made, SHORT)
            over_heads(pool, slot)

        @block.tensor
        def _(pe):
            def slot(H, a, k, begun, more):
                if k == 0:
                    pe.wait_ge(side.split_low, H * 3 + 3)
                if k < CHUNKS:
                    qb, j, cols = side.table[k]
                    queries = q_stack[a][:, qb * P:(qb + 1) * P]
                    pe.wait_ge(side.scores_used, H * CHUNKS + k + 1)
                    out = side.scores(k)
                    pe.matmul(out, queries, k_high[a][:, cols], start=True, stop=False)
                    mm = pe.matmul(out, queries, k_low[a][:, cols], start=False, stop=(j > 0))
                    if j == 0:
                        mm = pe.matmul(out[:, cols.stop - cols.start - P:], R["ident_r"][:, :], R["strict"][:, :], start=False, stop=True)
                    mm.then_inc(side.scores_done, 1)
                side.late_tensor(pe, weights, weights_made, SHORT, H, a, k, begun)

            pe.sem_inc(side.unit_used, UNIT_RING)
            over_heads(pe, slot)


def phase_latent_attention(nc, T, W, R):
    EXP_LATE = 4
    RING = 5
    with Scope(nc, "l") as s:
        side = AttentionSide(nc, s, W, SBW, chunks_of, RING)
        side.ident = R["ident"]
        q_raw = s.sb("q_raw", [QK, SEQ])
        k_raw = s.sb("k_raw", [QK, SEQ])
        q_high, q_low, k_high, k_low = ([s.sb(f"{n}{a}", [QK, SEQ], F32R) for a in range(2)] for n in ("q_high", "q_low", "k_high", "k_low"))
        weights = s.sb("weights", [P, RING, 512])
        chunk_max = s.sb("chunk_max", [P, 4])
        row_max = s.sb("row_max", [P, 1])
        bias = s.sb("bias", [P, TILES])
        sums = s.sb("sums", [P, TILES, 4])
        total = s.sb("total", [P, 1])
        inverse = s.sb("inverse", [P, TILES])
        inverse_rows = s.sb("inverse_rows", [HD, 2, TG])
        y_sum = s.sb("y_sum", [HD, TG])
        exp_made = side.scores_used
        bias_made, total_made, inverse_made, dve_own = s.sem("bias_made"), s.sem("total_made"), s.sem("inverse_made"), s.sem("dve_own")
        inverse_stored = s.sem("inverse_stored")
        inverse_loaded = [s.sem(f"inverse_loaded{i}") for i in range(2)]
        y_made = s.sem("y_made")
        block = s.block()
        OWN = CHUNKS + 2 * TILES

        @block.sync
        def _(sp):
            sp.sem_inc(side.y_stored, 16)

            def load(H):
                lq = W["lq"].rearrange("h r t -> (h r) t")
                sp.dma_start(q_raw[:, :], lq[bass.ds(H * QK, QK), :]).then_inc(side.raw_loaded, 16)
                sp.dma_start(k_raw[0:HD, :], W["lk"][bass.ds(H * HD, HD), :]).then_inc(side.raw_loaded, 16)
                sp.dma_start(k_raw[HD:QK, :], W["lkr"]).then_inc(side.raw_loaded, 16)
                side.load_values(sp, H, "lv")

            def turn_inverses(H, group):
                sp.wait_ge(inverse_made, H * TILES + 4 * group + 4)
                rows = W["inverse"][bass.ds(H, 1), group * TG:(group + 1) * TG]
                sp.dma_start(rows.rearrange("a (b p) -> p (a b)", p=P), inverse[:, 4 * group:4 * group + 4], allow_slow_non_contiguous=True).then_inc(inverse_stored, 16)
                sp.wait_ge(inverse_stored, H * (16 * NG) + group * 16 + 16)
                sp.dma_start(inverse_rows[:, group % 2, :], rows.to_broadcast([HD, TG])).then_inc(inverse_loaded[group % 2], 16)

            def head(H, begun, more):
                if more:
                    sp.wait_ge(side.split_low, H * 3 + 3)
                    load(H + 1)
                if begun:
                    turn_inverses(H - 1, 3)
                turn_inverses(H, 0)
                if begun:
                    side.store(sp, y_made, 1, H - 1, 3)
                turn_inverses(H, 1)
                side.store(sp, y_made, 1, H, 0)
                side.store(sp, y_made, 1, H, 1)
                turn_inverses(H, 2)
                side.store(sp, y_made, 1, H, 2)

            load(0)
            head(0, False, True)
            with sp.Fori(1, HEADS - 1) as H:
                head(H, True, True)
            head(HEADS - 1, True, False)
            turn_inverses(HEADS - 1, 3)
            side.store(sp, y_made, 1, HEADS - 1, 3)
            sp.wait_ge(side.y_stored, 16 + 16 * HEADS * NG)

        @block.scalar
        def _(act):
            def split(H, a, part):
                if part == 0:
                    act.wait_ge(side.raw_loaded, H * 64 + 64)
                to, raw = ((q_high[a][:, :], q_raw[:, :]), (k_high[a][:, :], k_raw[:, :]), (side.v_halves[a][:, :, 0:HD], side.v_raw[:, :, :]))[part]
                nc.scalar.activation(to, raw, ACT.Copy).then_inc(side.split_high, 1)

            def slot(H, a, k, begun, more):
                now = due(late_chunk(EXP_LATE), H, a, k, begun)
                if now:
                    h, _, n = now
                    qb, j, _ = side.table[n]
                    if j == 0:
                        act.wait_ge(bias_made, h * TILES + qb + 1)
                    nc.scalar.activation(weights[:, n % RING, side.place(n)], side.scores(n), ACT.Exp,
                                         bias=bias[:, qb:qb + 1], scale=MLA_SCALE, accum_out=sums[:, qb, j:j + 1]).then_inc(exp_made, 1)
                side.late_scalar(act, H, a, k, begun)
                if more and k in SPLIT_AT:
                    split(H + 1, 1 - a, SPLIT_AT[k])

            act.sem_inc(side.scores_used, S_BANKS)
            for part in range(3):
                split(0, 0, part)
            over_heads(act, slot)

        @block.vector
        def _(dve):
            def own_count(H, qb):
                return H * OWN + chunk_base(qb) + 2 * qb

            def y_free(h, group):
                dve.wait_ge(y_made, h * NG + group + 1)

            row_end = {chunk_base(qb + 1) - 1 + EXP_LATE + 1: qb for qb in range(TILES)}

            def slot(H, a, k, begun, more):
                if k < CHUNKS:
                    qb, j, _ = side.table[k]
                    length = len(chunks_of(qb))
                    if j == 0 and (begun or qb):
                        dve.wait_ge(dve_own, own_count(H, qb))
                    dve.wait_ge(side.scores_done, H * CHUNKS + k + 1)
                    nc.vector.reduce_max(chunk_max[:, j:j + 1], side.scores(k), mybir.AxisListType.X).then_inc(dve_own, 1)
                    if j == length - 1:
                        dve.wait_ge(dve_own, own_count(H, qb) + length)
                        nc.vector.reduce_max(row_max[:, :], chunk_max[:, 0:length], mybir.AxisListType.X).then_inc(dve_own, 1)
                        dve.wait_ge(dve_own, own_count(H, qb) + length + 1)
                        nc.vector.tensor_scalar(bias[:, qb:qb + 1], row_max[:, :], -MLA_SCALE, None, ALU.mult).then_inc(bias_made, 1)
                        dve.wait_ge(bias_made, H * TILES + qb + 1)
                        dve.sem_inc(dve_own, 1)
                side.late_vector(dve, y_sum, y_free, H, a, k, begun)
                row = due(row_end.get, H, a, k, begun)
                if row:
                    h, _, qb = row
                    length = len(chunks_of(qb))
                    dve.wait_ge(exp_made, h * CHUNKS + chunk_base(qb + 1) + S_BANKS)
                    nc.vector.reduce_sum(total[:, :], sums[:, qb, 0:length], mybir.AxisListType.X).then_inc(total_made, 1)
                    dve.wait_ge(total_made, h * TILES + qb + 1)
                    nc.vector.reciprocal(inverse[:, qb:qb + 1], total[:, :]).then_inc(inverse_made, 1)
                    dve.wait_ge(inverse_made, h * TILES + qb + 1)

            dve.sem_inc(side.low_done, T_BANKS)
            dve.sem_inc(side.y_summed, 1)
            over_heads(dve, slot)

        @block.gpsimd
        def _(pool):
            def split(H, a, part):
                pool.wait_ge(side.split_high, H * 3 + part + 1)
                low, raw, high = ((q_low[a][:, :], q_raw[:, :], q_high[a][:, :]), (k_low[a][:, :], k_raw[:, :], k_high[a][:, :]),
                                  (side.v_halves[a][:, :, HD:P], side.v_raw[:, :, :], side.v_halves[a][:, :, 0:HD]))[part]
                nc.gpsimd.tensor_tensor(low, raw, high.bitcast(F32), ALU.subtract).then_inc(side.split_low, 1)

            def slot(H, a, k, begun, more):
                sum_ = due(Y_AT.get, H, a, k, begun)
                if sum_:
                    h, _, group = sum_
                    pool.wait_ge(side.y_summed, h * NG + group + 2)
                    pool.wait_ge(inverse_loaded[group % 2], h * 32 + group // 2 * 16 + 16)
                    pool.wait_ge(side.y_stored, h * (16 * NG) + group * 16 + 16)
                    nc.gpsimd.tensor_tensor(side.y[:, :], y_sum[:, :], inverse_rows[:, group % 2, :], ALU.mult).then_inc(y_made, 1)
                if more and k in SPLIT_AT:
                    split(H + 1, 1 - a, SPLIT_AT[k])

            pool.sem_inc(y_made, 1)
            for part in range(3):
                split(0, 0, part)
            over_heads(pool, slot)

        @block.tensor
        def _(pe):
            def slot(H, a, k, begun, more):
                if k == 0:
                    pe.wait_ge(side.split_low, H * 3 + 3)
                if k < CHUNKS:
                    qb, j, cols = side.table[k]
                    rows = slice(qb * P, (qb + 1) * P)
                    pe.wait_ge(side.scores_used, H * CHUNKS + k + 1)
                    out = side.scores(k)
                    width = cols.stop - cols.start
                    diagonal = cols.stop == (qb + 1) * P
                    mm = products(pe, out, q_high[a][:, rows], q_low[a][:, rows], k_high[a][:, cols], k_low[a][:, cols], True, not diagonal)
                    if diagonal:
                        mm = pe.matmul(out[:, width - 64:width], R["ident_r"][:, :], R["halves"][:, :], start=False, stop=True)
                    mm.then_inc(side.scores_done, 1)
                side.late_tensor(pe, weights, exp_made, S_BANKS, H, a, k, begun)

            pe.sem_inc(side.unit_used, UNIT_RING)
            over_heads(pe, slot)

def load_rows(sp, s_loaded, W, T, gates, gate, gain, bias):
    sp.dma_start(gates[:, 0, :], W["gate"][gate:gate + 1, :].to_broadcast([P, D])).then_inc(s_loaded, 16)
    sp.dma_start(gates[:, 1, :], T[gain].to_broadcast([P, D])).then_inc(s_loaded, 16)
    sp.dma_start(gates[:, 2, :], T[bias].to_broadcast([P, D])).then_inc(s_loaded, 16)


def phase_output_projection(nc, T, W, R):
    PAIRS = TILES // 2
    PIECES = 4
    with Scope(nc, "o") as s:
        wraw = s.sb("wraw", [P, 2, 2, D])
        wh = s.sb("wh", [P, KD, D], F32R)
        wl = s.sb("wl", [P, KD, D], F32R)
        yraw = s.sb("yraw", [P, 2, KD, P])
        yh = s.sb("yh", [P, 2, KD, P], F32R)
        yl = s.sb("yl", [P, 2, KD, P], F32R)
        rows = s.sb("rows", [P, 3, D])
        xn = s.sb("xn", [P, 2, D])
        z = s.sb("z", [P, 2, D])
        xhat = s.sb("xhat", [P, D])
        xg = s.sb("xg", [P, 2, D])
        x1 = s.sb("x1", [P, 2, D])
        h2 = s.sb("h2", [P, 2, KD, P])
        stats = s.sb("stats", [P, 2, 6])
        moments = s.sb("moments", [P, 2, 2])
        var, root, rstd, tmp = (s.sb(n, [P, 2]) for n in ("var", "root", "rstd", "tmp"))
        ps = s.psum("ps", [P, 2, D])
        ps_t = s.psum("ps_t", [P, 2, KD, P])
        rows_loaded = s.sem("rows_loaded")
        w_loaded = [s.sem(f"w_loaded{i}") for i in range(2)]
        y_loaded = [s.sem(f"y_loaded{i}") for i in range(2)]
        xn_loaded = [s.sem(f"xn_loaded{i}") for i in range(2)]
        wh_made, wl_made, yh_made = s.sem("wh_made"), s.sem("wl_made"), s.sem("yh_made")
        yl_made = s.sem("yl_made")
        mixed = s.sem("mixed")
        gated = s.sem("gated")
        summed = s.sem("summed")
        var_made, root_made, xg_made = s.sem("var_made"), s.sem("root_made"), s.sem("xg_made")
        xg_free = s.sem("xg_free")
        x1_made, x1_turned, h2_made = s.sem("x1_made"), s.sem("x1_turned"), s.sem("h2_made")
        x1_free = s.sem("x1_free")
        x1_stored = [s.sem(f"x1_stored{i}") for i in range(2)]
        h2_stored = [s.sem(f"h2_stored{i}") for i in range(2)]
        dve_own, spare = s.sem("dve_own"), s.sem("spare")
        block = s.block()
        OWN = 2 * 1 + 2 * 2 + 4 + 2 * 2

        @block.sync
        def _(sp):
            load_rows(sp, rows_loaded, W, T, rows, 0, "ln1_g", "ln1_b")
            for m in range(PIECES):
                if m >= 2:
                    sp.wait_ge(wl_made, m - 1)
                sp.dma_start(wraw[:, m % 2, :, :], T["w_o"][0, m * 256:(m + 1) * 256, :].rearrange("(k p) n -> p k n", p=P)).then_inc(w_loaded[m % 2], 16)
            with sp.Fori(0, PAIRS) as i:
                for a in range(2):
                    tokens = bass.ds((i * 2 + a) * P, P)
                    sp.wait_ge(yl_made, i * 2 + a + 1)
                    sp.dma_start(yraw[:, a, :, :], W["yt"].rearrange("(k p) t -> p k t", p=P)[:, :, tokens]).then_inc(y_loaded[a], 16)
                    sp.wait_ge(summed, i * 2 + a + 1)
                    sp.dma_start(xn[:, a, :], W["xn"][tokens, :]).then_inc(xn_loaded[a], 16)

        @block.scalar
        def _(act):
            act.sem_inc(x1_free, 2)
            for a in range(2):
                act.sem_inc(h2_stored[a], 16)
            for m in range(PIECES):
                act.wait_ge(w_loaded[m % 2], 16 * (m // 2 + 1))
                nc.scalar.activation(wh[:, 2 * m:2 * m + 2, :], wraw[:, m % 2, :, :], ACT.Copy).then_inc(wh_made, 1)

            def high(i, a):
                act.wait_ge(y_loaded[a], i * 16 + 16)
                nc.scalar.activation(yh[:, a, :, :], yraw[:, a, :, :], ACT.Copy).then_inc(yh_made, 1)

            def late(i):
                for a in range(2):
                    act.wait_ge(x1_turned, i * 2 + a + 1)
                    act.dma_start(W["x1"][bass.ds((i * 2 + a) * P, P), :], x1[:, a, :]).then_inc(x1_stored[a], 16)
                    act.wait_ge(h2_stored[a], i * 16 + 16)
                    for k in range(KD):
                        last = nc.scalar.activation(h2[:, a, k, :], ps_t[:, a, k, :], ACT.Identity, bias=R["shift"][:, 1, k:k + 1], scale=R["scale"][:, 1, k:k + 1])
                    last.then_inc(h2_made, 1)
                    act.wait_ge(h2_made, i * 2 + a + 1)
                    act.dma_start(W["h2t"].rearrange("(k p) t -> p k t", p=P)[:, :, bass.ds((i * 2 + a) * P, P)], h2[:, a, :, :]).then_inc(h2_stored[a], 16)
                    act.wait_ge(x1_stored[a], i * 16 + 16)
                    act.sem_inc(x1_free, 1)

            def pair(i, begun, more):
                for a in range(2):
                    if more:
                        act.wait_ge(mixed, i * 2 + a + 1)
                        high(i + 1, a)
                act.wait_ge(var_made, i + 1)
                nc.scalar.activation(root[:, :], var[:, :], ACT.Sqrt).then_inc(root_made, 1)
                if begun:
                    late(i - 1)

            high(0, 0)
            high(0, 1)
            pair(0, False, True)
            with act.Fori(1, PAIRS - 1) as i:
                pair(i, True, True)
            pair(PAIRS - 1, True, False)
            late(PAIRS - 1)
            for a in range(2):
                act.wait_ge(h2_stored[a], 16 + 16 * PAIRS)

        @block.vector
        def _(dve):
            dve.sem_inc(gated, 2)
            dve.sem_inc(summed, 2)
            dve.sem_inc(yl_made, 2)
            dve.wait_ge(rows_loaded, 48)
            for m in range(PIECES):
                dve.wait_ge(wh_made, m + 1)
                nc.vector.tensor_tensor(wl[:, 2 * m:2 * m + 2, :], wraw[:, m % 2, :, :], wh[:, 2 * m:2 * m + 2, :].bitcast(F32), ALU.subtract).then_inc(wl_made, 1)

            def low(i, a):
                dve.wait_ge(yh_made, i * 2 + a + 1)
                nc.vector.tensor_tensor(yl[:, a, :, :], yraw[:, a, :, :], yh[:, a, :, :].bitcast(F32), ALU.subtract).then_inc(yl_made, 1)

            def pair(i, more):
                own = Chain(dve, dve_own, i * OWN, spare)
                for a in range(2):
                    dve.wait_ge(mixed, i * 2 + a + 1)
                    nc.vector.tensor_tensor(z[:, a, :], ps[:, a, :], rows[:, 0, :], ALU.mult).then_inc(gated, 1)
                    if more:
                        low(i + 1, a)
                    dve.wait_ge(gated, i * 2 + a + 3)
                    dve.wait_ge(xn_loaded[a], i * 16 + 16)
                    own.step(nc.vector.scalar_tensor_tensor(out=z[:, a, :], in0=xn[:, a, :], scalar=ALPHA, in1=z[:, a, :], op0=ALU.mult, op1=ALU.add))
                    dve.sem_inc(summed, 1)
                    layer_norm_moments(nc, own, z[:, a, :], stats, moments[:, a, :])
                nc.vector.tensor_scalar(var[:, :], moments[:, :, 1], LN_EPS, None, ALU.add).then_inc(var_made, 1)
                dve.wait_ge(root_made, i + 1)
                refine_rsqrt(nc, own, rstd[:, :], var[:, :], root[:, :], tmp[:, :])
                for a in range(2):
                    own.step(nc.vector.tensor_scalar(xhat[:, :], z[:, a, :], moments[:, a, 0:1], rstd[:, a:a + 1], ALU.subtract, ALU.mult))
                    dve.wait_ge(xg_free, i * 2 + a + 1)
                    own.step(nc.vector.tensor_tensor(xg[:, a, :], xhat[:, :], rows[:, 1, :], ALU.mult))
                    dve.sem_inc(xg_made, 1)
                assert own.n == OWN

            low(0, 0)
            low(0, 1)
            with dve.Fori(0, PAIRS - 1) as i:
                pair(i, True)
            pair(PAIRS - 1, False)

        @block.gpsimd
        def _(pool):
            pool.sem_inc(xg_free, 2)
            pool.wait_ge(rows_loaded, 48)
            with pool.Fori(0, PAIRS) as i:
                for a in range(2):
                    pool.wait_ge(xg_made, i * 2 + a + 1)
                    pool.wait_ge(x1_free, i * 2 + a + 1)
                    nc.gpsimd.tensor_tensor(x1[:, a, :], xg[:, a, :], rows[:, 2, :], ALU.add).then_inc(x1_made, 1)
                    pool.wait_ge(x1_made, i * 2 + a + 1)
                    pool.sem_inc(xg_free, 1)

        @block.tensor
        def _(pe):
            def late(i):
                for a in range(2):
                    pe.wait_ge(x1_made, i * 2 + a + 1)
                    for k in range(KD):
                        mm = pe.transpose(ps_t[:, a, k, :], x1[:, a, k * P:(k + 1) * P], R["ident"][:, :])
                    mm.then_inc(x1_turned, 1)

            def pair(i, begun, first):
                for a in range(2):
                    pe.wait_ge(yl_made, i * 2 + a + 3)
                    pe.wait_ge(gated, i * 2 + a + 1)
                    for half in range(2):
                        cols = slice(half * 512, half * 512 + 512)
                        for k in range(KD):
                            if first and a == 0 and half == 0 and k % 2 == 0:
                                pe.wait_ge(wl_made, k // 2 + 1)
                            mm = products(pe, ps[:, a, cols], yh[:, a, k, :], yl[:, a, k, :], wh[:, k, cols], wl[:, k, cols], k == 0, k == KD - 1)
                    mm.then_inc(mixed, 1)
                if begun:
                    late(i - 1)
            pair(0, False, True)
            with pe.Fori(1, PAIRS) as i:
                pair(i, True, False)
            late(PAIRS - 1)


def phase_mlp(nc, T, W, R):
    ROUNDS = D_FF // 512
    with Scope(nc, "f") as s:
        hraw = s.sb("hraw", [P, 2, TG])
        hh = s.sb("hh", [P, KD, TG], F32R)
        hl = s.sb("hl", [P, KD, TG], F32R)
        up_raw = s.sb("up_raw", [P, 2, KD, 256])
        down_raw = s.sb("down_raw", [P, 2, 2, D])
        uph = s.sb("uph", [P, 2, KD, 256], F32R)
        upl = s.sb("upl", [P, 2, KD, 256], F32R)
        downh = s.sb("downh", [P, 2, 2, D], F32R)
        downl = s.sb("downl", [P, 2, 2, D], F32R)
        relu = s.sb("relu", [P, 2, TG])
        act2 = s.sb("act2", [P, 2, TG])
        ah = s.sb("ah", [P, 4, TG], F32R)
        al = s.sb("al", [P, 4, TG], F32R)
        total = s.sb("total", [P, 4, D])
        ps_u = s.psum("ps_u", [P, 4, TG])
        ps_d = s.psum("ps_d", [P, 2, D])
        h_loaded = [s.sem(f"h_loaded{i}") for i in range(2)]
        up_loaded = [s.sem(f"up_loaded{i}") for i in range(2)]
        down_loaded = [s.sem(f"down_loaded{i}") for i in range(2)]
        hh_made = s.sem("hh_made")
        hl_made = s.sem("hl_made")
        uph_made, downh_made = s.sem("uph_made"), s.sem("downh_made")
        upl_made, downl_made = s.sem("upl_made"), s.sem("downl_made")
        up_done = s.sem("up_done")
        relu_made, act2_made, ah_made = s.sem("relu_made"), s.sem("act2_made"), s.sem("ah_made")
        al_made = s.sem("al_made")
        down_done = s.sem("down_done")
        added = s.sem("added")
        cleared = s.sem("cleared")
        total_stored = s.sem("total_stored")
        spare = s.sem("spare")
        block = s.block()

        def n_of(g, j):
            return g * ROUNDS + j

        @block.sync
        def _(sp):
            sp.sem_inc(total_stored, 16)
            with sp.Fori(0, NG) as g:
                for k in range(KD):
                    sp.wait_ge(hl_made, g * KD + k + 1)
                    sp.dma_start(hraw[:, k % 2, :], W["h2t"][k * P:(k + 1) * P, bass.ds(g * TG, TG)]).then_inc(h_loaded[k % 2], 16)
                with sp.Fori(0, ROUNDS) as j:
                    for a in range(2):
                        at = j * 512 + a * 256
                        sp.wait_ge(upl_made, g * (2 * ROUNDS) + j * 2 + a + 1)
                        sp.dma_start(up_raw[:, a, :, :], T["w_up"][0].rearrange("(k p) n -> p k n", p=P)[:, :, bass.ds(at, 256)]).then_inc(up_loaded[a], 16)
                        sp.wait_ge(downl_made, g * (2 * ROUNDS) + j * 2 + a + 1)
                        sp.dma_start(down_raw[:, a, :, :], T["w_down"][0, bass.ds(at, 256), :].rearrange("(k p) n -> p k n", p=P)).then_inc(down_loaded[a], 16)

        @block.scalar
        def _(act):
            act.sem_inc(hl_made, 2)
            with act.Fori(0, NG) as g:
                for k in range(KD):
                    act.wait_ge(h_loaded[k % 2], g * (16 * KD // 2) + 16 * (k // 2 + 1))
                    if k == 0:
                        act.wait_ge(up_done, g * (4 * ROUNDS) + 4)
                    nc.scalar.activation(hh[:, k, :], hraw[:, k % 2, :], ACT.Copy).then_inc(hh_made, 1)
                with act.Fori(0, ROUNDS) as j:
                    n = g * ROUNDS + j
                    for a in range(2):
                        act.wait_ge(up_loaded[a], n * 16 + 16)
                        act.wait_ge(down_done, n * 4 + 4)
                        nc.scalar.activation(uph[:, a, :, :], up_raw[:, a, :, :], ACT.Copy).then_inc(uph_made, 1)
                        act.wait_ge(down_loaded[a], n * 16 + 16)
                        nc.scalar.activation(downh[:, a, :, :], down_raw[:, a, :, :], ACT.Copy).then_inc(downh_made, 1)
                    for f in range(4):
                        b = f % 2
                        act.wait_ge(up_done, n * 4 + f + 5)
                        act.wait_ge(al_made, n * 4 + f + 1)
                        nc.scalar.activation(relu[:, b, :], ps_u[:, f, :], ACT.Relu).then_inc(relu_made, 1)
                        act.wait_ge(relu_made, n * 4 + f + 1)
                        nc.scalar.activation(act2[:, b, :], relu[:, b, :], ACT.Square).then_inc(act2_made, 1)
                        act.wait_ge(act2_made, n * 4 + f + 1)
                        nc.scalar.activation(ah[:, f, :], act2[:, b, :], ACT.Copy).then_inc(ah_made, 1)
                act.wait_ge(added, g * (4 * ROUNDS) + 4 * ROUNDS + 2)
                act.dma_start(W["ff"][bass.ds(g * TG, TG), :].rearrange("(t p) n -> p t n", p=P), total[:, :, :]).then_inc(total_stored, 16)
            act.wait_ge(total_stored, 16 + 16 * NG)

        @block.gpsimd
        def _(pool):
            with pool.Fori(0, NG) as g:
                pool.wait_ge(total_stored, g * 16 + 16)
                pool.sem_inc(cleared, 1)
                nc.gpsimd.memset(total[:, :, :], 0.0).then_inc(cleared, 1)

        @block.vector
        def _(dve):
            dve.sem_inc(upl_made, 2)
            dve.sem_inc(downl_made, 2)
            dve.sem_inc(al_made, 2)
            dve.sem_inc(added, 2)
            with dve.Fori(0, NG) as g:
                for k in range(KD):
                    dve.wait_ge(hh_made, g * KD + k + 1)
                    nc.vector.tensor_tensor(hl[:, k, :], hraw[:, k % 2, :], hh[:, k, :].bitcast(F32), ALU.subtract).then_inc(hl_made, 1)
                with dve.Fori(0, ROUNDS) as j:
                    n = g * ROUNDS + j
                    for a in range(2):
                        dve.wait_ge(uph_made, n * 2 + a + 1)
                        nc.vector.tensor_tensor(upl[:, a, :, :], up_raw[:, a, :, :], uph[:, a, :, :].bitcast(F32), ALU.subtract).then_inc(upl_made, 1)
                        dve.wait_ge(downh_made, n * 2 + a + 1)
                        nc.vector.tensor_tensor(downl[:, a, :, :], down_raw[:, a, :, :], downh[:, a, :, :].bitcast(F32), ALU.subtract).then_inc(downl_made, 1)
                    for f in range(4):
                        dve.wait_ge(ah_made, n * 4 + f + 1)
                        nc.vector.tensor_tensor(al[:, f, :], act2[:, f % 2, :], ah[:, f, :].bitcast(F32), ALU.subtract).then_inc(al_made, 1)
                    dve.wait_ge(cleared, g * 2 + 2)
                    for t in range(4):
                        dve.wait_ge(down_done, n * 4 + t + 5)
                        dve.wait_ge(added, n * 4 + 2)
                        nc.vector.tensor_tensor(total[:, t, :], ps_d[:, t % 2, :], total[:, t, :], ALU.add).then_inc(added, 1)

        @block.tensor
        def _(pe):
            pe.sem_inc(up_done, 4)
            pe.sem_inc(down_done, 4)
            with pe.Fori(0, NG) as g:
                pe.wait_ge(hl_made, g * KD + KD + 2)
                pe.sem_inc(spare, 1)
                with pe.Fori(0, ROUNDS) as j:
                    n = g * ROUNDS + j
                    for f in range(4):
                        a, cols = f // 2, slice((f % 2) * P, (f % 2) * P + P)
                        if f % 2 == 0:
                            pe.wait_ge(upl_made, n * 2 + a + 3)
                        for k in range(KD):
                            mm = products(pe, ps_u[:, f, :], uph[:, a, k, cols], upl[:, a, k, cols], hh[:, k, :], hl[:, k, :], k == 0, k == KD - 1)
                        mm.then_inc(up_done, 1)
                    for t in range(4):
                        tokens = slice(t * P, (t + 1) * P)
                        pe.wait_ge(added, n * 4 + t + 1)
                        for half in range(2):
                            cols = slice(half * 512, half * 512 + 512)
                            for f in range(4):
                                if t == 0 and half == 0:
                                    pe.wait_ge(al_made, n * 4 + f + 3)
                                    if f % 2 == 0:
                                        pe.wait_ge(downl_made, n * 2 + f // 2 + 3)
                                mm = products(pe, ps_d[:, t % 2, cols], ah[:, f, tokens], al[:, f, tokens], downh[:, f // 2, f % 2, cols], downl[:, f // 2, f % 2, cols], f == 0, f == 3)
                        mm.then_inc(down_done, 1)


def phase_last_norm(nc, T, W, R):
    GROUPS = TILES // 4
    with Scope(nc, "n") as s:
        rows = s.sb("rows", [P, 3, D])
        ff = s.sb("ff", [P, 4, D])
        x1 = s.sb("x1", [P, 4, D])
        z = s.sb("z", [P, 4, D])
        xhat = s.sb("xhat", [P, D])
        xg = s.sb("xg", [P, 2, D])
        y = s.sb("y", [P, 2, D])
        stats = s.sb("stats", [P, 2, 6])
        moments = s.sb("moments", [P, 4, 2])
        var, root, rstd, tmp = (s.sb(n, [P, 4]) for n in ("var", "root", "rstd", "tmp"))
        rows_loaded = s.sem("rows_loaded")
        loaded = [s.sem(f"loaded{i}") for i in range(4)]
        summed = s.sem("summed")
        var_made, root_made, xg_made, y_made = s.sem("var_made"), s.sem("root_made"), s.sem("xg_made"), s.sem("y_made")
        xg_free = s.sem("xg_free")
        y_stored = [s.sem(f"y_stored{i}") for i in range(2)]
        dve_own, spare = s.sem("dve_own"), s.sem("spare")
        block = s.block()
        OWN = 4 * 4 + 4 + 4 * 2

        @block.sync
        def _(sp):
            load_rows(sp, rows_loaded, W, T, rows, 1, "ln2_g", "ln2_b")
            with sp.Fori(0, GROUPS) as i:
                for b in range(4):
                    tokens = bass.ds((i * 4 + b) * P, P)
                    sp.wait_ge(summed, i * 4 + b + 1)
                    sp.dma_start(ff[:, b, :], W["ff"][tokens, :]).then_inc(loaded[b], 16)
                    sp.dma_start(x1[:, b, :], W["x1"][tokens, :]).then_inc(loaded[b], 16)

        @block.scalar
        def _(act):
            for a in range(2):
                act.sem_inc(y_stored[a], 16)
            with act.Fori(0, GROUPS) as i:
                act.wait_ge(var_made, i + 1)
                nc.scalar.activation(root[:, :], var[:, :], ACT.Sqrt).then_inc(root_made, 1)
                for b in range(4):
                    act.wait_ge(y_made, i * 4 + b + 1)
                    act.dma_start(W["out"][bass.ds((i * 4 + b) * P, P), :], y[:, b % 2, :]).then_inc(y_stored[b % 2], 16)
            for a in range(2):
                act.wait_ge(y_stored[a], 16 + 16 * (TILES // 2))

        @block.vector
        def _(dve):
            dve.sem_inc(summed, 4)
            dve.wait_ge(rows_loaded, 48)
            with dve.Fori(0, GROUPS) as i:
                own = Chain(dve, dve_own, i * OWN, spare)
                for b in range(4):
                    dve.wait_ge(loaded[b], i * 32 + 32)
                    own.step(nc.vector.tensor_tensor(z[:, b, :], ff[:, b, :], rows[:, 0, :], ALU.mult))
                    own.step(nc.vector.scalar_tensor_tensor(out=z[:, b, :], in0=x1[:, b, :], scalar=ALPHA, in1=z[:, b, :], op0=ALU.mult, op1=ALU.add))
                    dve.sem_inc(summed, 1)
                    layer_norm_moments(nc, own, z[:, b, :], stats, moments[:, b, :])
                nc.vector.tensor_scalar(var[:, :], moments[:, :, 1], LN_EPS, None, ALU.add).then_inc(var_made, 1)
                dve.wait_ge(root_made, i + 1)
                refine_rsqrt(nc, own, rstd[:, :], var[:, :], root[:, :], tmp[:, :])
                for b in range(4):
                    own.step(nc.vector.tensor_scalar(xhat[:, :], z[:, b, :], moments[:, b, 0:1], rstd[:, b:b + 1], ALU.subtract, ALU.mult))
                    dve.wait_ge(xg_free, i * 4 + b + 1)
                    own.step(nc.vector.tensor_tensor(xg[:, b % 2, :], xhat[:, :], rows[:, 1, :], ALU.mult))
                    dve.sem_inc(xg_made, 1)
                assert own.n == OWN

        @block.gpsimd
        def _(pool):
            pool.sem_inc(xg_free, 2)
            pool.wait_ge(rows_loaded, 48)
            with pool.Fori(0, GROUPS) as i:
                for b in range(4):
                    pool.wait_ge(xg_made, i * 4 + b + 1)
                    pool.wait_ge(y_stored[b % 2], i * 32 + (b // 2) * 16 + 16)
                    nc.gpsimd.tensor_tensor(y[:, b % 2, :], xg[:, b % 2, :], rows[:, 2, :], ALU.add).then_inc(y_made, 1)
                    pool.wait_ge(y_made, i * 4 + b + 1)
                    pool.sem_inc(xg_free, 1)



PHASES = [phase_modulation, phase_projection, phase_stick_breaking, phase_latent_attention, phase_output_projection, phase_mlp, phase_last_norm]
DEBUG = None

def build(nc, T, out):
    W = {
        "xn": nc.dram_tensor("xn_scratch", (SEQ, D), F32).ap(),
        "xt": nc.dram_tensor("xt_scratch", (D, SEQ), F32).ap(),
        "qk": nc.dram_tensor("qk_scratch", (2 * SBW, SEQ), F32).ap(),
        "v": nc.dram_tensor("v_scratch", (SEQ, SBW), F32).ap(),
        "lq": nc.dram_tensor("lq_scratch", (HEADS, QK, SEQ), F32).ap(),
        "lk": nc.dram_tensor("lk_scratch", (HEADS * HD, SEQ), F32).ap(),
        "lkr": nc.dram_tensor("lkr_scratch", (ROPE, SEQ), F32).ap(),
        "lv": nc.dram_tensor("lv_scratch", (SEQ, HEADS * HD), F32).ap(),
        "yt": nc.dram_tensor("yt_scratch", (D, SEQ), F32).ap(),
        "inverse": nc.dram_tensor("inverse_scratch", (HEADS, SEQ), F32).ap(),
        "x1": nc.dram_tensor("x1_scratch", (SEQ, D), F32).ap(),
        "h2t": nc.dram_tensor("h2t_scratch", (D, SEQ), F32).ap(),
        "gate": nc.dram_tensor("gate_scratch", (2, D), F32).ap(),
        "seed": nc.dram_tensor("seed_scratch", (1, 16), F32).ap(),
        "ff": nc.dram_tensor("ff_scratch", (SEQ, D), F32).ap(),
    }
    W["out"] = out[0]
    with Scope(nc, "r") as s:
        R = {
            "ident": s.sb("ident", [P, P]), "ident_r": s.sb("ident_r", [P, P], F32R), "zeros": s.sb("zeros", [P, P]),
            "strict": s.sb("strict", [P, P], F32R), "halves": s.sb("halves", [P, 64], F32R),
            "shift": s.sb("shift", [P, 2, KD]), "scale": s.sb("scale", [P, 2, KD]),
        }
        for phase in PHASES:
            phase(nc, T, W, R)
        if DEBUG:
            with Scope(nc, "dbg") as d:
                done = d.sem("done")
                block = d.block()

                @block.sync
                def _(sp):
                    w = W[DEBUG] if len(W[DEBUG].shape) == 2 else W[DEBUG].rearrange("a b c -> (a b) c")
                    w = w.rearrange("a b -> (a b)").rearrange("(a b) -> a b", b=D)
                    n = min(SEQ, w.shape[0])
                    sp.dma_start(out[0, 0:n, :], w[0:n, :]).then_inc(done, 16)
                    sp.wait_ge(done, 16)


_INS = ['x', 'c', 'ln_in_g', 'ln_in_b', 'w_ada', 'b_ada', 'w_in', 'q_norm_g', 'kv_norm_g', 'w_uq', 'w_ukv', 'w_o',
        'ln1_g', 'ln1_b', 'w_up', 'w_down', 'ln2_g', 'ln2_b']
_OUTS = [((1, 2048, 1024), 'float32')]


def _rope_table():
    import numpy as _np
    inv_freq = (1.0 / (_np.float32(10000.0) ** (_np.arange(0, 32, 2, dtype=_np.float32) / _np.float32(32)))).astype(_np.float32)
    ang = (_np.arange(2048, dtype=_np.float32)[:, None] * inv_freq[None, :]).astype(_np.float32)
    cos, sin = _np.cos(ang).T.astype(_np.float32), _np.sin(ang).T.astype(_np.float32)
    half = _np.concatenate([cos, cos, -sin, sin], axis=0)
    return _np.ascontiguousarray(_np.concatenate([half, half], axis=0))


def kernel(**inputs):
    import numpy as _np
    import concourse.bacc as _bacc
    from concourse import mybir as _mybir
    from concourse.bass_utils import run_bass_kernel_spmd as _run

    nc = _bacc.Bacc("TRN2", target_bir_lowering=False, num_devices=1)
    arrays, T = {}, {}
    for name in _INS:
        a = _np.ascontiguousarray(inputs[name])
        arrays[f"in_{name}_dram"] = a
        T[name] = nc.dram_tensor(f"in_{name}_dram", a.shape, _mybir.dt.from_np(a.dtype), kind="ExternalInput").ap()
    arrays["rope_dram"] = _rope_table()
    T["rope"] = nc.dram_tensor("rope_dram", (128, 2048), F32, kind="ExternalInput").ap()
    (shape, dtype), = _OUTS
    out = nc.dram_tensor("out_0_dram", shape, _mybir.dt.from_np(_np.dtype(dtype)), kind="ExternalOutput").ap()
    build(nc, T, out)
    r = _run(nc, [arrays], core_ids=[0])
    return r.results[0]["out_0_dram"]
```

```python
from contextlib import ExitStack

import concourse.bass as bass
from concourse import mybir

ALU = mybir.AluOpType
ACT = mybir.ActivationFunctionType
F32 = mybir.dt.float32
F32R = mybir.dt.float32r

P = 128
SEQ = 2048
D = 1024
KD = D // P
TG = 512
NG = SEQ // TG
TILES = SEQ // P
HEADS = 8
HD = 64
ROPE = 32
QK = HD + ROPE
SBW = HEADS * HD
Q_RANK = 384
KV_RANK = 256
KQ = Q_RANK // P
KV = KV_RANK // P
D_FF = 4 * D
LN_EPS = 1e-5
RMS_EPS = 1e-6
ALPHA = 2.0 ** 0.25
SB_SCALE = HD ** -0.5
MLA_SCALE = QK ** -0.5
MASKED = -1e30


class Chain:

    def __init__(self, eng, sem, base=0, spare=None):
        self.eng, self.sem, self.base, self.spare, self.n = eng, sem, base, spare, 0

    def stand(self):
        self.eng.sem_inc(self.spare, 1)

    def step(self, instruction):
        self.n += 1
        instruction.then_inc(self.sem, 1)
        self.eng.wait_ge(self.sem, self.base + self.n)


class Scope:

    def __init__(self, nc, phase):
        self.nc, self.phase, self.ctx, self.sems = nc, phase, ExitStack(), []

    def __enter__(self):
        return self

    def __exit__(self, *exc):
        self.ctx.__exit__(*exc)
        if self.sems and exc[0] is None:
            self.nc.clear_and_free_semaphores(self.sems)
            self.nc.all_engine_barrier()

    def sb(self, name, shape, dtype=F32):
        return self.ctx.enter_context(self.nc.sbuf_tensor(f"{self.phase}_{name}", shape, dtype))

    def psum(self, name, shape):
        return self.ctx.enter_context(self.nc.psum_tensor(f"{self.phase}_{name}", shape, F32))

    def sem(self, name):
        self.sems.append(self.nc.alloc_semaphore(f"{self.phase}_{name}"))
        return self.sems[-1]

    def block(self):
        return self.ctx.enter_context(self.nc.Block())


def products(pe, out, wh, wl, xh, xl, first, last):
    pe.matmul(out, wh, xh, start=first, stop=False)
    pe.matmul(out, wl, xh, start=False, stop=False)
    return pe.matmul(out, wh, xl, start=False, stop=last)


def layer_norm_moments(nc, own, x, stats, moments):
    nc.vector.bn_stats(stats[:, 0, :], x[:, 0:512])
    own.step(nc.vector.bn_stats(stats[:, 1, :], x[:, 512:1024]))
    own.stand()
    own.step(nc.vector.bn_aggr(moments, stats[:, :, :].rearrange("p a b -> p (a b)")))


def refine_rsqrt(nc, own, rstd, var, root, tmp):
    own.step(nc.vector.reciprocal(rstd, root))
    own.step(nc.vector.tensor_tensor(tmp, rstd, rstd, ALU.mult))
    own.step(nc.vector.scalar_tensor_tensor(out=tmp, in0=tmp, scalar=-0.5, in1=var, op0=ALU.mult, op1=ALU.mult))
    own.step(nc.vector.scalar_tensor_tensor(out=rstd, in0=tmp, scalar=1.5, in1=rstd, op0=ALU.add, op1=ALU.mult))


def phase_modulation(nc, T, W, R):
    with Scope(nc, "m") as s:
        c_col = s.sb("c_col", [P, KD])
        c_sig = s.sb("c_sig", [P, KD])
        c_act = s.sb("c_act", [P, KD])
        gate = s.sb("gate", [1, 2, D])
        ones = s.sb("ones", [P, P])
        w = s.sb("w", [P, 3, KD, 512])
        b_row = s.sb("b_row", [1, 3, 512])
        partial = s.sb("partial", [P, 3, 512])
        gb = s.sb("gb", [P, 2, D])
        x = s.sb("x", [P, 4, D])
        xhat = s.sb("xhat", [P, D])
        xg = s.sb("xg", [P, 2, D])
        xn = s.sb("xn", [P, 2, D])
        xt = s.sb("xt", [P, 2, KD, P])
        stats = s.sb("stats", [P, 2, 6])
        moments = s.sb("moments", [P, 4, 2])
        var, root, rstd, tmp = (s.sb(n, [P, 4]) for n in ("var", "root", "rstd", "tmp"))
        ps_row = s.psum("ps_row", [P, D])
        ps_t = s.psum("ps_t", [P, 4, 4, P])
        ps_col = s.psum("ps_col", [P, 512])

        c_loaded, gb_loaded = s.sem("c_loaded"), s.sem("gb_loaded")
        w_loaded = [s.sem(f"w_loaded{i}") for i in range(3)]
        x_loaded = [s.sem(f"x_loaded{i}") for i in range(4)]
        xn_stored = [s.sem(f"xn_stored{i}") for i in range(2)]
        xt_stored = [s.sem(f"xt_stored{i}") for i in range(2)]
        ones_set, ident_set, c_sigmoid = s.sem("ones_set"), s.sem("ident_set"), s.sem("c_sigmoid")
        partial_made, mod_summed = s.sem("partial_made"), s.sem("mod_summed")
        mods_taken = s.sem("mods_taken")
        x_free = s.sem("x_free")
        xg_made, xg_free = s.sem("xg_made"), s.sem("xg_free")
        xn_made = s.sem("xn_made")
        x_turned = s.sem("x_turned")
        x_evacuated = s.sem("x_evacuated")
        gate_stored = s.sem("gate_stored")
        var_made, root_made = s.sem("var_made"), s.sem("root_made")
        dve_own, pool_own, spare = s.sem("dve_own"), s.sem("pool_own"), s.sem("spare")
        block = s.block()
        OWN = 4 * 2 + 4 + 4 * 2 + 3 * (KD - 1)

        @block.sync
        def _(sp):
            sp.dma_start(c_col[:, :], T["c"].rearrange("a (p k) -> (a p) k", k=KD)).then_inc(c_loaded, 16)
            for n, name in enumerate(("ln_in_g", "ln_in_b")):
                sp.dma_start(gb[:, n, :], T[name].rearrange("(a d) -> a d", a=1).to_broadcast([P, D])).then_inc(gb_loaded, 16)
            with sp.Fori(0, 4) as i:
                for b in range(4):
                    sp.wait_ge(x_free, i * 4 + b + 1)
                    sp.dma_start(x[:, b, :], T["x"][0, bass.ds((i * 4 + b) * P, P), :]).then_inc(x_loaded[b], 16)
                for a in range(3):
                    sp.wait_ge(partial_made, i * 3 + a + 1)
                    sp.dma_start(w[:, a, :, :], T["w_ada"][0].rearrange("(p k) n -> p k n", k=KD)[:, :, bass.ds((i * 3 + a) * 512, 512)]).then_inc(w_loaded[a], 16)
                    sp.wait_ge(mod_summed, i * 3 + a + 1)
                    sp.dma_start(b_row[:, a, :], T["b_ada"][:, bass.ds((i * 3 + a) * 512, 512)]).then_inc(w_loaded[a], 16)

        @block.scalar
        def _(act):
            act.sem_inc(x_evacuated, 2)
            for a in range(2):
                act.sem_inc(xt_stored[a], 16)
                act.sem_inc(xn_stored[a], 16)
            act.wait_ge(c_loaded, 16)
            nc.scalar.activation(c_sig[:, :], c_col[:, :], ACT.Sigmoid).then_inc(c_sigmoid, 1)
            with act.Fori(0, 4) as i:
                act.wait_ge(var_made, i + 1)
                nc.scalar.activation(root[:, :], var[:, :], ACT.Sqrt).then_inc(root_made, 1)
                for b in range(4):
                    a = b % 2
                    act.wait_ge(x_turned, i * 4 + b + 3)
                    act.dma_start(W["xn"][bass.ds((i * 4 + b) * P, P), :], xn[:, a, :]).then_inc(xn_stored[a], 16)
                    act.wait_ge(xt_stored[a], i * 32 + (b // 2) * 16 + 16)
                    nc.scalar.activation(xt[:, a, 0:4, :], ps_t[:, 2 * a, :, :], ACT.Copy)
                    nc.scalar.activation(xt[:, a, 4:8, :], ps_t[:, 2 * a + 1, :, :], ACT.Copy).then_inc(x_evacuated, 1)
                    act.wait_ge(x_evacuated, i * 4 + b + 3)
                    act.dma_start(W["xt"].rearrange("(k p) t -> p k t", p=P)[:, :, bass.ds((i * 4 + b) * P, P)], xt[:, a, :, :]).then_inc(xt_stored[a], 16)
            act.wait_ge(mods_taken, 3)
            act.dma_start(W["gate"].rearrange("(a g) d -> a g d", a=1), gate[:, :, :]).then_inc(gate_stored, 16)
            act.wait_ge(gate_stored, 16)
            for a in range(2):
                act.wait_ge(xt_stored[a], 16 + 16 * (TILES // 2))
                act.wait_ge(xn_stored[a], 16 + 16 * (TILES // 2))

        @block.gpsimd
        def _(pool):
            pool.sem_inc(xg_free, 2)
            nc.gpsimd.memset(ones[:, :], 1.0).then_inc(ones_set, 1)
            pool.wait_ge(ones_set, 1)
            nc.gpsimd.affine_select(out=R["ident"][:, :], in_=ones[:, :], compare_op=ALU.is_equal, fill=0.0,
                                    base=0, pattern=[[-1, P]], channel_multiplier=1).then_inc(ident_set, 1)
            nc.gpsimd.affine_select(out=R["ident_r"][:, :], in_=ones[:, :], compare_op=ALU.is_equal, fill=0.0,
                                    base=0, pattern=[[-1, P]], channel_multiplier=1)
            nc.gpsimd.memset(R["zeros"][:, :], 0.0).then_inc(pool_own, 1)
            pool.wait_ge(pool_own, 1)
            nc.gpsimd.affine_select(out=R["strict"][:, :], in_=R["zeros"][:, :], compare_op=ALU.is_gt, fill=MASKED,
                                    base=0, pattern=[[-1, P]], channel_multiplier=1)
            nc.gpsimd.affine_select(out=R["halves"][:, :], in_=R["zeros"][:, 0:64], compare_op=ALU.is_ge, fill=MASKED,
                                    base=-64, pattern=[[0, 64]], channel_multiplier=1)
            pool.wait_ge(gb_loaded, 32)
            with pool.Fori(0, TILES // 2) as i:
                for a in range(2):
                    pool.wait_ge(xg_made, i * 2 + a + 1)
                    pool.wait_ge(xn_stored[a], i * 16 + 16)
                    pool.wait_ge(x_turned, i * 2 + a + 1)
                    nc.gpsimd.tensor_tensor(xn[:, a, :], xg[:, a, :], gb[:, 1, :], ALU.add).then_inc(xn_made, 1)
                    pool.wait_ge(xn_made, i * 2 + a + 1)
                    pool.sem_inc(xg_free, 1)

        @block.vector
        def _(dve):
            dve.sem_inc(mods_taken, 1)
            dve.sem_inc(partial_made, 3)
            dve.sem_inc(x_free, 4)
            dve.wait_ge(c_sigmoid, 1)
            own = Chain(dve, dve_own)
            own.step(nc.vector.tensor_tensor(c_act[:, :], c_col[:, :], c_sig[:, :], ALU.mult))
            dve.wait_ge(gb_loaded, 32)
            with dve.Fori(0, 2) as half:
                for h in range(2):
                    i = half * 2 + h
                    own = Chain(dve, dve_own, i * OWN + 1, spare)
                    for b in range(4):
                        dve.wait_ge(x_loaded[b], i * 16 + 16)
                        layer_norm_moments(nc, own, x[:, b, :], stats, moments[:, b, :])
                    nc.vector.tensor_scalar(var[:, :], moments[:, :, 1], LN_EPS, None, ALU.add).then_inc(var_made, 1)
                    dve.wait_ge(root_made, i + 1)
                    refine_rsqrt(nc, own, rstd[:, :], var[:, :], root[:, :], tmp[:, :])
                    for b in range(4):
                        own.step(nc.vector.tensor_scalar(xhat[:, :], x[:, b, :], moments[:, b, 0:1], rstd[:, b:b + 1], ALU.subtract, ALU.mult))
                        dve.sem_inc(x_free, 1)
                        dve.wait_ge(xg_free, i * 4 + b + 1)
                        own.step(nc.vector.tensor_tensor(xg[:, b % 2, :], xhat[:, :], gb[:, 0, :], ALU.mult))
                        dve.sem_inc(xg_made, 1)
                    for a in range(3):
                        dve.wait_ge(w_loaded[a], i * 32 + 32)
                        dve.wait_ge(mod_summed, i * 3 + a + 1)
                        part = partial[:, a, :]
                        own.step(nc.vector.tensor_scalar(part, w[:, a, 0, :], c_act[:, 0:1], None, ALU.mult))
                        for k in range(1, KD):
                            add = nc.vector.scalar_tensor_tensor(out=part, in0=w[:, a, k, :], scalar=c_act[:, k:k + 1], in1=part, op0=ALU.mult, op1=ALU.add)
                            if k < KD - 1:
                                own.step(add)
                        add.then_inc(partial_made, 1)
                    assert own.n == OWN
                dve.wait_ge(mod_summed, half * 6 + 9)
                columns = ps_col[:, 0:2 * KD].rearrange("p (v k) -> p v k", v=2)
                nc.vector.tensor_copy(R["shift"][:, bass.ds(half, 1), :], columns[:, 0:1, :])
                nc.vector.tensor_scalar(R["scale"][:, bass.ds(half, 1), :], columns[:, 1:2, :], 1.0, None, ALU.add)
                nc.vector.tensor_scalar(gate[0:1, bass.ds(half, 1), :], ps_row[0:1, :].rearrange("p (a n) -> p a n", a=1), 1.0, None, ALU.add).then_inc(mods_taken, 1)

        @block.tensor
        def _(pe):
            pe.sem_inc(x_turned, 2)
            pe.sem_inc(mod_summed, 3)
            pe.wait_ge(ident_set, 1)

            def chunk(c, a):
                if c < 4:
                    for t in range(4):
                        out, rows = ps_col[:, 4 * c + t:4 * c + t + 1], slice(t * P, (t + 1) * P)
                        pe.matmul(out, partial[:, a, rows], ones[:, 0:1], start=True, stop=False)
                        mm = pe.matmul(out, b_row[0:1, a, rows], ones[0:1, 0:1], start=False, stop=True)
                else:
                    out = ps_row[0:1, (c - 4) * 512:(c - 3) * 512]
                    pe.matmul(out, ones[:, 0:1], partial[:, a, :], start=True, stop=False)
                    mm = pe.matmul(out, ones[0:1, 0:1], b_row[0:1, a, :], start=False, stop=True)
                return mm

            with pe.Fori(0, 2) as half:
                pe.wait_ge(mods_taken, half + 1)
                for h in range(2):
                    i = half * 2 + h
                    for b in range(4):
                        a = b % 2
                        pe.wait_ge(xn_made, i * 4 + b + 1)
                        pe.wait_ge(x_evacuated, i * 4 + b + 1)
                        for k in range(KD):
                            mm = pe.transpose(ps_t[:, 2 * a + k // 4, k % 4, :], xn[:, a, k * P:(k + 1) * P], R["ident"][:, :])
                        mm.then_inc(x_turned, 1)
                    for a in range(3):
                        pe.wait_ge(w_loaded[a], i * 32 + 32)
                        pe.wait_ge(partial_made, i * 3 + a + 4)
                        chunk(h * 3 + a, a).then_inc(mod_summed, 1)

def phase_projection(nc, T, W, R):
    JOBS, BANKS = 36, 6
    UNIT_JOB = [0, 1, 2, 3, 4, 5, 6, 7, 8, 10, 11, 13, 14, 15]
    STREAM = len(UNIT_JOB)
    SUM_Q, SUM_KV, V_JOB, Q_JOB, K_JOB, LV_JOB = 9, 12, 16, 20, 28, 32
    STAGED_JOBS = [6, 7, 8, 10, 11, 13, 14, 15] + list(range(16, 36))
    STAGED = len(STAGED_JOBS)
    STAGES = 4
    FIXED = 9
    LAT = KQ + KV
    LATENT_AT, ROTARY_AT = 3 * SBW, 3 * SBW + Q_RANK + KV_RANK
    with Scope(nc, "p") as s:
        xraw = s.sb("xraw", [P, 2, TG])
        hmod = s.sb("hmod", [P, 2, TG])
        hh = s.sb("hh", [P, KD, TG], F32R)
        hl = s.sb("hl", [P, KD, TG], F32R)
        wraw = s.sb("wraw", [P, 2, 1024])
        wh = s.sb("wh", [P, 2, 1024], F32R)
        wl = s.sb("wl", [P, 2, 1024], F32R)
        wvh = s.sb("wvh", [P, KD, SBW], F32R)
        wvl = s.sb("wvl", [P, KD, SBW], F32R)
        wqh = s.sb("wqh", [P, KQ, HEADS, P], F32R)
        wql = s.sb("wql", [P, KQ, HEADS, P], F32R)
        wkh = s.sb("wkh", [P, KV, 1024], F32R)
        wkl = s.sb("wkl", [P, KV, 1024], F32R)
        gains = s.sb("gains", [P, LAT])
        ones = s.sb("ones", [P, P])
        lat = s.sb("lat", [P, LAT, TG])
        lsq = s.sb("lsq", [P, KQ, TG])
        var, root, rstd, tmp = (s.sb(n, [P, TG]) for n in ("var", "root", "rstd", "tmp"))
        lath = s.sb("lath", [P, LAT, TG], F32R)
        latl = s.sb("latl", [P, LAT, TG], F32R)
        table = s.sb("table", [P, SEQ])
        turn = s.sb("turn", [P, 2, TG])
        kr = s.sb("kr", [ROPE, TG])
        stage = s.sb("stage", [P, STAGES, TG])
        seed = s.sb("seed", [1, 16])
        ps = s.psum("ps", [P, BANKS, TG])

        xraw_loaded = [s.sem(f"xraw_loaded{i}") for i in range(2)]
        h_made = s.sem("h_made")
        w_loaded = [s.sem(f"w_loaded{i}") for i in range(2)]
        gains_loaded, table_loaded = s.sem("gains_loaded"), s.sem("table_loaded")
        hh_made, hl_made, wh_made, wl_made, ones_set = (s.sem(n) for n in ("hh_made", "hl_made", "wh_made", "wl_made", "ones_set"))
        job_done = s.sem("job_done")
        bank_free = [s.sem(f"bank_free{i}") for i in range(BANKS)]
        lsq_made, var_made, root_made, latn_made = (s.sem(n) for n in ("lsq_made", "var_made", "root_made", "latn_made"))
        lath_made, latl_made = s.sem("lath_made"), s.sem("latl_made")
        act_staged, dve_staged, kr_made = s.sem("act_staged"), s.sem("dve_staged"), s.sem("kr_made")
        stage_free = s.sem("stage_free")
        kr_free = s.sem("kr_free")
        stored = [s.sem(f"stored{i}") for i in range(2)]
        kr_stored, seed_set = s.sem("kr_stored"), s.sem("seed_set")
        dve_own, spare = s.sem("dve_own"), s.sem("spare")
        block = s.block()
        OWN = 2 * (HEADS + 1) + 4 * 2

        fixed_dmas = [1] * 4 + [3] * 3 + [1] * 2
        unit_dmas = [3 if u == 5 else 1 for u in range(STREAM)]

        def arrived(eng, g, m):
            slot = m % 2
            before = sum(n for j, n in enumerate(fixed_dmas) if j % 2 == slot and j <= m)
            if m >= FIXED:
                per_group = sum(n for u, n in enumerate(unit_dmas) if (FIXED + u) % 2 == slot)
                before += sum(n for u, n in enumerate(unit_dmas) if (FIXED + u) % 2 == slot and u <= m - FIXED)
                eng.wait_ge(w_loaded[slot], g * (16 * per_group) + 16 * before)
            else:
                eng.wait_ge(w_loaded[slot], 16 * before)

        def target(m, high):
            w, v, q, k = (wh, wvh, wqh, wkh) if high else (wl, wvl, wql, wkl)
            if m < 4:
                return v[:, 2 * m:2 * m + 2, :].rearrange("p k n -> p (k n)")
            if m < 7:
                return q[:, m - 4, :, :].rearrange("p h n -> p (h n)")
            if m < FIXED:
                return k[:, m - 7, :]
            return w[:, m % 2, 0:KD * 2 * ROPE] if m - FIXED == 5 else w[:, m % 2, :]

        def raw(m):
            return wraw[:, m % 2, 0:KD * 2 * ROPE] if m - FIXED == 5 else wraw[:, m % 2, :]

        def load_fixed(sp, m):
            done = w_loaded[m % 2]
            if m < 4:
                sp.dma_start(raw(m).rearrange("p (k n) -> p k n", k=2),
                             T["w_in"][0, m * 256:(m + 1) * 256, 2 * SBW:3 * SBW].rearrange("(k p) n -> p k n", p=P)).then_inc(done, 16)
            elif m < 7:
                rows = T["w_uq"][0, (m - 4) * P:(m - 3) * P, :].rearrange("p (h n) -> p h n", n=QK)
                to = raw(m).rearrange("p (h n) -> p h n", n=P)
                sp.dma_start(to[:, :, 0:QK], rows).then_inc(done, 16)
                sp.dma_start(to[:, :, QK:QK + 16], rows[:, :, HD + 16:QK]).then_inc(done, 16)
                sp.dma_start(to[:, :, QK + 16:P], rows[:, :, HD:HD + 16]).then_inc(done, 16)
            else:
                sp.dma_start(raw(m), T["w_ukv"][0, (m - 7) * P:(m - 6) * P, :]).then_inc(done, 16)

        def load_unit(sp, u):
            source = T["w_in"][0].rearrange("(k p) n -> p k n", p=P)
            to = raw(FIXED + u).rearrange("p (k n) -> p k n", k=KD)
            done = w_loaded[(FIXED + u) % 2]
            if u == 5:
                c = ROTARY_AT
                sp.dma_start(to[:, :, 0:ROPE], source[:, :, c:c + ROPE]).then_inc(done, 16)
                sp.dma_start(to[:, :, ROPE:ROPE + 16], source[:, :, c + 16:c + ROPE]).then_inc(done, 16)
                sp.dma_start(to[:, :, ROPE + 16:2 * ROPE], source[:, :, c:c + 16]).then_inc(done, 16)
            else:
                c = LATENT_AT + u * P if u < 5 else (u - 6) * P
                sp.dma_start(to, source[:, :, c:c + P]).then_inc(done, 16)

        @block.sync
        def _(sp):
            def load_slice(g, k):
                sp.wait_ge(h_made, g * KD + k + 1)
                sp.dma_start(xraw[:, k % 2, :], W["xt"][k * P:(k + 1) * P, bass.ds(g * TG, TG)]).then_inc(xraw_loaded[k % 2], 16)

            def stream(g, first, last):
                for u in range(first, last):
                    sp.wait_ge(wl_made, g * STREAM + FIXED + u - 1)
                    load_unit(sp, u)

            for m in range(FIXED):
                if m >= 2:
                    sp.wait_ge(wl_made, m - 1)
                load_fixed(sp, m)
                if m < KD:
                    load_slice(0, m)
            stream(0, 0, 2)
            sp.dma_start(table[:, :], T["rope"]).then_inc(table_loaded, 16)
            with nc.allow_non_contiguous_dma(reason="five columns of gains"):
                sp.dma_start(gains[:, 0:KQ], T["q_norm_g"][0].rearrange("(k p) -> p k", p=P)).then_inc(gains_loaded, 16)
                sp.dma_start(gains[:, KQ:LAT], T["kv_norm_g"][0].rearrange("(k p) -> p k", p=P)).then_inc(gains_loaded, 16)
            stream(0, 2, STREAM)
            with sp.Fori(1, NG) as g:
                stream(g, 0, 2)
                for k in range(KD):
                    load_slice(g, k)
                stream(g, 2, STREAM)

        @block.scalar
        def _(act):
            for b in range(BANKS):
                act.sem_inc(bank_free[b], 1)
            act.sem_inc(h_made, 2)
            act.sem_inc(stage_free, 3)

            def high_half(g, m):
                arrived(act, g, m)
                nc.scalar.activation(target(m, True), raw(m), ACT.Copy).then_inc(wh_made, 1)

            def high_slice(g, k, first):
                act.wait_ge(xraw_loaded[k % 2], g * (16 * KD // 2) + 16 * (k // 2 + 1))
                if k >= 2 or not first:
                    act.wait_ge(hl_made, g * KD + k - 1)
                nc.scalar.activation(hmod[:, k % 2, :], xraw[:, k % 2, :], ACT.Identity,
                                     bias=R["shift"][:, 0, k:k + 1], scale=R["scale"][:, 0, k:k + 1]).then_inc(h_made, 1)
                act.wait_ge(h_made, g * KD + k + 3)
                nc.scalar.activation(hh[:, k, :], hmod[:, k % 2, :], ACT.Copy).then_inc(hh_made, 1)

            def to_stage(g, job, rows=P):
                n = STAGED_JOBS.index(job)
                act.wait_ge(job_done, g * JOBS + job + 1)
                act.wait_ge(stage_free, g * STAGED + n + 1)
                out = nc.scalar.activation(stage[0:rows, n % STAGES, :], ps[0:rows, job % BANKS, :], ACT.Copy)
                if rows == P:
                    out.then_inc(bank_free[job % BANKS], 1)
                    act.wait_ge(bank_free[job % BANKS], g * (JOBS // BANKS) + job // BANKS + 2)
                    act.sem_inc(act_staged, 1)
                else:
                    out.then_inc(act_staged, 1)

            def group(g, more):
                for u in range(STREAM):
                    job = UNIT_JOB[u]
                    if u < LAT:
                        act.wait_ge(job_done, g * JOBS + job + 1)
                        if u < KQ:
                            nc.scalar.activation(lsq[:, u, :], ps[:, job % BANKS, :], ACT.Square).then_inc(lsq_made, 1)
                        nc.scalar.activation(lat[:, u, :], ps[:, job % BANKS, :], ACT.Copy).then_inc(bank_free[job % BANKS], 1)
                    elif u == 5:
                        act.wait_ge(job_done, g * JOBS + job + 1)
                    else:
                        to_stage(g, job)
                    if u + 2 < STREAM:
                        high_half(g, FIXED + u + 2)
                    if job == SUM_Q + 1:
                        for j in range(KV):
                            nc.scalar.activation(lsq[:, j, :], lat[:, KQ + j, :], ACT.Square).then_inc(lsq_made, 1)
                        act.wait_ge(var_made, g * 2 + 1)
                        nc.scalar.activation(root[:, :], var[:, :], ACT.Sqrt).then_inc(root_made, 1)
                    if job == SUM_Q + 2:
                        for j in range(KQ):
                            act.wait_ge(latn_made, g * LAT + j + 1)
                            nc.scalar.activation(lath[:, j, :], lat[:, j, :], ACT.Copy).then_inc(lath_made, 1)
                    if job == SUM_KV + 1:
                        act.wait_ge(var_made, g * 2 + 2)
                        nc.scalar.activation(root[:, :], var[:, :], ACT.Sqrt).then_inc(root_made, 1)
                for j in range(KQ, LAT):
                    act.wait_ge(latn_made, g * LAT + j + 1)
                    nc.scalar.activation(lath[:, j, :], lat[:, j, :], ACT.Copy).then_inc(lath_made, 1)
                for t in range(4):
                    to_stage(g, V_JOB + t)
                if more:
                    high_half(g + 1, FIXED)
                    high_half(g + 1, FIXED + 1)
                for h in range(HEADS):
                    to_stage(g, Q_JOB + h, HD)
                    if more:
                        high_slice(g + 1, h, False)
                for job in range(K_JOB, JOBS):
                    to_stage(g, job)

            for m in range(FIXED + 2):
                high_half(0, m)
                if m < KD:
                    high_slice(0, m, True)
            with act.Fori(0, NG - 1) as g:
                group(g, True)
            group(NG - 1, False)

        @block.vector
        def _(dve):
            def low_half(g, m):
                done = m + 1 if m < FIXED else g * STREAM + m + 1
                dve.wait_ge(wh_made, done)
                nc.vector.tensor_tensor(target(m, False), raw(m), target(m, True).bitcast(F32), ALU.subtract).then_inc(wl_made, 1)

            def low_slice(g, k):
                dve.wait_ge(hh_made, g * KD + k + 1)
                nc.vector.tensor_tensor(hl[:, k, :], hmod[:, k % 2, :], hh[:, k, :].bitcast(F32), ALU.subtract).then_inc(hl_made, 1)

            def rotate(own, g, job, lo, out):
                position = bass.ds(g * TG, TG)
                own.step(nc.vector.tensor_tensor(turn[lo:lo + ROPE, 0, :], ps[lo:lo + ROPE, job % BANKS, :], table[lo:lo + ROPE, position], ALU.mult))
                own.step(nc.vector.tensor_tensor(turn[lo:lo + ROPE, 1, :], ps[lo + ROPE:lo + 2 * ROPE, job % BANKS, :], table[lo + ROPE:lo + 2 * ROPE, position], ALU.mult))
                return nc.vector.tensor_tensor(out, turn[lo:lo + ROPE, 0, :], turn[lo:lo + ROPE, 1, :], ALU.add)

            def normalise(own, g, which, first, last, width):
                job = (SUM_Q, SUM_KV)[which]
                dve.wait_ge(job_done, g * JOBS + job + 1)
                nc.vector.tensor_scalar(var[:, :], ps[:, job % BANKS, :], 1.0 / width, RMS_EPS, ALU.mult, ALU.add).then_inc(var_made, 1)
                dve.wait_ge(var_made, g * 2 + which + 1)
                dve.sem_inc(bank_free[job % BANKS], 1)
                dve.wait_ge(root_made, g * 2 + which + 1)
                refine_rsqrt(nc, own, rstd[:, :], var[:, :], root[:, :], tmp[:, :])
                for j in range(first, last):
                    nc.vector.scalar_tensor_tensor(out=lat[:, j, :], in0=lat[:, j, :], scalar=gains[:, j:j + 1], in1=rstd[:, :],
                                                   op0=ALU.mult, op1=ALU.mult).then_inc(latn_made, 1)

            def low_latents(g, first, last):
                for j in range(first, last):
                    dve.wait_ge(lath_made, g * LAT + j + 1)
                    nc.vector.tensor_tensor(latl[:, j, :], lat[:, j, :], lath[:, j, :].bitcast(F32), ALU.subtract).then_inc(latl_made, 1)

            def group(g, more):
                own = Chain(dve, dve_own, g * OWN)
                for u in range(STREAM):
                    job = UNIT_JOB[u]
                    if u == 5:
                        dve.wait_ge(job_done, g * JOBS + job + 1)
                        dve.wait_ge(kr_free, g + 1)
                        rotate(own, g, job, 0, kr[:, :]).then_inc(kr_made, 1)
                        dve.sem_inc(bank_free[job % BANKS], 1)
                    if u + 2 < STREAM:
                        low_half(g, FIXED + u + 2)
                    if job == SUM_Q + 1:
                        normalise(own, g, 0, 0, KQ, Q_RANK)
                    if job == SUM_Q + 2:
                        low_latents(g, 0, KQ)
                    if job == SUM_KV + 1:
                        dve.wait_ge(latn_made, g * LAT + KQ)
                        normalise(own, g, 1, KQ, LAT, KV_RANK)
                low_latents(g, KQ, LAT)
                if more:
                    low_half(g + 1, FIXED)
                    low_half(g + 1, FIXED + 1)
                for h in range(HEADS):
                    n = STAGED_JOBS.index(Q_JOB + h)
                    dve.wait_ge(job_done, g * JOBS + Q_JOB + h + 1)
                    if h:
                        dve.wait_ge(dve_staged, g * HEADS + h)
                    dve.wait_ge(act_staged, g * STAGED + n + 1)
                    rotate(own, g, Q_JOB + h, HD, stage[HD:QK, n % STAGES, :]).then_inc(dve_staged, 1)
                    dve.sem_inc(bank_free[(Q_JOB + h) % BANKS], 1)
                    if more:
                        low_slice(g + 1, h)
                dve.wait_ge(dve_staged, g * HEADS + HEADS)
                assert own.n == OWN

            for m in range(FIXED + 2):
                low_half(0, m)
                if m < KD:
                    low_slice(0, m)
            dve.wait_ge(table_loaded, 16)
            dve.wait_ge(gains_loaded, 32)
            with dve.Fori(0, NG - 1) as g:
                group(g, True)
            group(NG - 1, False)

        @block.gpsimd
        def _(pool):
            nc.gpsimd.memset(ones[:, :], 1.0).then_inc(ones_set, 1)
            nc.gpsimd.memset(seed[:, :], 0.0).then_inc(seed_set, 1)
            pool.sem_inc(kr_free, 1)
            pool.wait_ge(seed_set, 1)
            pool.dma_start(W["seed"], seed[:, :]).then_inc(stored[1], 16)

            def target_of(g, job):
                tokens = bass.ds(g * TG, TG)
                if job < V_JOB:
                    r = UNIT_JOB.index(job) - 6
                    return W["qk"][r * P:(r + 1) * P, tokens], P
                if job < Q_JOB:
                    return W["v"][bass.ds(g * TG + (job - V_JOB) * P, P), :], P
                if job < K_JOB:
                    return W["lq"][job - Q_JOB][:, tokens], QK
                if job < LV_JOB:
                    return W["lk"][(job - K_JOB) * P:(job - K_JOB + 1) * P, tokens], P
                return W["lv"][bass.ds(g * TG + (job - LV_JOB) * P, P), :], P

            with pool.Fori(0, NG) as g:
                for n, job in enumerate(STAGED_JOBS):
                    if Q_JOB <= job < K_JOB:
                        pool.wait_ge(dve_staged, g * HEADS + job - Q_JOB + 1)
                    pool.wait_ge(act_staged, g * STAGED + n + 1)
                    pool.sem_inc(spare, 1)
                    to, rows = target_of(g, job)
                    pool.dma_start(to, stage[0:rows, n % STAGES, :]).then_inc(stored[n % 2], 16)
                    before = (n - 1) % 2
                    uses = g * (STAGED // 2) + ((n - 1) // 2 + 1) + before
                    pool.wait_ge(stored[before], uses * 16)
                    pool.sem_inc(stage_free, 1)
                    if n == 0:
                        pool.wait_ge(kr_made, g + 1)
                        pool.sem_inc(spare, 1)
                        pool.dma_start(W["lkr"][:, bass.ds(g * TG, TG)], kr[:, :]).then_inc(kr_stored, 16)
                        pool.wait_ge(kr_stored, g * 16 + 16)
                        pool.sem_inc(kr_free, 1)
            pool.wait_ge(stored[0], 16 * NG * STAGED // 2)
            pool.wait_ge(stored[1], 16 * (NG * STAGED // 2 + 1))

        @block.tensor
        def _(pe):
            def open_job(g, job):
                pe.wait_ge(bank_free[job % BANKS], g * (JOBS // BANKS) + job // BANKS + 1)
                return ps[:, job % BANKS, :]

            def squares_summed(g, job, first, n):
                pe.wait_ge(lsq_made, g * LAT + first + n)
                bank = open_job(g, job)
                for j in range(n):
                    mm = pe.matmul(bank, ones[:, :], lsq[:, j, :], start=(j == 0), stop=(j == n - 1))
                mm.then_inc(job_done, 1)

            pe.wait_ge(ones_set, 1)
            with pe.Fori(0, NG) as g:
                for u in range(STREAM):
                    job = UNIT_JOB[u]
                    if job == SUM_Q + 1:
                        squares_summed(g, SUM_Q, 0, KQ)
                    if job == SUM_KV + 1:
                        squares_summed(g, SUM_KV, KQ, KV)
                    m = FIXED + u
                    width = 2 * ROPE if u == 5 else P
                    high = target(m, True).rearrange("p (k n) -> p k n", k=KD)
                    low = target(m, False).rearrange("p (k n) -> p k n", k=KD)
                    pe.wait_ge(wl_made, g * STREAM + m + 1)
                    out = open_job(g, job)[0:width, :]
                    for k in range(KD):
                        if u == 0:
                            pe.wait_ge(hl_made, g * KD + k + 1)
                        mm = products(pe, out, high[:, k, :], low[:, k, :], hh[:, k, :], hl[:, k, :], k == 0, k == KD - 1)
                    mm.then_inc(job_done, 1)
                for t in range(4):
                    out = open_job(g, V_JOB + t)
                    rows = slice(t * P, (t + 1) * P)
                    for k in range(KD):
                        mm = products(pe, out, hh[:, k, rows], hl[:, k, rows], wvh[:, k, :], wvl[:, k, :], k == 0, k == KD - 1)
                    mm.then_inc(job_done, 1)
                pe.wait_ge(latl_made, g * LAT + LAT)
                for h in range(HEADS):
                    out = open_job(g, Q_JOB + h)
                    for k in range(KQ):
                        mm = products(pe, out, wqh[:, k, h, :], wql[:, k, h, :], lath[:, k, :], latl[:, k, :], k == 0, k == KQ - 1)
                    mm.then_inc(job_done, 1)
                for t in range(4):
                    out = open_job(g, K_JOB + t)
                    cols = slice(t * P, (t + 1) * P)
                    for k in range(KV):
                        mm = products(pe, out, wkh[:, k, cols], wkl[:, k, cols], lath[:, KQ + k, :], latl[:, KQ + k, :], k == 0, k == KV - 1)
                    mm.then_inc(job_done, 1)
                for t in range(4):
                    out = open_job(g, LV_JOB + t)
                    rows = slice(t * P, (t + 1) * P)
                    for k in range(KV):
                        mm = products(pe, out, lath[:, KQ + k, rows], latl[:, KQ + k, rows], wkh[:, k, 512:1024], wkl[:, k, 512:1024], k == 0, k == KV - 1)
                    mm.then_inc(job_done, 1)


S_BANKS, T_BANKS = 5, 2


def chunks_of(qb):
    length = (qb + 1) * P
    return [slice(c, min(c + 512, length)) for c in range(0, length, 512)]


def chunk_base(qb):
    return sum(len(chunks_of(q)) for q in range(qb))


CHUNKS = chunk_base(TILES)
UNITS = sum(g + 1 for g in range(NG))
UNIT_RING = 5
LATE = 6
VALUES_AT = ((15, (2, 2)), (19, (2, 2, 2, 2)), (31, (4, 2, 2, 2, 2)), (47, (4, 4, 2, 2, 2, 2)))
PIECE_AT = {start + i: (g, range(sum(sizes[:i]), sum(sizes[:i + 1])))
            for g, (start, sizes) in enumerate(VALUES_AT) for i in range(len(sizes))}
Y_AT = {start + len(sizes): g for g, (start, sizes) in enumerate(VALUES_AT)}
SLOTS = max(Y_AT) + 1
SPLIT_AT = {24: 0, 28: 1, 34: 2}
SPLIT_LOW_AT = {k + 2: part for k, part in SPLIT_AT.items()}


def late_chunk(lag):
    return lambda k: k - lag if 0 <= k - lag < CHUNKS else None


def due(what, H, a, k, begun):
    if what(k) is not None:
        return H, a, what(k)
    if begun and k < CHUNKS and what(k + CHUNKS) is not None:
        return H - 1, 1 - a, what(k + CHUNKS)
    return None


def over_heads(eng, slot):
    def pair(i, begun, more):
        for a in range(2):
            for k in range(CHUNKS):
                slot(i * 2 + a, a, k, begun or a > 0, more or a == 0)
    pair(0, False, True)
    with eng.Fori(1, HEADS // 2 - 1) as i:
        pair(i, True, True)
    pair(HEADS // 2 - 1, True, False)
    for k in range(CHUNKS, SLOTS):
        slot(HEADS - 1, 1, k, True, False)


class AttentionSide:

    def __init__(self, nc, s, W, row0, order, ring):
        self.nc, self.W, self.row0, self.order, self.ring = nc, W, row0, order, ring
        self.table = [(qb, j, cols) for qb in range(TILES) for j, cols in enumerate(order(qb))]
        self.v_raw = s.sb("v_raw", [P, TILES, HD])
        self.v_halves = [s.sb(f"v_halves{a}", [P, TILES, 2 * HD], F32R) for a in range(2)]
        self.turned_high = s.sb("turned_high", [P, UNIT_RING * 4, TG], F32R)
        self.turned_low = s.sb("turned_low", [P, UNIT_RING * 4, TG], F32R)
        self.y_low = s.sb("y_low", [HD, TG])
        self.y = s.sb("y", [HD, TG])
        self.ps_s = s.psum("ps_s", [P, S_BANKS, 512])
        self.ps_t = s.psum("ps_t", [P, T_BANKS, 4, P])
        self.ps_y = s.psum("ps_y", [P, TG])
        sem = s.sem
        self.raw_loaded, self.split_high, self.split_low = sem("raw_loaded"), sem("split_high"), sem("split_low")
        self.scores_done = sem("scores_done")
        self.scores_used = sem("scores_used")
        self.turn_done = sem("turn_done")
        self.high_done = sem("high_done")
        self.low_done = sem("low_done")
        self.unit_used = sem("unit_used")
        self.y_low_made = sem("y_low_made")
        self.y_summed = sem("y_summed")
        self.y_stored = sem("y_stored")

    def scores(self, n):
        cols = self.table[n][2]
        return self.ps_s[:, n % S_BANKS, 0:cols.stop - cols.start]

    def place(self, n):
        cols = self.table[n][2]
        return slice(512 - (cols.stop - cols.start), 512)

    def unit(self, group, j):
        return sum(g + 1 for g in range(group)) + j

    def turned(self, n, halves):
        qb, j, cols = self.table[n]
        tile = self.unit(qb // 4, j) % UNIT_RING * 4
        return halves[:, tile:tile + (cols.stop - cols.start) // P, qb % 4 * P:qb % 4 * P + P]

    def late_tensor(self, pe, weights, weights_made, credit, H, a, k, begun):
        late = due(late_chunk(LATE), H, a, k, begun)
        if late:
            h, _, n = late
            pe.wait_ge(weights_made, h * CHUNKS + n + 1 + credit)
            pe.wait_ge(self.low_done, h * CHUNKS + n + 1)
            at = self.place(n)
            for b in range((at.stop - at.start) // P):
                mm = pe.transpose(self.ps_t[:, n % T_BANKS, b, :], weights[:, n % self.ring, at.start + b * P:at.start + b * P + P], self.ident[:, :])
            mm.then_inc(self.turn_done, 1)
        piece = due(PIECE_AT.get, H, a, k, begun)
        if piece:
            h, ha, (group, tiles) = piece
            if tiles.start == 0:
                pe.wait_ge(self.low_done, h * CHUNKS + chunk_base(4 * group + 4) + T_BANKS)
                pe.wait_ge(self.y_summed, h * NG + group + 1)
                if group == 0:
                    pe.wait_ge(self.split_low, h * 3 + 3)
            for i in tiles:
                j, b = i // 4, i % 4
                kb = self.order(4 * group + 3)[j].start // P + b
                lo = max(0, kb - 4 * group) * P
                tile = self.unit(group, j) % UNIT_RING * 4 + b
                pe.matmul(self.ps_y[:, lo:TG], self.v_halves[ha][:, kb, :], self.turned_high[:, tile, lo:TG], start=i == 0, stop=False)
                mm = pe.matmul(self.ps_y[:, lo:TG], self.v_halves[ha][:, kb, :], self.turned_low[:, tile, lo:TG], start=False, stop=i == 4 * group + 3)
            if tiles.stop % 4 == 0:
                mm.then_inc(self.unit_used, 1)

    def late_scalar(self, act, H, a, k, begun):
        nc = self.nc
        late = due(late_chunk(LATE), H, a, k, begun)
        if late:
            h, _, n = late
            qb, j, _ = self.table[n]
            act.wait_ge(self.turn_done, h * CHUNKS + n + 1)
            if qb % 4 == 0:
                act.wait_ge(self.unit_used, h * UNITS + self.unit(qb // 4, j) + 1)
            blocks = self.turned(n, self.turned_high)
            nc.scalar.activation(blocks, self.ps_t[:, n % T_BANKS, 0:blocks.shape[1], :], ACT.Copy).then_inc(self.high_done, 1)
        sum_ = due(Y_AT.get, H, a, k, begun)
        if sum_:
            h, _, group = sum_
            act.wait_ge(self.unit_used, h * UNITS + self.unit(group + 1, 0) + UNIT_RING)
            act.wait_ge(self.y_summed, h * NG + group + 1)
            nc.scalar.activation(self.y_low[:, :], self.ps_y[HD:P, :], ACT.Copy).then_inc(self.y_low_made, 1)

    def late_vector(self, dve, y, y_free, H, a, k, begun):
        nc = self.nc
        late = due(late_chunk(LATE), H, a, k, begun)
        if late:
            h, _, n = late
            dve.wait_ge(self.high_done, h * CHUNKS + n + 1)
            high = self.turned(n, self.turned_high)
            nc.vector.tensor_tensor(self.turned(n, self.turned_low), self.ps_t[:, n % T_BANKS, 0:high.shape[1], :], high.bitcast(F32), ALU.subtract).then_inc(self.low_done, 1)
        sum_ = due(Y_AT.get, H, a, k, begun)
        if sum_:
            h, _, group = sum_
            dve.wait_ge(self.y_low_made, h * NG + group + 1)
            y_free(h, group)
            nc.vector.tensor_tensor(y[:, :], self.ps_y[0:HD, :], self.y_low[:, :], ALU.add).then_inc(self.y_summed, 1)

    def load_values(self, sp, H, name):
        source = self.W[name].rearrange("(b p) n -> p b n", p=P)
        sp.dma_start(self.v_raw[:, :, :], source[:, :, bass.ds(H * HD, HD)]).then_inc(self.raw_loaded, 16)

    def store(self, sp, y_made, credit, H, group):
        sp.wait_ge(y_made, H * NG + group + 1 + credit)
        sp.dma_start(self.W["yt"][bass.ds(self.row0 + H * HD, HD), group * TG:(group + 1) * TG], self.y[:, :]).then_inc(self.y_stored, 16)


def phase_stick_breaking(nc, T, W, R):
    RING = 8
    SHORT = 5
    KEEP_LATE = 1
    with Scope(nc, "s") as s:
        side = AttentionSide(nc, s, W, 0, lambda qb: chunks_of(qb)[::-1], RING)
        side.ident = R["ident"]
        q_raw = s.sb("q_raw", [P, SEQ])
        k_raw = s.sb("k_raw", [P, SEQ])
        q_stack = [s.sb(f"q_stack{a}", [P, SEQ], F32R) for a in range(2)]
        k_high = [s.sb(f"k_high{a}", [P, SEQ], F32R) for a in range(2)]
        k_low = [s.sb(f"k_low{a}", [P, SEQ], F32R) for a in range(2)]
        sig = s.sb("sig", [P, SHORT, 512])
        weights = s.sb("weights", [P, RING, 513])
        later = s.sb("later", [P, SHORT, 513])
        sig_made = side.scores_used
        weights_made = s.sem("weights_made")
        keep_made, scanned, ones_set = s.sem("keep_made"), s.sem("scanned"), s.sem("ones_set")
        block = s.block()

        @block.sync
        def _(sp):
            sp.sem_inc(side.y_stored, 16)

            def load(H):
                for half in range(2):
                    sp.dma_start(q_raw[half * HD:(half + 1) * HD, :], W["qk"][bass.ds(H * HD, HD), :]).then_inc(side.raw_loaded, 16)
                    sp.dma_start(k_raw[half * HD:(half + 1) * HD, :], W["qk"][bass.ds(SBW + H * HD, HD), :]).then_inc(side.raw_loaded, 16)
                side.load_values(sp, H, "v")

            def head(H, begun, more):
                if more:
                    sp.wait_ge(side.split_low, H * 3 + 3)
                    load(H + 1)
                if begun:
                    side.store(sp, side.y_summed, 1, H - 1, NG - 1)
                for group in range(NG - 1):
                    side.store(sp, side.y_summed, 1, H, group)

            load(0)
            head(0, False, True)
            with sp.Fori(1, HEADS - 1) as H:
                head(H, True, True)
            head(HEADS - 1, True, False)
            side.store(sp, side.y_summed, 1, HEADS - 1, NG - 1)
            sp.wait_ge(side.y_stored, 16 + 16 * HEADS * NG)

        @block.scalar
        def _(act):
            def slot(H, a, k, begun, more):
                side.late_scalar(act, H, a, k, begun)
                if k < CHUNKS:
                    act.wait_ge(side.scores_done, H * CHUNKS + k + 1)
                    act.wait_ge(weights_made, H * CHUNKS + k + 1)
                    nc.scalar.activation(sig[:, k % SHORT, side.place(k)], side.scores(k), ACT.Sigmoid, scale=SB_SCALE).then_inc(sig_made, 1)
                keep = due(late_chunk(KEEP_LATE), H, a, k, begun)
                if keep:
                    h, _, n = keep
                    act.wait_ge(sig_made, h * CHUNKS + n + 1 + S_BANKS)
                    nc.scalar.activation(weights[:, n % RING, side.place(n)], sig[:, n % SHORT, side.place(n)], ACT.Copy, scale=-1.0, bias=1.0).then_inc(keep_made, 1)

            act.sem_inc(side.scores_used, S_BANKS)
            over_heads(act, slot)

        @block.vector
        def _(dve):
            def split_high(H, a, part):
                if part == 0:
                    dve.wait_ge(side.raw_loaded, H * 80 + 80)
                to, raw = ((q_stack[a][:, :], q_raw[:, :]), (k_high[a][:, :], k_raw[:, :]), (side.v_halves[a][:, :, 0:HD], side.v_raw[:, :, :]))[part]
                nc.vector.tensor_copy(to, raw).then_inc(side.split_high, 1)

            def split_low(H, a, part):
                dve.wait_ge(side.split_high, H * 3 + part + 1)
                low, raw, high = ((q_stack[a][HD:P, :], q_raw[HD:P, :], q_stack[a][HD:P, :]), (k_low[a][:, :], k_raw[:, :], k_high[a][:, :]),
                                  (side.v_halves[a][:, :, HD:P], side.v_raw[:, :, :], side.v_halves[a][:, :, 0:HD]))[part]
                nc.vector.tensor_tensor(low, raw, high.bitcast(F32), ALU.subtract).then_inc(side.split_low, 1)

            def y_free(h, group):
                dve.wait_ge(side.y_stored, h * (16 * NG) + group * 16 + 16)

            def slot(H, a, k, begun, more):
                side.late_vector(dve, side.y, y_free, H, a, k, begun)
                keep = due(late_chunk(KEEP_LATE), H, a, k, begun)
                if keep:
                    h, _, n = keep
                    dve.wait_ge(keep_made, h * CHUNKS + n + 1)
                    if side.table[n][1]:
                        dve.wait_ge(scanned, h * CHUNKS + n)
                        start_at = side.place(n - 1).start
                        start = later[:, (n - 1) % SHORT, start_at:start_at + 1]
                    else:
                        start = 1.0
                    first = side.place(n).start
                    back = slice(512, first - 1 if first else None, -1)
                    keeps = weights[:, n % RING, back]
                    nc.vector.tensor_tensor_scan(later[:, n % SHORT, back], keeps, keeps, start, ALU.mult, ALU.bypass).then_inc(scanned, 1)
                if more and k in SPLIT_AT:
                    split_high(H + 1, 1 - a, SPLIT_AT[k])
                if more and k in SPLIT_LOW_AT:
                    split_low(H + 1, 1 - a, SPLIT_LOW_AT[k])

            nc.vector.memset(weights[:, :, 512:513], 1.0).then_inc(ones_set, 1)
            dve.wait_ge(ones_set, 1)
            dve.sem_inc(side.low_done, T_BANKS)
            dve.sem_inc(side.y_summed, 1)
            for part in range(3):
                split_high(0, 0, part)
                split_low(0, 0, part)
            over_heads(dve, slot)

        @block.gpsimd
        def _(pool):
            def slot(H, a, k, begun, more):
                if k < CHUNKS:
                    pool.wait_ge(scanned, H * CHUNKS + k + 1)
                    at = side.place(k)
                    nc.gpsimd.tensor_tensor(weights[:, k % RING, at], sig[:, k % SHORT, at], later[:, k % SHORT, at.start + 1:513], ALU.mult).then_inc(weights_made, 1)
            pool.sem_inc(weights_made, SHORT)
            over_heads(pool, slot)

        @block.tensor
        def _(pe):
            def slot(H, a, k, begun, more):
                if k == 0:
                    pe.wait_ge(side.split_low, H * 3 + 2)
                if k < CHUNKS:
                    qb, j, cols = side.table[k]
                    queries = q_stack[a][:, qb * P:(qb + 1) * P]
                    pe.wait_ge(side.scores_used, H * CHUNKS + k + 1)
                    out = side.scores(k)
                    pe.matmul(out, queries, k_high[a][:, cols], start=True, stop=False)
                    mm = pe.matmul(out, queries, k_low[a][:, cols], start=False, stop=(j > 0))
                    if j == 0:
                        mm = pe.matmul(out[:, cols.stop - cols.start - P:], R["ident_r"][:, :], R["strict"][:, :], start=False, stop=True)
                    mm.then_inc(side.scores_done, 1)
                side.late_tensor(pe, weights, weights_made, SHORT, H, a, k, begun)

            pe.sem_inc(side.unit_used, UNIT_RING)
            over_heads(pe, slot)


def phase_latent_attention(nc, T, W, R):
    EXP_LATE = 4
    RING = 5
    with Scope(nc, "l") as s:
        side = AttentionSide(nc, s, W, SBW, chunks_of, RING)
        side.ident = R["ident"]
        q_raw = s.sb("q_raw", [QK, SEQ])
        k_raw = s.sb("k_raw", [QK, SEQ])
        q_high, q_low, k_high, k_low = ([s.sb(f"{n}{a}", [QK, SEQ], F32R) for a in range(2)] for n in ("q_high", "q_low", "k_high", "k_low"))
        weights = s.sb("weights", [P, RING, 512])
        chunk_max = s.sb("chunk_max", [P, 4])
        row_max = s.sb("row_max", [P, 1])
        bias = s.sb("bias", [P, TILES])
        sums = s.sb("sums", [P, TILES, 4])
        total = s.sb("total", [P, 4])
        inverse = s.sb("inverse", [P, TILES])
        inverse_rows = s.sb("inverse_rows", [HD, 2, TG])
        y_sum = s.sb("y_sum", [HD, TG])
        exp_made = side.scores_used
        bias_made, total_made, inverse_made, dve_own = s.sem("bias_made"), s.sem("total_made"), s.sem("inverse_made"), s.sem("dve_own")
        inverse_stored, sums_cleared = s.sem("inverse_stored"), s.sem("sums_cleared")
        inverse_loaded = [s.sem(f"inverse_loaded{i}") for i in range(2)]
        y_made = s.sem("y_made")
        block = s.block()
        OWN = CHUNKS + 2 * TILES

        @block.sync
        def _(sp):
            sp.sem_inc(side.y_stored, 16)

            def load(H):
                lq = W["lq"].rearrange("h r t -> (h r) t")
                sp.dma_start(q_raw[:, :], lq[bass.ds(H * QK, QK), :]).then_inc(side.raw_loaded, 16)
                sp.dma_start(k_raw[0:HD, :], W["lk"][bass.ds(H * HD, HD), :]).then_inc(side.raw_loaded, 16)
                sp.dma_start(k_raw[HD:QK, :], W["lkr"]).then_inc(side.raw_loaded, 16)
                side.load_values(sp, H, "lv")

            def turn_inverses(H, group):
                sp.wait_ge(inverse_made, H * NG + group + 1)
                rows = W["inverse"][bass.ds(H, 1), group * TG:(group + 1) * TG]
                sp.dma_start(rows.rearrange("a (b p) -> p (a b)", p=P), inverse[:, 4 * group:4 * group + 4], allow_slow_non_contiguous=True).then_inc(inverse_stored, 16)
                sp.wait_ge(inverse_stored, H * (16 * NG) + group * 16 + 16)
                sp.dma_start(inverse_rows[:, group % 2, :], rows.to_broadcast([HD, TG])).then_inc(inverse_loaded[group % 2], 16)

            def head(H, begun, more):
                if more:
                    sp.wait_ge(side.split_low, H * 3 + 3)
                    load(H + 1)
                if begun:
                    turn_inverses(H - 1, 3)
                turn_inverses(H, 0)
                if begun:
                    side.store(sp, y_made, 1, H - 1, 3)
                turn_inverses(H, 1)
                side.store(sp, y_made, 1, H, 0)
                side.store(sp, y_made, 1, H, 1)
                turn_inverses(H, 2)
                side.store(sp, y_made, 1, H, 2)

            load(0)
            head(0, False, True)
            with sp.Fori(1, HEADS - 1) as H:
                head(H, True, True)
            head(HEADS - 1, True, False)
            turn_inverses(HEADS - 1, 3)
            side.store(sp, y_made, 1, HEADS - 1, 3)
            sp.wait_ge(side.y_stored, 16 + 16 * HEADS * NG)

        @block.scalar
        def _(act):
            def split(H, a, part):
                if part == 0:
                    act.wait_ge(side.raw_loaded, H * 64 + 64)
                to, raw = ((q_high[a][:, :], q_raw[:, :]), (k_high[a][:, :], k_raw[:, :]), (side.v_halves[a][:, :, 0:HD], side.v_raw[:, :, :]))[part]
                nc.scalar.activation(to, raw, ACT.Copy).then_inc(side.split_high, 1)

            def slot(H, a, k, begun, more):
                now = due(late_chunk(EXP_LATE), H, a, k, begun)
                if now:
                    h, _, n = now
                    qb, j, _ = side.table[n]
                    if j == 0:
                        act.wait_ge(bias_made, h * TILES + qb + 1)
                    nc.scalar.activation(weights[:, n % RING, side.place(n)], side.scores(n), ACT.Exp,
                                         bias=bias[:, qb:qb + 1], scale=MLA_SCALE, accum_out=sums[:, qb, j:j + 1]).then_inc(exp_made, 1)
                side.late_scalar(act, H, a, k, begun)
                if more and k in SPLIT_AT:
                    split(H + 1, 1 - a, SPLIT_AT[k])

            act.sem_inc(side.scores_used, S_BANKS)
            for part in range(3):
                split(0, 0, part)
            over_heads(act, slot)

        @block.vector
        def _(dve):
            def own_count(H, qb):
                return H * OWN + chunk_base(qb) + 2 * qb

            def y_free(h, group):
                dve.wait_ge(y_made, h * NG + group + 1)

            group_end = {chunk_base(4 * group + 4) + EXP_LATE: group for group in range(NG)}

            def slot(H, a, k, begun, more):
                if k < CHUNKS:
                    qb, j, _ = side.table[k]
                    length = len(chunks_of(qb))
                    if j == 0 and (begun or qb):
                        dve.wait_ge(dve_own, own_count(H, qb))
                    dve.wait_ge(side.scores_done, H * CHUNKS + k + 1)
                    nc.vector.reduce_max(chunk_max[:, j:j + 1], side.scores(k), mybir.AxisListType.X).then_inc(dve_own, 1)
                    if j == length - 1:
                        dve.wait_ge(dve_own, own_count(H, qb) + length)
                        nc.vector.reduce_max(row_max[:, :], chunk_max[:, 0:length], mybir.AxisListType.X).then_inc(dve_own, 1)
                        dve.wait_ge(dve_own, own_count(H, qb) + length + 1)
                        nc.vector.tensor_scalar(bias[:, qb:qb + 1], row_max[:, :], -MLA_SCALE, None, ALU.mult).then_inc(bias_made, 1)
                        dve.wait_ge(bias_made, H * TILES + qb + 1)
                        dve.sem_inc(dve_own, 1)
                side.late_vector(dve, y_sum, y_free, H, a, k, begun)
                done = due(group_end.get, H, a, k, begun)
                if done:
                    h, _, group = done
                    rows = slice(4 * group, 4 * group + 4)
                    dve.wait_ge(exp_made, h * CHUNKS + chunk_base(4 * group + 4) + S_BANKS)
                    nc.vector.reduce_sum(total[:, :], sums[:, rows, :], mybir.AxisListType.X).then_inc(total_made, 1)
                    dve.wait_ge(total_made, h * NG + group + 1)
                    nc.vector.reciprocal(inverse[:, rows], total[:, :]).then_inc(inverse_made, 1)

            nc.vector.memset(sums[:, :, :], 0.0).then_inc(sums_cleared, 1)
            dve.wait_ge(sums_cleared, 1)
            dve.sem_inc(side.low_done, T_BANKS)
            dve.sem_inc(side.y_summed, 1)
            over_heads(dve, slot)

        @block.gpsimd
        def _(pool):
            def split(H, a, part):
                pool.wait_ge(side.split_high, H * 3 + part + 1)
                low, raw, high = ((q_low[a][:, :], q_raw[:, :], q_high[a][:, :]), (k_low[a][:, :], k_raw[:, :], k_high[a][:, :]),
                                  (side.v_halves[a][:, :, HD:P], side.v_raw[:, :, :], side.v_halves[a][:, :, 0:HD]))[part]
                nc.gpsimd.tensor_tensor(low, raw, high.bitcast(F32), ALU.subtract).then_inc(side.split_low, 1)

            def slot(H, a, k, begun, more):
                sum_ = due(Y_AT.get, H, a, k, begun)
                if sum_:
                    h, _, group = sum_
                    pool.wait_ge(side.y_summed, h * NG + group + 2)
                    pool.wait_ge(inverse_loaded[group % 2], h * 32 + group // 2 * 16 + 16)
                    pool.wait_ge(side.y_stored, h * (16 * NG) + group * 16 + 16)
                    nc.gpsimd.tensor_tensor(side.y[:, :], y_sum[:, :], inverse_rows[:, group % 2, :], ALU.mult).then_inc(y_made, 1)
                if more and k in SPLIT_LOW_AT:
                    split(H + 1, 1 - a, SPLIT_LOW_AT[k])

            pool.sem_inc(y_made, 1)
            for part in range(3):
                split(0, 0, part)
            over_heads(pool, slot)

        @block.tensor
        def _(pe):
            def slot(H, a, k, begun, more):
                if k == 0:
                    pe.wait_ge(side.split_low, H * 3 + 2)
                if k < CHUNKS:
                    qb, j, cols = side.table[k]
                    rows = slice(qb * P, (qb + 1) * P)
                    pe.wait_ge(side.scores_used, H * CHUNKS + k + 1)
                    out = side.scores(k)
                    width = cols.stop - cols.start
                    diagonal = cols.stop == (qb + 1) * P
                    mm = products(pe, out, q_high[a][:, rows], q_low[a][:, rows], k_high[a][:, cols], k_low[a][:, cols], True, not diagonal)
                    if diagonal:
                        mm = pe.matmul(out[:, width - 64:width], R["ident_r"][:, :], R["halves"][:, :], start=False, stop=True)
                    mm.then_inc(side.scores_done, 1)
                side.late_tensor(pe, weights, exp_made, S_BANKS, H, a, k, begun)

            pe.sem_inc(side.unit_used, UNIT_RING)
            over_heads(pe, slot)

def load_rows(sp, s_loaded, W, T, gates, gate, gain, bias):
    sp.dma_start(gates[:, 0, :], W["gate"][gate:gate + 1, :].to_broadcast([P, D])).then_inc(s_loaded, 16)
    sp.dma_start(gates[:, 1, :], T[gain].to_broadcast([P, D])).then_inc(s_loaded, 16)
    sp.dma_start(gates[:, 2, :], T[bias].to_broadcast([P, D])).then_inc(s_loaded, 16)


def phase_output_projection(nc, T, W, R):
    PAIRS = TILES // 2
    PIECES = 4
    with Scope(nc, "o") as s:
        wraw = s.sb("wraw", [P, 2, 2, D])
        wh = s.sb("wh", [P, KD, D], F32R)
        wl = s.sb("wl", [P, KD, D], F32R)
        yraw = s.sb("yraw", [P, 2, KD, P])
        yh = s.sb("yh", [P, 2, KD, P], F32R)
        yl = s.sb("yl", [P, 2, KD, P], F32R)
        rows = s.sb("rows", [P, 3, D])
        xn = s.sb("xn", [P, 2, D])
        z = s.sb("z", [P, 2, D])
        xhat = s.sb("xhat", [P, D])
        xg = s.sb("xg", [P, 2, D])
        x1 = s.sb("x1", [P, 2, D])
        h2 = s.sb("h2", [P, 2, KD, P])
        stats = s.sb("stats", [P, 2, 6])
        moments = s.sb("moments", [P, 2, 2])
        var, root, rstd, tmp = (s.sb(n, [P, 2]) for n in ("var", "root", "rstd", "tmp"))
        ps = s.psum("ps", [P, 2, D])
        ps_t = s.psum("ps_t", [P, 2, KD, P])
        rows_loaded = s.sem("rows_loaded")
        w_loaded = [s.sem(f"w_loaded{i}") for i in range(2)]
        y_loaded = [s.sem(f"y_loaded{i}") for i in range(2)]
        xn_loaded = [s.sem(f"xn_loaded{i}") for i in range(2)]
        wh_made, wl_made, yh_made = s.sem("wh_made"), s.sem("wl_made"), s.sem("yh_made")
        yl_made = s.sem("yl_made")
        mixed = s.sem("mixed")
        gated = s.sem("gated")
        summed = s.sem("summed")
        var_made, root_made, xg_made = s.sem("var_made"), s.sem("root_made"), s.sem("xg_made")
        xg_free = s.sem("xg_free")
        x1_made, x1_turned, h2_made = s.sem("x1_made"), s.sem("x1_turned"), s.sem("h2_made")
        x1_free = s.sem("x1_free")
        x1_stored = [s.sem(f"x1_stored{i}") for i in range(2)]
        h2_stored = [s.sem(f"h2_stored{i}") for i in range(2)]
        dve_own, spare = s.sem("dve_own"), s.sem("spare")
        block = s.block()
        OWN = 2 * 1 + 2 * 2 + 4 + 2 * 2

        @block.sync
        def _(sp):
            def load_tile(i, a):
                tokens = bass.ds((i * 2 + a) * P, P)
                sp.wait_ge(yl_made, i * 2 + a + 1)
                sp.dma_start(yraw[:, a, :, :], W["yt"].rearrange("(k p) t -> p k t", p=P)[:, :, tokens]).then_inc(y_loaded[a], 16)
                sp.wait_ge(summed, i * 2 + a + 1)
                sp.dma_start(xn[:, a, :], W["xn"][tokens, :]).then_inc(xn_loaded[a], 16)

            for m in range(PIECES):
                if m >= 2:
                    sp.wait_ge(wl_made, m - 1)
                sp.dma_start(wraw[:, m % 2, :, :], T["w_o"][0, m * 256:(m + 1) * 256, :].rearrange("(k p) n -> p k n", p=P)).then_inc(w_loaded[m % 2], 16)
                if m == 0:
                    load_tile(0, 0)
            load_tile(0, 1)
            load_rows(sp, rows_loaded, W, T, rows, 0, "ln1_g", "ln1_b")
            with sp.Fori(1, PAIRS) as i:
                for a in range(2):
                    load_tile(i, a)

        @block.scalar
        def _(act):
            act.sem_inc(x1_free, 2)
            for a in range(2):
                act.sem_inc(h2_stored[a], 16)

            def high(i, a):
                act.wait_ge(y_loaded[a], i * 16 + 16)
                nc.scalar.activation(yh[:, a, :, :], yraw[:, a, :, :], ACT.Copy).then_inc(yh_made, 1)

            def late(i):
                for a in range(2):
                    act.wait_ge(x1_turned, i * 2 + a + 1)
                    act.dma_start(W["x1"][bass.ds((i * 2 + a) * P, P), :], x1[:, a, :]).then_inc(x1_stored[a], 16)
                    act.wait_ge(h2_stored[a], i * 16 + 16)
                    for k in range(KD):
                        last = nc.scalar.activation(h2[:, a, k, :], ps_t[:, a, k, :], ACT.Identity, bias=R["shift"][:, 1, k:k + 1], scale=R["scale"][:, 1, k:k + 1])
                    last.then_inc(h2_made, 1)
                    act.wait_ge(h2_made, i * 2 + a + 1)
                    act.dma_start(W["h2t"].rearrange("(k p) t -> p k t", p=P)[:, :, bass.ds((i * 2 + a) * P, P)], h2[:, a, :, :]).then_inc(h2_stored[a], 16)
                    act.wait_ge(x1_stored[a], i * 16 + 16)
                    act.sem_inc(x1_free, 1)

            def pair(i, begun, more):
                for a in range(2):
                    if more:
                        act.wait_ge(mixed, i * 2 + a + 1)
                        high(i + 1, a)
                act.wait_ge(var_made, i + 1)
                nc.scalar.activation(root[:, :], var[:, :], ACT.Sqrt).then_inc(root_made, 1)
                if begun:
                    late(i - 1)

            for m in range(PIECES):
                act.wait_ge(w_loaded[m % 2], 16 * (m // 2 + 1))
                nc.scalar.activation(wh[:, 2 * m:2 * m + 2, :], wraw[:, m % 2, :, :], ACT.Copy).then_inc(wh_made, 1)
                if m == 0:
                    high(0, 0)
            high(0, 1)
            pair(0, False, True)
            with act.Fori(1, PAIRS - 1) as i:
                pair(i, True, True)
            pair(PAIRS - 1, True, False)
            late(PAIRS - 1)
            for a in range(2):
                act.wait_ge(h2_stored[a], 16 + 16 * PAIRS)

        @block.vector
        def _(dve):
            dve.sem_inc(gated, 2)
            dve.sem_inc(summed, 2)
            dve.sem_inc(yl_made, 2)

            def low(i, a):
                dve.wait_ge(yh_made, i * 2 + a + 1)
                nc.vector.tensor_tensor(yl[:, a, :, :], yraw[:, a, :, :], yh[:, a, :, :].bitcast(F32), ALU.subtract).then_inc(yl_made, 1)

            def pair(i, more):
                own = Chain(dve, dve_own, i * OWN, spare)
                for a in range(2):
                    dve.wait_ge(mixed, i * 2 + a + 1)
                    nc.vector.tensor_tensor(z[:, a, :], ps[:, a, :], rows[:, 0, :], ALU.mult).then_inc(gated, 1)
                    if more:
                        low(i + 1, a)
                    dve.wait_ge(gated, i * 2 + a + 3)
                    dve.wait_ge(xn_loaded[a], i * 16 + 16)
                    own.step(nc.vector.scalar_tensor_tensor(out=z[:, a, :], in0=xn[:, a, :], scalar=ALPHA, in1=z[:, a, :], op0=ALU.mult, op1=ALU.add))
                    dve.sem_inc(summed, 1)
                    layer_norm_moments(nc, own, z[:, a, :], stats, moments[:, a, :])
                nc.vector.tensor_scalar(var[:, :], moments[:, :, 1], LN_EPS, None, ALU.add).then_inc(var_made, 1)
                dve.wait_ge(root_made, i + 1)
                refine_rsqrt(nc, own, rstd[:, :], var[:, :], root[:, :], tmp[:, :])
                for a in range(2):
                    own.step(nc.vector.tensor_scalar(xhat[:, :], z[:, a, :], moments[:, a, 0:1], rstd[:, a:a + 1], ALU.subtract, ALU.mult))
                    dve.wait_ge(xg_free, i * 2 + a + 1)
                    own.step(nc.vector.tensor_tensor(xg[:, a, :], xhat[:, :], rows[:, 1, :], ALU.mult))
                    dve.sem_inc(xg_made, 1)
                assert own.n == OWN

            for m in range(PIECES):
                dve.wait_ge(wh_made, m + 1)
                nc.vector.tensor_tensor(wl[:, 2 * m:2 * m + 2, :], wraw[:, m % 2, :, :], wh[:, 2 * m:2 * m + 2, :].bitcast(F32), ALU.subtract).then_inc(wl_made, 1)
                if m == 0:
                    low(0, 0)
            low(0, 1)
            dve.wait_ge(rows_loaded, 48)
            with dve.Fori(0, PAIRS - 1) as i:
                pair(i, True)
            pair(PAIRS - 1, False)

        @block.gpsimd
        def _(pool):
            pool.sem_inc(xg_free, 2)
            pool.wait_ge(rows_loaded, 48)
            with pool.Fori(0, PAIRS) as i:
                for a in range(2):
                    pool.wait_ge(xg_made, i * 2 + a + 1)
                    pool.wait_ge(x1_free, i * 2 + a + 1)
                    nc.gpsimd.tensor_tensor(x1[:, a, :], xg[:, a, :], rows[:, 2, :], ALU.add).then_inc(x1_made, 1)
                    pool.wait_ge(x1_made, i * 2 + a + 1)
                    pool.sem_inc(xg_free, 1)

        @block.tensor
        def _(pe):
            def late(i):
                for a in range(2):
                    pe.wait_ge(x1_made, i * 2 + a + 1)
                    for k in range(KD):
                        mm = pe.transpose(ps_t[:, a, k, :], x1[:, a, k * P:(k + 1) * P], R["ident"][:, :])
                    mm.then_inc(x1_turned, 1)

            def pair(i, begun, first):
                for a in range(2):
                    pe.wait_ge(yl_made, i * 2 + a + 3)
                    pe.wait_ge(gated, i * 2 + a + 1)
                    for half in range(2):
                        cols = slice(half * 512, half * 512 + 512)
                        for k in range(KD):
                            if first and a == 0 and half == 0 and k % 2 == 0:
                                pe.wait_ge(wl_made, k // 2 + 1)
                            mm = products(pe, ps[:, a, cols], yh[:, a, k, :], yl[:, a, k, :], wh[:, k, cols], wl[:, k, cols], k == 0, k == KD - 1)
                    mm.then_inc(mixed, 1)
                if begun:
                    late(i - 1)
            pair(0, False, True)
            with pe.Fori(1, PAIRS) as i:
                pair(i, True, False)
            late(PAIRS - 1)


def phase_mlp(nc, T, W, R):
    ROUNDS = D_FF // 512
    H_SLOTS = 4
    with Scope(nc, "f") as s:
        rows = s.sb("rows", [P, 3, D])
        hraw = s.sb("hraw", [P, H_SLOTS, TG])
        hh = s.sb("hh", [P, KD, TG], F32R)
        hl = s.sb("hl", [P, KD, TG], F32R)
        up_raw = s.sb("up_raw", [P, 2, KD, 256])
        down_raw = s.sb("down_raw", [P, 2, 2, D])
        uph = s.sb("uph", [P, 2, KD, 256], F32R)
        upl = s.sb("upl", [P, 2, KD, 256], F32R)
        downh = s.sb("downh", [P, 2, 2, D], F32R)
        downl = s.sb("downl", [P, 2, 2, D], F32R)
        relu = s.sb("relu", [P, TG])
        act2 = s.sb("act2", [P, 2, TG])
        ah = s.sb("ah", [P, 4, TG], F32R)
        al = s.sb("al", [P, 4, TG], F32R)
        total = s.sb("total", [P, 4, D])
        z = s.sb("z", [P, 4, D])
        stats = s.sb("stats", [P, 2, 6])
        moments = s.sb("moments", [P, 4, 2])
        var, root, rstd, tmp = (s.sb(n, [P, 4]) for n in ("var", "root", "rstd", "tmp"))
        ps_u = s.psum("ps_u", [P, 4, TG])
        ps_d = s.psum("ps_d", [P, 2, D])
        rows_loaded = s.sem("rows_loaded")
        h_loaded = [s.sem(f"h_loaded{i}") for i in range(H_SLOTS)]
        up_loaded = [s.sem(f"up_loaded{i}") for i in range(2)]
        down_loaded = [s.sem(f"down_loaded{i}") for i in range(2)]
        z_loaded = s.sem("z_loaded")
        hh_made = s.sem("hh_made")
        hl_made = s.sem("hl_made")
        uph_made, downh_made = s.sem("uph_made"), s.sem("downh_made")
        upl_made, downl_made = s.sem("upl_made"), s.sem("downl_made")
        up_done = s.sem("up_done")
        relu_made, act2_made, ah_made = s.sem("relu_made"), s.sem("act2_made"), s.sem("ah_made")
        al_made = s.sem("al_made")
        down_done = s.sem("down_done")
        added = s.sem("added")
        var_made, root_made, xg_made, y_made = s.sem("var_made"), s.sem("root_made"), s.sem("xg_made"), s.sem("y_made")
        y_stored = s.sem("y_stored")
        dve_own, spare = s.sem("dve_own"), s.sem("spare")
        block = s.block()
        OWN_MOMENTS, OWN_NORM = 4 * 4, 4 + 4

        @block.sync
        def _(sp):
            sp.sem_inc(y_stored, 64)

            def load_round(g, j):
                for a in range(2):
                    sp.wait_ge(upl_made, g * (2 * ROUNDS) + j * 2 + a + 1)
                    sp.dma_start(up_raw[:, a, :, :], T["w_up"][0].rearrange("(k p) n -> p k n", p=P)[:, :, bass.ds(j * 512 + a * 256, 256)]).then_inc(up_loaded[a], 16)
                for a in range(2):
                    sp.wait_ge(downl_made, g * (2 * ROUNDS) + j * 2 + a + 1)
                    sp.dma_start(down_raw[:, a, :, :], T["w_down"][0, bass.ds(j * 512 + a * 256, 256), :].rearrange("(k p) n -> p k n", p=P)).then_inc(down_loaded[a], 16)

            def store(g):
                for t in range(4):
                    sp.wait_ge(y_made, g * 4 + t + 1)
                    sp.dma_start(W["out"][bass.ds(g * TG + t * P, P), :], z[:, t, :]).then_inc(y_stored, 16)

            def group(g, begun):
                for k in range(KD):
                    sp.wait_ge(hl_made, g * KD + k + 1)
                    sp.dma_start(hraw[:, k % H_SLOTS, :], W["h2t"][k * P:(k + 1) * P, bass.ds(g * TG, TG)]).then_inc(h_loaded[k % H_SLOTS], 16)
                with sp.Fori(0, 3) as j:
                    load_round(g, j)
                if begun:
                    store(g - 1)
                else:
                    load_rows(sp, rows_loaded, W, T, rows, 1, "ln2_g", "ln2_b")
                with sp.Fori(3, ROUNDS) as j:
                    load_round(g, j)
                sp.wait_ge(y_stored, g * 64 + 64)
                sp.dma_start(z[:, :, :], W["x1"][bass.ds(g * TG, TG), :].rearrange("(t p) n -> p t n", p=P)).then_inc(z_loaded, 16)

            group(0, False)
            with sp.Fori(1, NG) as g:
                group(g, True)
            store(NG - 1)
            sp.wait_ge(y_stored, 64 + 64 * NG)

        @block.scalar
        def _(act):
            def take_root(g):
                act.wait_ge(var_made, g + 1)
                nc.scalar.activation(root[:, :], var[:, :], ACT.Sqrt).then_inc(root_made, 1)

            def round_(g, j):
                n = g * ROUNDS + j
                for a in range(2):
                    act.wait_ge(up_loaded[a], n * 16 + 16)
                    act.wait_ge(up_done, n * 4 + 2 * a + 2)
                    nc.scalar.activation(uph[:, a, :, :], up_raw[:, a, :, :], ACT.Copy).then_inc(uph_made, 1)
                for a in range(2):
                    act.wait_ge(down_loaded[a], n * 16 + 16)
                    act.wait_ge(down_done, n * 4 + 4)
                    nc.scalar.activation(downh[:, a, :, :], down_raw[:, a, :, :], ACT.Copy).then_inc(downh_made, 1)
                for f in range(4):
                    b = f % 2
                    act.wait_ge(up_done, n * 4 + f + 5)
                    act.wait_ge(al_made, n * 4 + f + 1)
                    nc.scalar.activation(relu[:, :], ps_u[:, f, :], ACT.Relu).then_inc(relu_made, 1)
                    act.wait_ge(relu_made, n * 4 + f + 1)
                    nc.scalar.activation(act2[:, b, :], relu[:, :], ACT.Square).then_inc(act2_made, 1)
                    act.wait_ge(act2_made, n * 4 + f + 1)
                    nc.scalar.activation(ah[:, f, :], act2[:, b, :], ACT.Copy).then_inc(ah_made, 1)

            def group(g, begun):
                for k in range(KD):
                    act.wait_ge(h_loaded[k % H_SLOTS], g * (16 * KD // H_SLOTS) + 16 * (k // H_SLOTS + 1))
                    if k == 0:
                        act.wait_ge(up_done, g * (4 * ROUNDS) + 4)
                    nc.scalar.activation(hh[:, k, :], hraw[:, k % H_SLOTS, :], ACT.Copy).then_inc(hh_made, 1)
                round_(g, 0)
                if begun:
                    take_root(g - 1)
                with act.Fori(1, ROUNDS) as j:
                    round_(g, j)

            group(0, False)
            with act.Fori(1, NG) as g:
                group(g, True)
            take_root(NG - 1)

        @block.gpsimd
        def _(pool):
            def low_of_round(g, j):
                n = g * ROUNDS + j
                for a in range(2):
                    pool.wait_ge(uph_made, n * 2 + a + 1)
                    nc.gpsimd.tensor_tensor(upl[:, a, :, :], up_raw[:, a, :, :], uph[:, a, :, :].bitcast(F32), ALU.subtract).then_inc(upl_made, 1)
                for a in range(2):
                    pool.wait_ge(downh_made, n * 2 + a + 1)
                    nc.gpsimd.tensor_tensor(downl[:, a, :, :], down_raw[:, a, :, :], downh[:, a, :, :].bitcast(F32), ALU.subtract).then_inc(downl_made, 1)

            def add_bias(g):
                for t in range(4):
                    pool.wait_ge(xg_made, g * 4 + t + 1)
                    nc.gpsimd.tensor_tensor(z[:, t, :], z[:, t, :], rows[:, 2, :], ALU.add).then_inc(y_made, 1)

            def group(g, begun):
                if begun:
                    for k in range(KD):
                        pool.wait_ge(hh_made, g * KD + k + 1)
                        nc.gpsimd.tensor_tensor(hl[:, k, :], hraw[:, k % H_SLOTS, :], hh[:, k, :].bitcast(F32), ALU.subtract).then_inc(hl_made, 1)
                for j in range(2):
                    low_of_round(g, j)
                if begun:
                    add_bias(g - 1)
                else:
                    pool.wait_ge(rows_loaded, 48)
                with pool.Fori(2, ROUNDS) as j:
                    low_of_round(g, j)

            pool.sem_inc(upl_made, 2)
            pool.sem_inc(downl_made, 2)
            group(0, False)
            with pool.Fori(1, NG) as g:
                group(g, True)
            add_bias(NG - 1)

        @block.vector
        def _(dve):
            def moments_chain(g):
                return Chain(dve, dve_own, g * (OWN_MOMENTS + OWN_NORM), spare)

            def tile_moments(g, t, own):
                if t == 0:
                    dve.wait_ge(z_loaded, g * 16 + 16)
                dve.wait_ge(added, (g + 1) * (4 * ROUNDS) + t - 1)
                own.step(nc.vector.tensor_tensor(total[:, t, :], total[:, t, :], rows[:, 0, :], ALU.mult))
                own.step(nc.vector.scalar_tensor_tensor(out=z[:, t, :], in0=z[:, t, :], scalar=ALPHA, in1=total[:, t, :], op0=ALU.mult, op1=ALU.add))
                layer_norm_moments(nc, own, z[:, t, :], stats, moments[:, t, :])
                if t == 3:
                    nc.vector.tensor_scalar(var[:, :], moments[:, :, 1], LN_EPS, None, ALU.add).then_inc(var_made, 1)
                    assert own.n == OWN_MOMENTS

            def normalise(g):
                own = Chain(dve, dve_own, g * (OWN_MOMENTS + OWN_NORM) + OWN_MOMENTS, spare)
                dve.wait_ge(root_made, g + 1)
                refine_rsqrt(nc, own, rstd[:, :], var[:, :], root[:, :], tmp[:, :])
                for t in range(4):
                    own.step(nc.vector.tensor_scalar(z[:, t, :], z[:, t, :], moments[:, t, 0:1], rstd[:, t:t + 1], ALU.subtract, ALU.mult))
                    nc.vector.tensor_tensor(z[:, t, :], z[:, t, :], rows[:, 1, :], ALU.mult).then_inc(xg_made, 1)
                assert own.n == OWN_NORM

            def round_(g, j, first, own=None):
                n = g * ROUNDS + j
                for f in range(4):
                    dve.wait_ge(ah_made, n * 4 + f + 1)
                    nc.vector.tensor_tensor(al[:, f, :], act2[:, f % 2, :], ah[:, f, :].bitcast(F32), ALU.subtract).then_inc(al_made, 1)
                for t in range(4):
                    dve.wait_ge(down_done, n * 4 + t + 5)
                    if first:
                        nc.vector.tensor_copy(total[:, t, :], ps_d[:, t % 2, :]).then_inc(added, 1)
                    else:
                        dve.wait_ge(added, n * 4 + 2)
                        nc.vector.tensor_tensor(total[:, t, :], ps_d[:, t % 2, :], total[:, t, :], ALU.add).then_inc(added, 1)
                    if own:
                        tile_moments(g, t, own)

            def group(g, begun, more):
                if begun:
                    own = moments_chain(g - 1)
                    for t in range(4):
                        tile_moments(g - 1, t, own)
                round_(g, 0, True)
                if begun:
                    normalise(g - 1)
                with dve.Fori(1, ROUNDS if more else ROUNDS - 1) as j:
                    round_(g, j, False)
                if not more:
                    round_(g, ROUNDS - 1, False, moments_chain(g))

            dve.sem_inc(al_made, 2)
            dve.sem_inc(added, 2)
            dve.sem_inc(hl_made, H_SLOTS)
            for k in range(KD):
                dve.wait_ge(hh_made, k + 1)
                nc.vector.tensor_tensor(hl[:, k, :], hraw[:, k % H_SLOTS, :], hh[:, k, :].bitcast(F32), ALU.subtract).then_inc(hl_made, 1)
            group(0, False, True)
            dve.wait_ge(rows_loaded, 48)
            with dve.Fori(1, NG - 1) as g:
                group(g, True, True)
            group(NG - 1, True, False)
            normalise(NG - 1)

        @block.tensor
        def _(pe):
            pe.sem_inc(up_done, 4)
            pe.sem_inc(down_done, 4)
            with pe.Fori(0, NG) as g:
                pe.wait_ge(hl_made, g * KD + KD + H_SLOTS)
                pe.sem_inc(spare, 1)
                with pe.Fori(0, ROUNDS) as j:
                    n = g * ROUNDS + j
                    for f in range(4):
                        a, cols = f // 2, slice((f % 2) * P, (f % 2) * P + P)
                        if f % 2 == 0:
                            pe.wait_ge(upl_made, n * 2 + a + 3)
                        for k in range(KD):
                            mm = products(pe, ps_u[:, f, :], uph[:, a, k, cols], upl[:, a, k, cols], hh[:, k, :], hl[:, k, :], k == 0, k == KD - 1)
                        mm.then_inc(up_done, 1)
                    for t in range(4):
                        tokens = slice(t * P, (t + 1) * P)
                        pe.wait_ge(added, n * 4 + t + 1)
                        for half in range(2):
                            cols = slice(half * 512, half * 512 + 512)
                            for f in range(4):
                                if t == 0 and half == 0:
                                    pe.wait_ge(al_made, n * 4 + f + 3)
                                    if f % 2 == 0:
                                        pe.wait_ge(downl_made, n * 2 + f // 2 + 3)
                                mm = products(pe, ps_d[:, t % 2, cols], ah[:, f, tokens], al[:, f, tokens], downh[:, f // 2, f % 2, cols], downl[:, f // 2, f % 2, cols], f == 0, f == 3)
                        mm.then_inc(down_done, 1)


PHASES = [phase_modulation, phase_projection, phase_stick_breaking, phase_latent_attention, phase_output_projection, phase_mlp]



def build(nc, T, out):
    W = {
        "xn": nc.dram_tensor("xn_scratch", (SEQ, D), F32).ap(),
        "xt": nc.dram_tensor("xt_scratch", (D, SEQ), F32).ap(),
        "qk": nc.dram_tensor("qk_scratch", (2 * SBW, SEQ), F32).ap(),
        "v": nc.dram_tensor("v_scratch", (SEQ, SBW), F32).ap(),
        "lq": nc.dram_tensor("lq_scratch", (HEADS, QK, SEQ), F32).ap(),
        "lk": nc.dram_tensor("lk_scratch", (HEADS * HD, SEQ), F32).ap(),
        "lkr": nc.dram_tensor("lkr_scratch", (ROPE, SEQ), F32).ap(),
        "lv": nc.dram_tensor("lv_scratch", (SEQ, HEADS * HD), F32).ap(),
        "yt": nc.dram_tensor("yt_scratch", (D, SEQ), F32).ap(),
        "inverse": nc.dram_tensor("inverse_scratch", (HEADS, SEQ), F32).ap(),
        "x1": nc.dram_tensor("x1_scratch", (SEQ, D), F32).ap(),
        "h2t": nc.dram_tensor("h2t_scratch", (D, SEQ), F32).ap(),
        "gate": nc.dram_tensor("gate_scratch", (2, D), F32).ap(),
        "seed": nc.dram_tensor("seed_scratch", (1, 16), F32).ap(),
    }
    W["out"] = out[0]
    with Scope(nc, "r") as s:
        R = {
            "ident": s.sb("ident", [P, P]), "ident_r": s.sb("ident_r", [P, P], F32R), "zeros": s.sb("zeros", [P, P]),
            "strict": s.sb("strict", [P, P], F32R), "halves": s.sb("halves", [P, 64], F32R),
            "shift": s.sb("shift", [P, 2, KD]), "scale": s.sb("scale", [P, 2, KD]),
        }
        for phase in PHASES:
            phase(nc, T, W, R)


_INS = ['x', 'c', 'ln_in_g', 'ln_in_b', 'w_ada', 'b_ada', 'w_in', 'q_norm_g', 'kv_norm_g', 'w_uq', 'w_ukv', 'w_o',
        'ln1_g', 'ln1_b', 'w_up', 'w_down', 'ln2_g', 'ln2_b']
_OUTS = [((1, 2048, 1024), 'float32')]


def _rope_table():
    import numpy as _np
    inv_freq = (1.0 / (_np.float32(10000.0) ** (_np.arange(0, 32, 2, dtype=_np.float32) / _np.float32(32)))).astype(_np.float32)
    ang = (_np.arange(2048, dtype=_np.float32)[:, None] * inv_freq[None, :]).astype(_np.float32)
    cos, sin = _np.cos(ang).T.astype(_np.float32), _np.sin(ang).T.astype(_np.float32)
    half = _np.concatenate([cos, cos, -sin, sin], axis=0)
    return _np.ascontiguousarray(_np.concatenate([half, half], axis=0))


def kernel(**inputs):
    import numpy as _np
    import concourse.bacc as _bacc
    from concourse import mybir as _mybir
    from concourse.bass_utils import run_bass_kernel_spmd as _run

    nc = _bacc.Bacc("TRN2", target_bir_lowering=False, num_devices=1)
    arrays, T = {}, {}
    for name in _INS:
        a = _np.ascontiguousarray(inputs[name])
        arrays[f"in_{name}_dram"] = a
        T[name] = nc.dram_tensor(f"in_{name}_dram", a.shape, _mybir.dt.from_np(a.dtype), kind="ExternalInput").ap()
    arrays["rope_dram"] = _rope_table()
    T["rope"] = nc.dram_tensor("rope_dram", (128, 2048), F32, kind="ExternalInput").ap()
    (shape, dtype), = _OUTS
    out = nc.dram_tensor("out_0_dram", shape, _mybir.dt.from_np(_np.dtype(dtype)), kind="ExternalOutput").ap()
    build(nc, T, out)
    r = _run(nc, [arrays], core_ids=[0])
    return r.results[0]["out_0_dram"]
```
